# Optimizing a Trainium2 kernel written in Bass

```python
import jax, jax.numpy as jnp
from jax import lax
import numpy as np

D_MODEL = 1024
BATCH = 1
SEQ = 512
DEPTH = 1

D_MIX = D_MODEL
ATT_HEADS = 8
ATT_KV_HEADS = 2
ATT_HEAD_DIM = 64
ATT_GROUP = ATT_HEADS // ATT_KV_HEADS
WINDOW = 128
ATT_BLOCK = WINDOW
ROPE_THETA = 10000.0
MLSTM_HEADS = 4
MLSTM_V_DIM = D_MIX // 2 // MLSTM_HEADS
MLSTM_QK_DIM = MLSTM_V_DIM // 2
MLSTM_CHUNK = 64
CONV_WIDTH = 4
F_BIAS_LO = 3.0
F_BIAS_HI = 6.0
PEER_HEADS = 8
PEER_KEYS = 128
PEER_EXPERTS = PEER_KEYS * PEER_KEYS
PEER_QUERY_DIM = 256
PEER_HALF = PEER_QUERY_DIM // 2
PEER_TOPK = 16
PEER_BLOCK = 64
N_MOD = 6
NORM_EPS = 1e-6

ATT_WIDTH = ATT_HEADS * ATT_HEAD_DIM
ATT_KV_WIDTH = ATT_KV_HEADS * ATT_HEAD_DIM
MLSTM_QK_WIDTH = MLSTM_HEADS * MLSTM_QK_DIM
MLSTM_WIDTH = MLSTM_HEADS * MLSTM_V_DIM
IN_SIZES = (ATT_WIDTH, ATT_KV_WIDTH, ATT_KV_WIDTH, MLSTM_QK_WIDTH, MLSTM_QK_WIDTH, MLSTM_WIDTH, MLSTM_HEADS, MLSTM_HEADS, MLSTM_WIDTH)
IN_SPLITS = tuple(int(s) for s in np.cumsum(IN_SIZES)[:-1])
D_IN = int(sum(IN_SIZES))

kernel_name = 'hymba_swa_mlstm_peer_adaln'

def rmsnorm(x, g):
    xf = x.astype(jnp.float32)
    y = xf * lax.rsqrt(jnp.mean(xf * xf, axis=-1, keepdims=True) + NORM_EPS)
    return (y * g.astype(jnp.float32)).astype(x.dtype)

def rope(x, positions):
    dh = x.shape[-1]
    inv_freq = ROPE_THETA ** (-jnp.arange(0, dh, 2, dtype=jnp.float32) / dh)
    ang = positions.astype(jnp.float32)[..., None] * inv_freq
    cos = jnp.cos(ang)[:, :, None, :]
    sin = jnp.sin(ang)[:, :, None, :]
    xf = x.astype(jnp.float32)
    x1, x2 = jnp.split(xf, 2, axis=-1)
    return jnp.concatenate([x1 * cos - x2 * sin, x2 * cos + x1 * sin], axis=-1).astype(x.dtype)

def sliding_window_attention(q, k, v, sinks):
    B, S, H, Dh = q.shape
    nb = S // ATT_BLOCK
    qb = q.reshape(B, nb, ATT_BLOCK, ATT_KV_HEADS, ATT_GROUP, Dh)

    def band(t):
        tb = t.reshape(B, nb, ATT_BLOCK, ATT_KV_HEADS, Dh)
        prev = jnp.pad(tb, ((0, 0), (1, 0), (0, 0), (0, 0), (0, 0)))[:, :-1]
        return jnp.concatenate([prev, tb], axis=2)

    kb = band(k)
    vb = band(v)
    scores = jnp.einsum('bnqkgd,bnskd->bnkgqs', qb, kb).astype(jnp.float32) * (Dh ** -0.5)
    qi = jnp.arange(ATT_BLOCK)[:, None]
    si = jnp.arange(2 * ATT_BLOCK)[None, :]
    delta = qi + ATT_BLOCK - si
    key_pos = jnp.arange(nb)[:, None, None] * ATT_BLOCK + si - ATT_BLOCK
    valid = (delta >= 0) & (delta < WINDOW) & (key_pos >= 0)
    scores = jnp.where(valid[None, :, None, None], scores, -jnp.inf)
    sink = sinks.astype(jnp.float32).reshape(1, 1, ATT_KV_HEADS, ATT_GROUP, 1, 1)
    m = jnp.maximum(scores.max(axis=-1, keepdims=True), sink)
    p = jnp.exp(scores - m)
    probs = (p / (p.sum(axis=-1, keepdims=True) + jnp.exp(sink - m))).astype(v.dtype)
    out = jnp.einsum('bnkgqs,bnskd->bnqkgd', probs, vb)
    return out.reshape(B, S, H * Dh)

def causal_dwconv(x, w):
    S = x.shape[1]
    xp = jnp.pad(x, ((0, 0), (CONV_WIDTH - 1, 0), (0, 0)))
    acc = xp[:, 0:S] * w[0]
    for j in range(1, CONV_WIDTH):
        acc = acc + xp[:, j:j + S] * w[j]
    return acc

def mlstm_chunkwise(q, k, v, i_pre, f_pre):
    B, S, H, Dk = q.shape
    Dv = v.shape[-1]
    L = MLSTM_CHUNK
    nc = S // L
    f32 = jnp.float32

    def to_chunks(t):
        t = t.astype(f32).reshape((B, nc, L) + t.shape[2:])
        return jnp.moveaxis(t, 1, 0)

    qc = to_chunks(q) * (Dk ** -0.5)
    kc = to_chunks(k)
    vc = to_chunks(v)
    ic = to_chunks(i_pre)
    fc = to_chunks(jax.nn.log_sigmoid(f_pre.astype(f32)))
    causal = jnp.tril(jnp.ones((L, L), dtype=bool))

    def step(carry, xs):
        C, n, m_prev = carry
        qt, kt, vt, it, lf = xs
        b = jnp.cumsum(lf, axis=1)
        bh = b.transpose(0, 2, 1)
        ih = it.transpose(0, 2, 1)
        dlog = bh[..., :, None] - bh[..., None, :] + ih[..., None, :]
        dlog = jnp.where(causal, dlog, -jnp.inf)
        m_inter = bh + m_prev[..., None]
        m_t = jnp.maximum(m_inter, dlog.max(axis=-1))
        w_intra = jnp.exp(dlog - m_t[..., None])
        a_inter = jnp.exp(m_inter - m_t)
        s = jnp.einsum('blhd,bshd->bhls', qt, kt) * w_intra
        a_bl = a_inter.transpose(0, 2, 1)[..., None]
        num = jnp.einsum('bhls,bshv->blhv', s, vt) + a_bl * jnp.einsum('blhd,bhvd->blhv', qt, C)
        den = s.sum(axis=-1) + a_inter * jnp.einsum('blhd,bhd->bhl', qt, n)
        denom = jnp.maximum(jnp.abs(den), jnp.exp(-m_t)).transpose(0, 2, 1)[..., None]
        h = num / denom
        bL = b[:, -1, :]
        g = bL[:, None, :] - b + it
        m_new = jnp.maximum(bL + m_prev, g.max(axis=1))
        w = jnp.exp(g - m_new[:, None, :])
        decay = jnp.exp(bL + m_prev - m_new)
        C_new = decay[..., None, None] * C + jnp.einsum('bsh,bshv,bshd->bhvd', w, vt, kt)
        n_new = decay[..., None] * n + jnp.einsum('bsh,bshd->bhd', w, kt)
        return (C_new, n_new, m_new), h

    init = (jnp.zeros((B, H, Dv, Dk), f32), jnp.zeros((B, H, Dk), f32), jnp.zeros((B, H), f32))
    _, hs = lax.scan(step, init, (qc, kc, vc, ic, fc))
    return jnp.moveaxis(hs, 0, 1).reshape(B, S, H, Dv)

def peer_ffn(h, w_q, keys1, keys2, u, v):
    B, S, D = h.shape
    nblk = S // PEER_BLOCK
    hb = h.reshape(B, nblk, PEER_BLOCK, D).swapaxes(0, 1).reshape(nblk, B * PEER_BLOCK, D)

    def block(ht):
        T = ht.shape[0]
        q = (ht @ w_q).reshape(T, PEER_HEADS, 2, PEER_HALF)
        s1 = jnp.einsum('thd,hkd->thk', q[:, :, 0], keys1).astype(jnp.float32)
        s2 = jnp.einsum('thd,hkd->thk', q[:, :, 1], keys2).astype(jnp.float32)
        v1, i1 = lax.top_k(s1, PEER_TOPK)
        v2, i2 = lax.top_k(s2, PEER_TOPK)
        cand = (v1[..., :, None] + v2[..., None, :]).reshape(T, PEER_HEADS, PEER_TOPK * PEER_TOPK)
        cidx = (i1[..., :, None] * PEER_KEYS + i2[..., None, :]).reshape(T, PEER_HEADS, PEER_TOPK * PEER_TOPK)
        top, pos = lax.top_k(cand, PEER_TOPK)
        eidx = jnp.take_along_axis(cidx, pos, axis=-1)
        gate = jax.nn.softmax(top, axis=-1)
        ug = u[eidx]
        act = jax.nn.gelu(jnp.einsum('thkd,td->thk', ug, ht).astype(jnp.float32), approximate=False) * gate
        vg = v[eidx]
        return jnp.einsum('thk,thkd->td', act.astype(ht.dtype), vg)

    yb = lax.map(block, hb)
    return yb.reshape(nblk, B, PEER_BLOCK, D).swapaxes(0, 1).reshape(B, S, D)

def setup_inputs(seed: int = 0) -> dict:
    key = jax.random.key(seed)
    ks = jax.random.split(key, 22)
    f32 = jnp.float32

    def nrm(k, shape, scale):
        return jax.random.normal(k, shape, f32) * scale

    x = nrm(ks[0], (BATCH, SEQ, D_MODEL), 1.0)
    c = nrm(ks[1], (BATCH, D_MODEL), 1.0)
    positions = jnp.broadcast_to(jnp.arange(SEQ, dtype=jnp.int32), (BATCH, SEQ))
    w_mod = nrm(ks[2], (DEPTH, D_MODEL, N_MOD * D_MODEL), 0.3 * D_MODEL ** -0.5)
    b_mod = nrm(ks[3], (DEPTH, N_MOD * D_MODEL), 0.02)
    g_pre_mix = 1.0 + nrm(ks[4], (DEPTH, D_MODEL), 0.05)
    g_post_mix = 1.0 + nrm(ks[5], (DEPTH, D_MODEL), 0.05)
    w_in = nrm(ks[6], (DEPTH, D_MODEL, D_IN), D_MODEL ** -0.5)
    conv_w = nrm(ks[7], (DEPTH, CONV_WIDTH, 2 * MLSTM_QK_WIDTH), CONV_WIDTH ** -0.5)
    b_igate = nrm(ks[8], (DEPTH, MLSTM_HEADS), 0.1)
    b_fgate = jnp.linspace(F_BIAS_LO, F_BIAS_HI, MLSTM_HEADS, dtype=f32)[None, :] + nrm(ks[9], (DEPTH, MLSTM_HEADS), 0.1)
    mlstm_norm_g = 1.0 + nrm(ks[10], (DEPTH, MLSTM_HEADS, MLSTM_V_DIM), 0.05)
    att_sinks = nrm(ks[11], (DEPTH, ATT_HEADS), 0.5)
    w_out = nrm(ks[12], (DEPTH, D_MIX, D_MODEL), D_MIX ** -0.5)
    g_pre_ffn = 1.0 + nrm(ks[13], (DEPTH, D_MODEL), 0.05)
    g_post_ffn = 1.0 + nrm(ks[14], (DEPTH, D_MODEL), 0.05)
    peer_wq = nrm(ks[15], (DEPTH, D_MODEL, PEER_HEADS * PEER_QUERY_DIM), D_MODEL ** -0.5)
    peer_keys1 = nrm(ks[16], (DEPTH, PEER_HEADS, PEER_KEYS, PEER_HALF), PEER_HALF ** -0.5)
    peer_keys2 = nrm(ks[17], (DEPTH, PEER_HEADS, PEER_KEYS, PEER_HALF), PEER_HALF ** -0.5)
    peer_u = nrm(ks[18], (DEPTH, PEER_EXPERTS, D_MODEL), D_MODEL ** -0.5)
    peer_v = nrm(ks[19], (DEPTH, PEER_EXPERTS, D_MODEL), (PEER_HEADS * PEER_TOPK) ** -0.5)
    return {'x': x, 'c': c, 'positions': positions, 'w_mod': w_mod, 'b_mod': b_mod,
            'g_pre_mix': g_pre_mix, 'g_post_mix': g_post_mix, 'w_in': w_in, 'conv_w': conv_w,
            'b_igate': b_igate, 'b_fgate': b_fgate, 'mlstm_norm_g': mlstm_norm_g,
            'att_sinks': att_sinks, 'w_out': w_out, 'g_pre_ffn': g_pre_ffn, 'g_post_ffn': g_post_ffn,
            'peer_wq': peer_wq, 'peer_keys1': peer_keys1, 'peer_keys2': peer_keys2,
            'peer_u': peer_u, 'peer_v': peer_v}

def reference(x, c, positions, w_mod, b_mod, g_pre_mix, g_post_mix, w_in, conv_w, b_igate, b_fgate,
              mlstm_norm_g, att_sinks, w_out, g_pre_ffn, g_post_ffn, peer_wq, peer_keys1, peer_keys2,
              peer_u, peer_v):
    B, S, D = x.shape
    for l in range(DEPTH):
        mod = (c @ w_mod[l] + b_mod[l])[:, None, :]
        shift1, scale1, gate1, shift2, scale2, gate2 = jnp.split(mod, N_MOD, axis=-1)

        h = rmsnorm(x, g_pre_mix[l]) * (1.0 + scale1) + shift1
        proj = h @ w_in[l]
        aq, ak, av, mq, mk, mv, mi, mf, mo = jnp.split(proj, IN_SPLITS, axis=-1)

        aq = rope(aq.reshape(B, S, ATT_HEADS, ATT_HEAD_DIM), positions)
        ak = rope(ak.reshape(B, S, ATT_KV_HEADS, ATT_HEAD_DIM), positions)
        av = av.reshape(B, S, ATT_KV_HEADS, ATT_HEAD_DIM)
        att = sliding_window_attention(aq, ak, av, att_sinks[l])

        mqk = jax.nn.silu(causal_dwconv(jnp.concatenate([mq, mk], axis=-1), conv_w[l]))
        mq, mk = jnp.split(mqk, 2, axis=-1)
        mh = mlstm_chunkwise(mq.reshape(B, S, MLSTM_HEADS, MLSTM_QK_DIM),
                             mk.reshape(B, S, MLSTM_HEADS, MLSTM_QK_DIM),
                             mv.reshape(B, S, MLSTM_HEADS, MLSTM_V_DIM),
                             mi + b_igate[l], mf + b_fgate[l])
        mh = rmsnorm(mh, mlstm_norm_g[l]).astype(x.dtype)
        mh = (mh * jax.nn.sigmoid(mo).reshape(B, S, MLSTM_HEADS, MLSTM_V_DIM)).reshape(B, S, MLSTM_WIDTH)

        mix = jnp.concatenate([att, mh], axis=-1) @ w_out[l]
        x = x + gate1 * rmsnorm(mix, g_post_mix[l])

        h2 = rmsnorm(x, g_pre_ffn[l]) * (1.0 + scale2) + shift2
        y = peer_ffn(h2, peer_wq[l], peer_keys1[l], peer_keys2[l], peer_u[l], peer_v[l])
        x = x + gate2 * rmsnorm(y, g_post_ffn[l])
    return x


_drawn_inputs = setup_inputs


def setup_inputs(seed=0):
    import zlib

    import numpy as np

    out = dict(_drawn_inputs(seed))
    spreads = {}
    factors = {'b_igate': 64.0, 'att_sinks': 5.27, 'g_post_ffn': 4.365}
    for name, (base, spread) in spreads.items():
        noise = np.random.default_rng([zlib.crc32(name.encode()), seed]).standard_normal(out[name].shape)
        drawn = base * np.exp(spread * noise) if base else spread * noise
        out[name] = __import__('jax').numpy.asarray(drawn.astype(out[name].dtype))
    for name, factor in factors.items():
        out[name] = (out[name] * factor).astype(out[name].dtype)
    return out
```

```python
from contextlib import ExitStack

import concourse.bass as bass
from concourse import mybir

F32 = mybir.dt.float32
F32R = mybir.dt.float32r
I32 = mybir.dt.int32
U32 = mybir.dt.uint32
ALU = mybir.AluOpType
ACT = mybir.ActivationFunctionType
AX = mybir.AxisListType.X

P = 128
T = 512
NT = T // P
D = 1024
DC = D // P
HEADS, KV, DH = 8, 2, 64
GROUP = HEADS // KV
MH, MV, MQ = 4, 128, 64
TAPS = 4
NEG = -1.0e30
EPS = 1e-6
PI = 3.141592653589793
TWO_PI_HI, TWO_PI_MID = 6.28125, 0.0019350051879882812
TWO_PI_LO = 2 * PI - TWO_PI_HI - TWO_PI_MID
ROUND = 12582912.0

C_AQ, C_AK, C_MQ, C_MV, C_MI, C_MF, C_MO, C_END = 0, 512, 768, 1280, 1792, 1796, 1800, 2312
SHIFT1, SCALE1, GATE1, SHIFT2, SCALE2, GATE2 = range(6)

PH, PK, PTOP = 8, 128, 16
NE = PK * PK
NBLK = NE // P
CAND = [(a, b) for a in range(PTOP) for b in range(PTOP) if (a + 1) * (b + 1) <= PTOP]
NCAND = len(CAND)
TB = 16
NTB = T // TB
BG = 8
NBG = NBLK // BG
LEAD = 46
GT = 8


class Chain:

    def __init__(self, eng, sem):
        self.eng, self.sem, self.n = eng, sem, 0

    def put(self, ins):
        self.n += 1
        ins.then_inc(self.sem, 1)

    def wait(self):
        self.eng.wait_ge(self.sem, self.n)

    def __call__(self, ins):
        self.put(ins)
        self.wait()


class Banks:

    def __init__(self, psum, order, full, free):
        self.psum, self.full, self.free, self.n = psum, full, free, len(full)
        self.number = {name: i for i, name in enumerate(order)}
        assert len(self.number) == len(order)

    def __call__(self, *name):
        return self.psum[:, self.number[name] % self.n, :]

    def wait_free(self, pe, *name):
        k = self.number[name]
        if k >= self.n:
            pe.wait_ge(self.free[k % self.n], k // self.n)

    def wait_full(self, eng, *name):
        k = self.number[name]
        eng.wait_ge(self.full[k % self.n], k // self.n + 1)

    def wait_released(self, eng, *name):
        k = self.number[name]
        eng.wait_ge(self.free[k % self.n], k // self.n + 1)

    def done(self, ins, *name):
        ins.then_inc(self.full[self.number[name] % self.n], 1)

    def release(self, ins, *name):
        ins.then_inc(self.free[self.number[name] % self.n], 1)


def rsqrt(nc, step, y, a, half_a, t):
    step(nc.vector.tensor_scalar(t.bitcast(U32), a.bitcast(U32), 1, None, ALU.logical_shift_right))
    step(nc.vector.tensor_scalar(y.bitcast(I32), t.bitcast(I32), -1.0, float(0x5F3759DF), ALU.mult, ALU.add))
    step(nc.vector.tensor_scalar(half_a, a, -0.5, None, ALU.mult))
    for _ in range(3):
        step(nc.vector.tensor_tensor(t, y, y, ALU.mult))
        step(nc.vector.tensor_tensor(t, t, half_a, ALU.mult))
        step(nc.vector.scalar_tensor_tensor(out=y, in0=t, scalar=1.5, in1=y, op0=ALU.add, op1=ALU.mult))


def mix_block(nc, A, keep):
    x_sb, hT, ident, cols, gg2 = keep["x"], keep["hT"], keep["ident"], keep["cols"], keep["gg2"]
    with ExitStack() as ctx:
        def sb(name, shape, dt=F32):
            return ctx.enter_context(nc.sbuf_tensor(name, shape, dt))

        def sem(name):
            return ctx.enter_context(nc.semaphore(name))

        slabs = [("mod", s, h) for s in (SCALE1, SHIFT1) for h in range(2)]
        slabs += [("in", C_MQ), ("in", C_AQ), ("in", C_AK), ("in", C_MV), ("in", C_MO)]
        slabs += [("mod", s, h) for s in (GATE1, SCALE2, SHIFT2, GATE2) for h in range(2)]
        slabs += [("out", h) for h in range(2)]
        NW = 3
        slab_no = {s: i for i, s in enumerate(slabs)}

        scores = lambda n: [("sc", n, g, jp) for g in range(KV) for jp in range(2)]
        probsT = lambda n: [("pT", n, i) for i in range(4)]
        mscore = lambda h: [("ms", h, s) for s in range(NT)]
        mvalue = lambda h: [("mv2", h, i) for i in range(2)]
        modr = lambda s: [("modr", s, h) for h in range(2)]
        modg = lambda s: [("modg", s, h) for h in range(2)]
        order = [("rows",)] + [("xT", c) for c in range(DC)] + modr(SCALE1) + modr(SHIFT1)
        order += [("modc", SCALE1), ("modc", SHIFT1)]
        order += [("mq", j) for j in range(4)] + [(k, t) for k in ("aq", "kv") for t in range(NT)]
        order += [("gi",), ("gf",)] + [(k, t) for k in ("mv", "mo") for t in range(NT)]
        order += modg(GATE1) + [("qT", t) for t in range(NT)] + [("kT",)]
        order += [("gcol",)] + [("rb", h) for h in range(MH)]
        order += scores(0) + mscore(0) + modr(SCALE2)
        order += scores(1) + probsT(0) + [("av", 0)] + mvalue(0) + mscore(1)
        order += [("modc", SCALE2)] + modr(SHIFT2)
        order += scores(2) + probsT(1) + [("av", 1)] + mvalue(1) + mscore(2)
        order += [("modc", SHIFT2)] + modg(GATE2)
        order += scores(3) + probsT(2) + [("av", 2)] + mvalue(2) + mscore(3)
        order += probsT(3) + [("av", 3)] + mvalue(3)
        order += [("mixT", c) for c in range(DC)] + [("out", h, t) for h in range(2) for t in range(NT)]
        order += [("h2T", c) for c in range(DC)]
        last_use = {("mod", s, h): ("modr", s, h) for s in (SCALE1, SHIFT1, SCALE2, SHIFT2) for h in range(2)}
        last_use |= {("mod", s, h): ("modg", s, h) for s in (GATE1, GATE2) for h in range(2)}
        last_use |= {("in", C_MQ): ("mq", 3), ("in", C_AQ): ("aq", 3), ("in", C_AK): ("kv", 3),
                     ("in", C_MV): ("mv", 3), ("in", C_MO): ("mo", 3)}
        last_use |= {("out", h): ("out", h, 3) for h in range(2)}

        psum = ctx.enter_context(nc.psum_tensor("mix_psum", [P, 8, 512], F32))
        slab = sb("slab", [P, NW, DC, 520])
        rows = sb("rows", [88, P])
        c_rep = sb("c_rep", [P, DC, P])
        bias_if = sb("bias_if", [MH, 2])
        pos_i = sb("pos_i", [P, NT], I32)
        pos = sb("pos", [P, NT])
        inv_freq = sb("inv_freq", [P, DH // 2])
        sinks = sb("sinks", [P, HEADS])
        g_post = sb("g_post", [P, D])
        gg1 = sb("gg1", [P, D])
        m_norm = sb("m_norm", [P, MH * MV])
        mod_r = sb("mod_r", [1, D])
        stat = sb("stat", [P, 5, 16])
        angle = sb("angle", [P, 3, NT, DH // 2])
        trig = sb("trig", [P, 2, NT, DH // 2])
        cos_sin = sb("cos_sin", [P, NT, 2, DH])
        band = sb("band", [P, 2 * P])
        pick = sb("pick", [MH, MH, P])
        late = sb("late", [P, 2048 + 2 * 10 * P])
        gate = late[0:MH, 0:8 * T].rearrange("h (i t) -> h i t", i=8)
        I_, F_, E_, LF, B_, M_, R_, CS = range(8)
        zeros = late[0:MH, 8 * T:9 * T]
        gcol = sb("gcol", [P, NT, 8])
        em = sb("em", [P, NT, MH])
        both = sb("both", [P, NT, D])
        q_rot = both[:, :, 0:512]
        wide = both[:, :, 512:1024]
        k_rot = sb("k_rot", [P, NT, KV * DH])
        v_att = sb("v_att", [P, NT, KV * DH])
        qT = sb("qT", [P, NT, GROUP, P])
        mod_place = lambda s: qT[0:1, :, :, :].rearrange("a t g q -> a (t g q)")[:, 0:D] if s == SHIFT1 else mod_r[:]
        kT = sb("kT", [P, T])
        v_ext = sb("v_ext", [P, NT, MH, MV + 1])
        o_gate = sb("o_gate", [P, NT, MH * MV])
        mqk = sb("mqk", [P, 4, T])
        rr = hT
        r_all = rr[:, 0:4, :]
        r_diag = rr[:, 4:8, :].rearrange("p h (b t) -> p h b t", b=NT)
        decay = sb("decay", [P, 2, T])
        TRI = [0, 4, 7, 9]
        pm = late[:, 2048:2048 + 20 * P].rearrange("p (a n) -> p a n", a=2)
        sc = sb("sc", [P, 2, HEADS, 2 * P])
        conv_in = sc[:, :, :, :].rearrange("p a b c -> p (a b c)")[:, 0:4 * 515].rearrange("p (j t) -> p j t", j=4)
        junk = sc[:, :, :, :].rearrange("p a b c -> p (a b c)")[:, 0:2048]
        pT = late[:, 0:2048].rearrange("p (h b q) -> p h b q", h=HEADS, b=2)
        mx = sb("mx", [P, 2, 6, HEADS])
        den = sb("den", [P, 4])

        bank_full = [sem(f"bank_full{i}") for i in range(8)]
        bank_free = [sem(f"bank_free{i}") for i in range(8)]
        bk = Banks(psum, order, bank_full, bank_free)
        slab_in = [sem(f"slab_in{i}") for i in range(NW)]
        x_in = [sem(f"x_in{i}") for i in range(NT)]
        names = ("rows_in bc_in small_in dve_chain act_chain pool_chain consts xn_ready c_ready angles trig_done "
                 "hT_ready f_abs f_exp f_ln gates_done diag_done em_done conv_pad conv_done silu_e mqk_ready "
                 "g_post2_in decay_done qrot_done krot_done v_done att_max att_exp mh_done mix_sq xn2_ready").split()
        S = {n: sem(n) for n in names}

        block = ctx.enter_context(nc.Block())

        def slab_of(name):
            return slab[:, slab_no[name] % NW, :, :]

        def wait_slab(pe, name):
            n = slab_no[name]
            pe.wait_ge(slab_in[n % NW], 16 * (n // NW + 1))

        @block.sync
        def _(sp):
            for t in range(NT):
                sp.dma_start(x_sb[:, t, :], A["x"][0, t * P:(t + 1) * P, :]).then_inc(x_in[t], 16)
            sp.dma_start(rows[0:48, :], A["b_mod"][0].rearrange("(r p) -> r p", p=P)).then_inc(S["rows_in"], 16)
            sp.dma_start(rows[48:56, :], A["g_pre_mix"][0].rearrange("(r p) -> r p", p=P)).then_inc(S["rows_in"], 16)
            sp.dma_start(rows[56:64, :], A["g_pre_ffn"][0].rearrange("(r p) -> r p", p=P)).then_inc(S["rows_in"], 16)
            sp.dma_start(rows[64:80, :], A["conv_w"][0].rearrange("j (r p) -> (j r) p", p=P)).then_inc(S["rows_in"], 16)
            sp.dma_start(rows[80:88, :], A["c"][0].rearrange("(r p) -> r p", p=P)).then_inc(S["rows_in"], 16)
            for n, name in enumerate(slabs):
                if n >= NW:
                    bk.wait_full(sp, *last_use[slabs[n - NW]])
                if name[0] == "mod":
                    src, c0, w = A["w_mod"], name[1] * D + name[2] * 512, 512
                elif name[0] == "in":
                    src, c0 = A["w_in"], name[1]
                    w = {C_MQ: 512, C_AQ: 512, C_AK: 256, C_MV: 520, C_MO: 512}[c0]
                else:
                    src, c0, w = A["w_out"], name[1] * 512, 512
                sp.dma_start(slab_of(name)[:, :, 0:w],
                             src[0, :, c0:c0 + w].rearrange("(c p) n -> p c n", p=P)).then_inc(slab_in[n % NW], 16)

        @block.gpsimd
        def _(pool):
            step = Chain(pool, S["pool_chain"])
            pool.dma_start(pos_i[:], A["positions"][0].rearrange("(t p) -> p t", p=P), allow_slow_non_contiguous=True).then_inc(S["small_in"], 16)
            pool.dma_start(bias_if[:, 0:1], A["b_igate"].rearrange("a h -> h a"), allow_slow_non_contiguous=True).then_inc(S["small_in"], 16)
            pool.dma_start(bias_if[:, 1:2], A["b_fgate"].rearrange("a h -> h a"), allow_slow_non_contiguous=True).then_inc(S["small_in"], 16)
            step(nc.gpsimd.memset(ident[:], 0.0))
            nc.gpsimd.affine_select(out=ident[:], in_=ident[:], compare_op=ALU.not_equal, fill=1.0, base=0,
                                    pattern=[[-1, P]], channel_multiplier=1).then_inc(S["consts"], 1)
            nc.gpsimd.memset(conv_in[:, :, 0:3], 0.0).then_inc(S["conv_pad"], 1)
            nc.gpsimd.memset(zeros, 0.0).then_inc(S["consts"], 1)
            nc.gpsimd.memset(v_ext[:, :, :, MV:MV + 1], 1.0).then_inc(S["consts"], 1)
            step(nc.gpsimd.memset(pick[:], 1.0))
            nc.gpsimd.affine_select(out=pick[:], in_=pick[:], compare_op=ALU.is_equal, fill=0.0, base=0,
                                    pattern=[[-1, MH], [0, P]], channel_multiplier=1).then_inc(S["consts"], 1)
            step(nc.gpsimd.memset(band[:], 0.0))
            step(nc.gpsimd.affine_select(out=band[:], in_=band[:], compare_op=ALU.is_gt, fill=NEG, base=0,
                                         pattern=[[1, 2 * P]], channel_multiplier=-1))
            nc.gpsimd.affine_select(out=band[:], in_=band[:], compare_op=ALU.is_ge, fill=NEG, base=P,
                                    pattern=[[-1, 2 * P]], channel_multiplier=1).then_inc(S["consts"], 1)
            for h in range(MH):
                bk.wait_released(pool, "rb", h)
                nc.gpsimd.affine_select(out=r_diag[:, h, :, :], in_=r_all[:, h, :].rearrange("p (b t) -> p b t", b=NT),
                                        compare_op=ALU.is_ge, fill=NEG, base=0, pattern=[[0, NT], [1, P]],
                                        channel_multiplier=-1).then_inc(S["diag_done"], 1)

        CONSTS = 5

        @block.tensor
        def _(pe):
            mm, tr = nc.tensor.matmul, nc.tensor.transpose
            pe.wait_ge(S["consts"], 1)
            pe.wait_ge(S["rows_in"], 80)
            bk.done(tr(bk("rows")[:, 0:88], rows[:], ident[0:88, 0:88]), "rows")
            pe.wait_ge(S["xn_ready"], NT)
            for c in range(DC):
                bk.wait_free(pe, "xT", c)
                for t in range(NT):
                    last = tr(bk("xT", c)[:, t * P:(t + 1) * P], both[:, t, c * P:(c + 1) * P], ident[:])
                bk.done(last, "xT", c)

            def mod_row1(s, h):
                wait_slab(pe, ("mod", s, h))
                bk.wait_free(pe, "modr", s, h)
                for c in range(DC):
                    last = mm(bk("modr", s, h)[0:1, :], cols[:, 80 + c:81 + c], slab_of(("mod", s, h))[:, c, 0:512],
                              start=(c == 0), stop=(c == DC - 1))
                bk.done(last, "modr", s, h)

            def mod_columns(s):
                for h in range(2):
                    bk.wait_released(pe, "modr", s, h)
                bk.wait_free(pe, "modc", s)
                for j in range(8):
                    last = mm(bk("modc", s)[:, j:j + 1], mod_place(s)[:, j * P:(j + 1) * P], ident[0:1, 0:1],
                              start=True, stop=True)
                bk.done(last, "modc", s)

            def mod_rows(s):
                for h in range(2):
                    wait_slab(pe, ("mod", s, h))
                    bk.wait_free(pe, "modg", s, h)
                    for c in range(DC):
                        last = mm(bk("modg", s, h), c_rep[:, c, :], slab_of(("mod", s, h))[:, c, 0:512],
                                  start=(c == 0), stop=(c == DC - 1))
                    bk.done(last, "modg", s, h)

            pe.wait_ge(S["c_ready"], 1)
            for s in (SCALE1, SHIFT1):
                for h in range(2):
                    mod_row1(s, h)
            mod_columns(SCALE1)
            mod_columns(SHIFT1)
            pe.wait_ge(S["hT_ready"], DC)
            w = slab_of(("in", C_MQ))
            wait_slab(pe, ("in", C_MQ))
            order_of_gates = (("gi", C_MI), ("gf", C_MF))
            for j in range(4):
                bk.wait_free(pe, "mq", j)
                for c in range(DC):
                    last = mm(bk("mq", j), w[:, c, j * P:(j + 1) * P], hT[:, c, :], start=(c == 0), stop=(c == DC - 1))
                bk.done(last, "mq", j)
            for kind, c0, width in (("aq", C_AQ, 512), ("kv", C_AK, 256)):
                w = slab_of(("in", c0))
                wait_slab(pe, ("in", c0))
                for t in range(NT):
                    bk.wait_free(pe, kind, t)
                    for c in range(DC):
                        last = mm(bk(kind, t)[:, 0:width], hT[:, c, t * P:(t + 1) * P], w[:, c, 0:width],
                                  start=(c == 0), stop=(c == DC - 1))
                    bk.done(last, kind, t)
            w = slab_of(("in", C_MV))
            wait_slab(pe, ("in", C_MV))
            for name, col in order_of_gates:
                bk.wait_free(pe, name)
                for c in range(DC):
                    last = mm(bk(name)[0:MH, :], w[:, c, col - C_MV:col - C_MV + MH], hT[:, c, :],
                              start=(c == 0), stop=(c == DC - 1))
                bk.done(last, name)
            for kind, c0, width in (("mv", C_MV, 512), ("mo", C_MO, 512)):
                w = slab_of(("in", c0))
                wait_slab(pe, ("in", c0))
                for t in range(NT):
                    bk.wait_free(pe, kind, t)
                    for c in range(DC):
                        last = mm(bk(kind, t)[:, 0:width], hT[:, c, t * P:(t + 1) * P], w[:, c, 0:width],
                                  start=(c == 0), stop=(c == DC - 1))
                    bk.done(last, kind, t)
            mod_rows(GATE1)
            for t in range(NT):
                pe.wait_ge(S["qrot_done"], t + 1)
                bk.wait_free(pe, "qT", t)
                for j in range(GROUP):
                    last = tr(bk("qT", t)[:, j * P:(j + 1) * P], q_rot[:, t, j * P:(j + 1) * P], ident[:])
                bk.done(last, "qT", t)
            pe.wait_ge(S["krot_done"], NT)
            bk.wait_free(pe, "kT")
            for t in range(NT):
                last = tr(bk("kT")[:, t * P:(t + 1) * P], k_rot[:, t, :], ident[:])
            bk.done(last, "kT")
            pe.wait_ge(S["gates_done"], 1)
            bk.wait_free(pe, "gcol")
            for t in range(NT):
                for i, row in enumerate((CS, M_)):
                    last = tr(bk("gcol")[:, t * 8 + i * 4:t * 8 + i * 4 + 4], gate[:, row, t * P:(t + 1) * P], ident[0:MH, 0:MH])
            bk.done(last, "gcol")
            pe.wait_ge(S["consts"], CONSTS)
            for h in range(MH):
                bk.wait_free(pe, "rb", h)
                bk.done(mm(bk("rb", h), pick[:, h, :], gate[:, R_, :], start=True, stop=True), "rb", h)

            def att_scores(n):
                k0 = max(n - 1, 0) * P
                wide_ = (n + 1) * P - k0
                bk.wait_released(pe, "qT", n)
                bk.wait_released(pe, "kT")
                for name in scores(n):
                    _, _, g, jp = name
                    bk.wait_free(pe, *name)
                    for i in range(2):
                        last = mm(bk(*name)[:, i * wide_:(i + 1) * wide_], qT[g * DH:(g + 1) * DH, n, jp * 2 + i, :],
                                  kT[g * DH:(g + 1) * DH, k0:k0 + wide_], start=True, stop=True)
                    bk.done(last, *name)

            def att_values(n):
                pe.wait_ge(S["att_exp"], n + 1)
                blocks = 1 if n == 0 else 2
                for i, name in enumerate(probsT(n)):
                    bk.wait_free(pe, *name)
                    for hh in range(2):
                        for b in range(blocks):
                            at = (hh * blocks + b) * P
                            last = tr(bk(*name)[:, at:at + P], sc[:, n % 2, 2 * i + hh, b * P:(b + 1) * P], ident[:])
                    bk.done(last, *name)
                for name in probsT(n):
                    bk.wait_released(pe, *name)
                pe.wait_ge(S["v_done"], NT)
                bk.wait_free(pe, "av", n)
                for h in range(HEADS):
                    for b in range(blocks):
                        last = mm(bk("av", n)[:, h * DH:(h + 1) * DH], pT[:, h, b, :],
                                  v_att[:, n - blocks + 1 + b, (h // GROUP) * DH:(h // GROUP + 1) * DH],
                                  start=(b == 0), stop=(b == blocks - 1))
                bk.done(last, "av", n)

            def mlstm_scores(h):
                pe.wait_ge(S["mqk_ready"], 1)
                p0 = (h % 2) * MQ
                for s in range(NT):
                    bk.wait_free(pe, "ms", h, s)
                    bk.done(mm(bk("ms", h, s)[:, 0:T - s * P], mqk[p0:p0 + MQ, 2 + h // 2, s * P:(s + 1) * P],
                               mqk[p0:p0 + MQ, h // 2, s * P:T], start=True, stop=True), "ms", h, s)

            def mlstm_values(h):
                for s in range(NT):
                    bk.wait_released(pe, "ms", h, s)
                    bk.wait_released(pe, "mv", s)
                for i in range(2):
                    bk.wait_free(pe, "mv2", h, i)
                    for tt in range(2):
                        t = 2 * i + tt
                        for s in range(t + 1):
                            at = (TRI[s] + t - s) * P
                            last = mm(bk("mv2", h, i)[:, tt * (MV + 1):(tt + 1) * (MV + 1)], pm[:, h % 2, at:at + P],
                                      v_ext[:, s, h, :], start=(s == 0), stop=(s == t))
                    bk.done(last, "mv2", h, i)

            att_scores(0)
            mlstm_scores(0)
            mod_row1(SCALE2, 0)
            mod_row1(SCALE2, 1)
            att_scores(1)
            att_values(0)
            mlstm_values(0)
            mlstm_scores(1)
            mod_columns(SCALE2)
            mod_row1(SHIFT2, 0)
            mod_row1(SHIFT2, 1)
            att_scores(2)
            att_values(1)
            mlstm_values(1)
            mlstm_scores(2)
            mod_columns(SHIFT2)
            mod_rows(GATE2)
            att_scores(3)
            att_values(2)
            mlstm_values(2)
            mlstm_scores(3)
            att_values(3)
            mlstm_values(3)
            for c in range(DC):
                if c < 4:
                    for n in range(NT):
                        bk.wait_released(pe, "av", n)
                else:
                    pe.wait_ge(S["mh_done"], 1)
                bk.wait_free(pe, "mixT", c)
                for t in range(NT):
                    last = tr(bk("mixT", c)[:, t * P:(t + 1) * P], both[:, t, c * P:(c + 1) * P], ident[:])
                bk.done(last, "mixT", c)
            for c in range(DC):
                bk.wait_released(pe, "mixT", c)
            for h in range(2):
                wait_slab(pe, ("out", h))
                for t in range(NT):
                    bk.wait_free(pe, "out", h, t)
                    for c in range(DC):
                        last = mm(bk("out", h, t), rr[:, c, t * P:(t + 1) * P], slab_of(("out", h))[:, c, 0:512],
                                  start=(c == 0), stop=(c == DC - 1))
                    bk.done(last, "out", h, t)
            pe.wait_ge(S["xn2_ready"], NT)
            for c in range(DC):
                bk.wait_free(pe, "h2T", c)
                for t in range(NT):
                    last = tr(bk("h2T", c)[:, t * P:(t + 1) * P], both[:, t, c * P:(c + 1) * P], ident[:])
                bk.done(last, "h2T", c)

        @block.scalar
        def _(act):
            func = nc.scalar.activation
            step = Chain(act, S["act_chain"])
            for dst, src in ((inv_freq, A["inv_freq"]), (sinks, A["att_sinks"][0]), (gg1, A["b_mod"][0, GATE1 * D:(GATE1 + 1) * D]),
                             (g_post, A["g_post_mix"][0]), (gg2, A["b_mod"][0, GATE2 * D:(GATE2 + 1) * D]),
                             (m_norm, A["mlstm_norm_g"][0].rearrange("h v -> (h v)"))):
                act.dma_start(dst[:], src.partition_broadcast(P)).then_inc(S["bc_in"], 16)
            act.wait_ge(S["angles"], 1)
            func(trig[:].rearrange("p a t f -> p (a t f)"), angle[:, 1:3, :, :].rearrange("p a t f -> p (a t f)"),
                 ACT.Sin).then_inc(S["trig_done"], 1)
            for c in range(DC):
                bk.wait_full(act, "xT", c)
                ins = func(hT[:, c, :], bk("xT", c), ACT.Copy)
                bk.release(ins, "xT", c)
            act.wait_ge(S["conv_pad"], 1)
            act.wait_ge(S["xn_ready"], NT)
            for j in range(4):
                bk.wait_full(act, "mq", j)
                bk.release(func(conv_in[:, j, 3:3 + T], bk("mq", j), ACT.Copy), "mq", j)
            act.wait_ge(S["conv_done"], 1)
            func(wide, mqk[:], ACT.Sigmoid).then_inc(S["silu_e"], 1)
            act.wait_ge(S["f_abs"], 1)
            func(gate[:, E_, :], gate[:, E_, :], ACT.Exp, scale=-1.0).then_inc(S["f_exp"], 1)
            act.wait_ge(S["f_exp"], 1)
            func(gate[:, E_, :], gate[:, E_, :], ACT.Ln, bias=1.0).then_inc(S["f_ln"], 1)
            act.wait_ge(S["consts"], CONSTS)
            for t in range(NT):
                bk.wait_full(act, "mv", t)
                ins = func(v_ext[:, t, :, 0:MV], bk("mv", t).rearrange("p (h v) -> p h v", h=MH), ACT.Copy)
                bk.release(ins, "mv", t)
            for t in range(NT):
                bk.wait_full(act, "mo", t)
                bk.release(func(o_gate[:, t, :], bk("mo", t), ACT.Sigmoid), "mo", t)
            for h in range(MH):
                bk.wait_full(act, "rb", h)
                bk.release(func(r_all[:, h, :], bk("rb", h), ACT.Copy), "rb", h)
            bk.wait_released(act, "gcol")
            act.dma_start(g_post[:], A["g_post_ffn"][0].partition_broadcast(P)).then_inc(S["g_post2_in"], 16)
            func(em[:], gcol[:, :, 4:8], ACT.Exp, scale=-1.0).then_inc(S["em_done"], 1)

            def att_exp(n):
                act.wait_ge(S["att_max"], n + 1)
                keys = P if n == 0 else 2 * P
                for h in range(HEADS):
                    func(sc[:, n % 2, h, 0:keys], sc[:, n % 2, h, 0:keys], ACT.Exp, bias=mx[:, n % 2, 1, h:h + 1],
                         accum_out=mx[:, n % 2, 3, h:h + 1])
                func(mx[:, n % 2, 4, :], mx[:, n % 2, 2, :], ACT.Exp).then_inc(S["att_exp"], 1)

            def probs_T(n):
                blocks = 1 if n == 0 else 2
                for i in range(2):
                    name = ("pT", n, i)
                    bk.wait_full(act, *name)
                    if n and i == 0:
                        bk.wait_full(act, "av", n - 1)
                    ins = func(pT[:, 2 * i:2 * i + 2, 0:blocks, :],
                               bk(*name)[:, 0:2 * blocks * P].rearrange("p (h b q) -> p h b q", h=2, b=blocks), ACT.Copy)
                    bk.release(ins, *name)

            def decays(h):
                act.wait_ge(S["diag_done"], h + 1)
                for s in range(NT):
                    k = h * NT + s - 2
                    if k >= 0:
                        bk.wait_released(act, "ms", k // NT, k % NT)
                    bias = gcol[:, s, h:h + 1]
                    ins = func(decay[:, s % 2, 0:P], r_diag[:, h, s, :], ACT.Exp, bias=bias)
                    if s < NT - 1:
                        ins = func(decay[:, s % 2, P:T - s * P], r_all[:, h, (s + 1) * P:T], ACT.Exp, bias=bias)
                    ins.then_inc(S["decay_done"], 1)

            decays(0)
            att_exp(0)
            att_exp(1)
            probs_T(0)
            decays(1)
            att_exp(2)
            probs_T(1)
            decays(2)
            att_exp(3)
            probs_T(2)
            decays(3)
            probs_T(3)
            for c in range(DC):
                bk.wait_full(act, "mixT", c)
                bk.release(func(rr[:, c, :], bk("mixT", c), ACT.Copy), "mixT", c)
            for h in range(2):
                for t in range(NT):
                    bk.wait_full(act, "out", h, t)
                    func(sc[:, 0, 0:2, :], bk("out", h, t).rearrange("p (a b) -> p a b", a=2), ACT.Square,
                         accum_out=stat[:, 0, 2 * t + h:2 * t + h + 1]).then_inc(S["mix_sq"], 1)
                    act.wait_ge(S["mix_sq"], NT * h + t + 1)
            for c in range(0, DC, 2):
                bk.wait_full(act, "h2T", c)
                ins = func(hT[:, c, :], bk("h2T", c), ACT.Identity, scale=cols[:, SCALE2 * 8 + c:SCALE2 * 8 + c + 1],
                           bias=cols[:, SHIFT2 * 8 + c:SHIFT2 * 8 + c + 1])
                bk.release(ins, "h2T", c)

        @block.vector
        def _(dve):
            v = nc.vector
            step = Chain(dve, S["dve_chain"])

            def mean_to_rstd(width, n):
                step(v.tensor_scalar(stat[:, 2, 0:n], stat[:, 0, 0:n], 1.0 / width, EPS, ALU.mult, ALU.add))
                rsqrt(nc, step, stat[:, 1, 0:n], stat[:, 2, 0:n], stat[:, 3, 0:n], stat[:, 4, 0:n])

            for t in range(NT):
                dve.wait_ge(x_in[t], 16)
                step(v.tensor_tensor_reduce(out=both[:, t, :], in0=x_sb[:, t, :], in1=x_sb[:, t, :], scale=1.0, scalar=0.0,
                                            op0=ALU.mult, op1=ALU.add, accum_out=stat[:, 0, t:t + 1]))
            mean_to_rstd(D, NT)
            for t in range(NT):
                v.tensor_scalar(both[:, t, :], x_sb[:, t, :], stat[:, 1, t:t + 1], None, ALU.mult).then_inc(S["xn_ready"], 1)
            bk.wait_full(dve, "rows")
            ins = v.tensor_copy(cols[:, 0:88], bk("rows")[:, 0:88])
            bk.release(ins, "rows")
            bk.wait_released(dve, "rows")
            v.tensor_copy(c_rep[:], cols[:, 80:88].unsqueeze(2).broadcast_to([P, DC, P])).then_inc(S["c_ready"], 1)
            dve.wait_ge(S["small_in"], 48)
            dve.wait_ge(S["bc_in"], 6 * 16)
            step(v.tensor_copy(pos[:], pos_i[:]))
            for t in range(NT):
                step(v.tensor_scalar(angle[:, 0, t, :], inv_freq[:], pos[:, t:t + 1], None, ALU.mult))
            for i, quarter in ((2, 0.0), (1, 0.25)):
                a, k = angle[:, i, :, :], trig[:, 0, :, :]
                step(v.tensor_scalar(k, angle[:, 0, :, :], 1.0 / (2 * PI), quarter, ALU.mult, ALU.add))
                step(v.tensor_scalar(k, k, ROUND, None, ALU.add))
                step(v.tensor_scalar(k, k, ROUND, None, ALU.subtract))
                step(v.scalar_tensor_tensor(out=a, in0=k, scalar=-TWO_PI_HI, in1=angle[:, 0, :, :], op0=ALU.mult, op1=ALU.add))
                for part in (TWO_PI_MID, TWO_PI_LO):
                    step(v.scalar_tensor_tensor(out=a, in0=k, scalar=-part, in1=a, op0=ALU.mult, op1=ALU.add))
                if quarter:
                    step(v.tensor_scalar(a, a, PI / 2, None, ALU.add))
                ins = v.tensor_scalar(a, a, 3.1415925, -3.1415925, ALU.min, ALU.max)
                if quarter:
                    ins.then_inc(S["angles"], 1)
                else:
                    step(ins)
            dve.wait_ge(S["trig_done"], 1)
            for half in range(2):
                v.tensor_copy(cos_sin[:, :, 0, half * 32:half * 32 + 32], trig[:, 0, :, :])
            v.tensor_copy(cos_sin[:, :, 1, 32:64], trig[:, 1, :, :])
            step(v.tensor_scalar(cos_sin[:, :, 1, 0:32], trig[:, 1, :, :], -1.0, None, ALU.mult))

            def mod_rowcopy(s):
                for half in range(2):
                    bk.wait_full(dve, "modr", s, half)
                    ins = v.tensor_copy(mod_place(s)[:, half * 512:half * 512 + 512], bk("modr", s, half)[0:1, :])
                    bk.release(ins, "modr", s, half)

            def mod_col(s):
                a = s * 8
                bk.wait_full(dve, "modc", s)
                ins = v.tensor_tensor(cols[:, a:a + 8], bk("modc", s)[:, 0:8], cols[:, a:a + 8], ALU.add)
                bk.release(ins, "modc", s)
                bk.wait_released(dve, "modc", s)

            def mod_scale(s, g0):
                a = s * 8
                step(v.scalar_tensor_tensor(out=cols[:, a:a + 8], in0=cols[:, a:a + 8], scalar=1.0, in1=cols[:, g0:g0 + 8],
                                            op0=ALU.add, op1=ALU.mult))

            def mod_row(s, dst, g):
                for half in range(2):
                    at = slice(half * 512, half * 512 + 512)
                    bk.wait_full(dve, "modg", s, half)
                    ins = v.tensor_tensor(dst[:, at], bk("modg", s, half), dst[:, at], ALU.add)
                    bk.release(ins, "modg", s, half)
                    bk.wait_released(dve, "modg", s, half)
                    step(v.tensor_tensor(dst[:, at], dst[:, at], g[:, at], ALU.mult))

            mod_rowcopy(SCALE1)
            mod_rowcopy(SHIFT1)
            mod_col(SCALE1)
            mod_scale(SCALE1, 48)
            mod_col(SHIFT1)
            for c in range(DC):
                bk.wait_released(dve, "xT", c)
                v.tensor_scalar(hT[:, c, :], hT[:, c, :], cols[:, 8 * SCALE1 + c:8 * SCALE1 + c + 1],
                                cols[:, 8 * SHIFT1 + c:8 * SHIFT1 + c + 1], ALU.mult, ALU.add).then_inc(S["hT_ready"], 1)
            for j in range(4):
                bk.wait_released(dve, "mq", j)
                acc = mqk[:, j, :]
                step(v.tensor_scalar(acc, conv_in[:, j, 0:T], cols[:, 64 + j:65 + j], None, ALU.mult))
                for tap in range(1, TAPS):
                    w = cols[:, 64 + tap * 4 + j:65 + tap * 4 + j]
                    ins = v.scalar_tensor_tensor(out=acc, in0=conv_in[:, j, tap:tap + T], scalar=w, in1=acc,
                                                 op0=ALU.mult, op1=ALU.add)
                    if j == 3 and tap == TAPS - 1:
                        ins.then_inc(S["conv_done"], 1)
                    else:
                        step(ins)
            tmp = junk[:, 0:512].rearrange("p (g j d) -> p g j d", g=KV, j=GROUP)
            dve.wait_ge(S["conv_done"], 1)
            for t in range(NT):
                bk.wait_full(dve, "aq", t)
                src = bk("aq", t).rearrange("p (g j d) -> p g j d", g=KV, j=GROUP)
                dst = q_rot[:, t, :].rearrange("p (j g d) -> p g j d", g=KV, j=GROUP)
                for g in range(KV):
                    cs = lambda i, a, b: cos_sin[:, t, i, a:b].unsqueeze(1).broadcast_to([P, GROUP, b - a])
                    v.tensor_tensor(tmp[:, g, :, 0:32], src[:, g, :, 32:64], cs(1, 0, 32), ALU.mult)
                    v.tensor_tensor(tmp[:, g, :, 32:64], src[:, g, :, 0:32], cs(1, 32, 64), ALU.mult)
                    ins = v.tensor_tensor(dst[:, g, :, :], src[:, g, :, :], cs(0, 0, 64), ALU.mult)
                    if g == KV - 1:
                        bk.release(ins, "aq", t)
                        bk.wait_released(dve, "aq", t)
                    else:
                        step(ins)
                for g in range(KV):
                    ins = v.tensor_tensor(dst[:, g, :, :], dst[:, g, :, :], tmp[:, g, :, :], ALU.add)
                    if g == KV - 1:
                        ins.then_inc(S["qrot_done"], 1)
                        dve.wait_ge(S["qrot_done"], t + 1)
            tmp = junk[:, 0:128].rearrange("p (g d) -> p g d", g=KV)
            for t in range(NT):
                bk.wait_full(dve, "kv", t)
                src = bk("kv", t)[:, 0:P].rearrange("p (g d) -> p g d", g=KV)
                dst = k_rot[:, t, :].rearrange("p (g d) -> p g d", g=KV)
                cs = lambda i, a, b: cos_sin[:, t, i, a:b].unsqueeze(1).broadcast_to([P, KV, b - a])
                v.tensor_tensor(tmp[:, :, 0:32], src[:, :, 32:64], cs(1, 0, 32), ALU.mult)
                v.tensor_tensor(tmp[:, :, 32:64], src[:, :, 0:32], cs(1, 32, 64), ALU.mult)
                v.tensor_copy(v_att[:, t, :], bk("kv", t)[:, P:2 * P]).then_inc(S["v_done"], 1)
                ins = v.tensor_tensor(dst, src, cs(0, 0, 64), ALU.mult)
                bk.release(ins, "kv", t)
                bk.wait_released(dve, "kv", t)
                v.tensor_tensor(dst, dst, tmp, ALU.add).then_inc(S["krot_done"], 1)
                dve.wait_ge(S["krot_done"], t + 1)
            dve.wait_ge(S["silu_e"], 1)
            v.tensor_tensor(mqk[:], mqk[:], wide, ALU.mult).then_inc(S["mqk_ready"], 1)
            bk.wait_full(dve, "gi")
            bk.release(v.tensor_scalar(gate[:, I_, :], bk("gi")[0:MH, :], bias_if[:, 0:1], None, ALU.add), "gi")
            bk.wait_full(dve, "gf")
            ins = v.tensor_scalar(gate[:, F_, :], bk("gf")[0:MH, :], bias_if[:, 1:2], None, ALU.add)
            bk.release(ins, "gf")
            bk.wait_released(dve, "gf")
            v.scalar_tensor_tensor(out=gate[:, E_, :], in0=gate[:, F_, :], scalar=-1.0, in1=gate[:, F_, :],
                                   op0=ALU.mult, op1=ALU.max).then_inc(S["f_abs"], 1)
            dve.wait_ge(S["f_ln"], 1)
            step(v.scalar_tensor_tensor(out=gate[:, LF, :], in0=gate[:, F_, :], scalar=0.0, in1=gate[:, E_, :],
                                        op0=ALU.min, op1=ALU.subtract))
            dve.wait_ge(S["consts"], CONSTS)
            step(v.tensor_tensor_scan(gate[:, B_, :], gate[:, LF, :], zeros, 0.0, ALU.add, ALU.add))
            step(v.tensor_tensor_scan(gate[:, M_, :], gate[:, LF, :], gate[:, I_, :], 0.0, ALU.add, ALU.max))
            step(v.tensor_tensor(gate[:, R_, :], gate[:, B_, :], gate[:, M_, :], ALU.subtract))
            v.tensor_tensor(gate[:, CS, :], gate[:, I_, :], gate[:, B_, :], ALU.subtract).then_inc(S["gates_done"], 1)
            mod_row(GATE1, gg1, g_post)
            for t in range(NT):
                bk.wait_full(dve, "qT", t)
                ins = v.tensor_copy(qT[:, t, :, :], bk("qT", t).rearrange("p (j q) -> p j q", j=GROUP))
                bk.release(ins, "qT", t)
                bk.wait_released(dve, "qT", t)
            bk.wait_full(dve, "kT")
            ins = v.tensor_copy(kT[:], bk("kT"))
            bk.release(ins, "kT")
            bk.wait_released(dve, "kT")
            bk.wait_full(dve, "gcol")
            ins = v.tensor_copy(gcol[:], bk("gcol")[:, 0:NT * 8].rearrange("p (t i) -> p t i", t=NT))
            bk.release(ins, "gcol")
            def att_soft(n):
                keys = P if n == 0 else 2 * P
                if n >= 2:
                    bk.wait_full(dve, "pT", n - 2, 3)
                for name in scores(n):
                    _, _, g, jp = name
                    bk.wait_full(dve, *name)
                    h = g * GROUP + 2 * jp
                    ins = v.scalar_tensor_tensor(
                        out=sc[:, n % 2, h:h + 2, 0:keys], in0=bk(*name)[:, 0:2 * keys].rearrange("p (h s) -> p h s", h=2),
                        scalar=DH ** -0.5, in1=band[:, 2 * P - keys:2 * P].unsqueeze(1).broadcast_to([P, 2, keys]),
                        op0=ALU.mult, op1=ALU.add)
                    bk.release(ins, *name)
                for name in scores(n):
                    bk.wait_released(dve, *name)
                m = mx[:, n % 2, :, :]
                step(v.tensor_reduce(m[:, 0, :], sc[:, n % 2, :, 0:keys], AX, ALU.max))
                step(v.tensor_tensor(m[:, 0, :], m[:, 0, :], sinks[:], ALU.max))
                step(v.tensor_scalar(m[:, 1, :], m[:, 0, :], -1.0, None, ALU.mult))
                v.tensor_tensor(m[:, 2, :], sinks[:], m[:, 0, :], ALU.subtract).then_inc(S["att_max"], 1)

            def att_out(n):
                blocks = 1 if n == 0 else 2
                m = mx[:, n % 2, :, :]
                dve.wait_ge(S["att_exp"], n + 1)
                step(v.tensor_tensor(m[:, 5, :], m[:, 3, :], m[:, 4, :], ALU.add))
                step(v.reciprocal(m[:, 5, :], m[:, 5, :]))
                for i in range(2, 4):
                    name = ("pT", n, i)
                    bk.wait_full(dve, *name)
                    if n and i == 2:
                        bk.wait_full(dve, "av", n - 1)
                    ins = v.tensor_copy(pT[:, 2 * i:2 * i + 2, 0:blocks, :],
                                        bk(*name)[:, 0:2 * blocks * P].rearrange("p (h b q) -> p h b q", h=2, b=blocks))
                    bk.release(ins, *name)
                bk.wait_full(dve, "av", n)
                ins = v.tensor_tensor(both[:, n, 0:512].rearrange("p (h d) -> p h d", h=HEADS),
                                      bk("av", n).rearrange("p (h d) -> p h d", h=HEADS),
                                      m[:, 5, :].unsqueeze(2).broadcast_to([P, HEADS, DH]), ALU.mult)
                bk.release(ins, "av", n)

            def mlstm_weights(h):
                if h >= 2:
                    bk.wait_full(dve, "mv2", h - 2, 1)
                for s in range(NT):
                    n = T - s * P
                    bk.wait_full(dve, "ms", h, s)
                    dve.wait_ge(S["decay_done"], NT * h + s + 1)
                    ins = v.scalar_tensor_tensor(out=pm[:, h % 2, TRI[s] * P:TRI[s] * P + n], in0=bk("ms", h, s)[:, 0:n],
                                                 scalar=MQ ** -0.5, in1=decay[:, s % 2, 0:n], op0=ALU.mult, op1=ALU.mult)
                    bk.release(ins, "ms", h, s)

            def mlstm_out(h):
                dve.wait_ge(S["em_done"], 1)
                for i in range(2):
                    bk.wait_full(dve, "mv2", h, i)
                    src = bk("mv2", h, i)[:, 0:2 * (MV + 1)].rearrange("p (t v) -> p t v", t=2)
                    d = den[:, 2 * i:2 * i + 2].unsqueeze(2)
                    step(v.scalar_tensor_tensor(out=d, in0=src[:, :, MV:MV + 1], scalar=-1.0,
                                                in1=em[:, 2 * i:2 * i + 2, h:h + 1], op0=ALU.mult, op1=ALU.max))
                    step(v.tensor_tensor(d, src[:, :, MV:MV + 1], d, ALU.max))
                    step(v.reciprocal(d, d))
                    ins = v.tensor_tensor(wide[:, 2 * i:2 * i + 2, h * MV:(h + 1) * MV], src[:, :, 0:MV],
                                          d.broadcast_to([P, 2, MV]), ALU.mult)
                    bk.release(ins, "mv2", h, i)

            att_soft(0)
            mlstm_weights(0)
            mod_rowcopy(SCALE2)
            att_soft(1)
            att_out(0)
            mlstm_out(0)
            mlstm_weights(1)
            mod_col(SCALE2)
            mod_scale(SCALE2, 56)
            mod_rowcopy(SHIFT2)
            att_soft(2)
            att_out(1)
            mlstm_out(1)
            mlstm_weights(2)
            mod_col(SHIFT2)
            dve.wait_ge(S["g_post2_in"], 16)
            mod_row(GATE2, gg2, g_post)
            att_soft(3)
            att_out(2)
            mlstm_out(2)
            mlstm_weights(3)
            att_out(3)
            mlstm_out(3)
            bk.wait_released(dve, "mv2", 3, 1)
            heads = wide.rearrange("p t (h v) -> p t h v", h=MH)
            sq = junk.rearrange("p (t h v) -> p t h v", t=NT, h=MH)
            step(v.tensor_tensor(sq, heads, heads, ALU.mult))
            step(v.tensor_reduce(stat[:, 0, :].rearrange("p (t h) -> p t h", t=NT), sq, AX, ALU.add))
            mean_to_rstd(MV, 16)
            step(v.tensor_tensor(heads, heads, stat[:, 1, :].rearrange("p (t h) -> p t h", t=NT).unsqueeze(3)
                                 .broadcast_to([P, NT, MH, MV]), ALU.mult))
            step(v.tensor_tensor(wide, wide, m_norm[:].unsqueeze(1).broadcast_to([P, NT, MH * MV]), ALU.mult))
            for t in range(NT):
                bk.wait_released(dve, "mo", t)
            v.tensor_tensor(wide, wide, o_gate[:], ALU.mult).then_inc(S["mh_done"], 1)
            dve.wait_ge(S["mix_sq"], 2 * NT)
            step(v.tensor_reduce(stat[:, 0, 8:12], stat[:, 0, 0:8].rearrange("p (t h) -> p t h", t=NT), AX, ALU.add))
            step(v.tensor_copy(stat[:, 0, 0:4], stat[:, 0, 8:12]))
            mean_to_rstd(D, NT)
            for h in range(2):
                at = slice(h * 512, h * 512 + 512)
                for t in range(NT):
                    ins = v.scalar_tensor_tensor(out=both[:, t, at], in0=bk("out", h, t), scalar=stat[:, 1, t:t + 1],
                                                 in1=gg1[:, at], op0=ALU.mult, op1=ALU.mult)
                    bk.release(ins, "out", h, t)
                    bk.wait_released(dve, "out", h, t)
                    step(v.tensor_tensor(x_sb[:, t, at], x_sb[:, t, at], both[:, t, at], ALU.add))
            for t in range(NT):
                step(v.tensor_tensor_reduce(out=both[:, t, :], in0=x_sb[:, t, :], in1=x_sb[:, t, :], scale=1.0, scalar=0.0,
                                            op0=ALU.mult, op1=ALU.add, accum_out=stat[:, 0, t:t + 1]))
            mean_to_rstd(D, NT)
            for t in range(NT):
                v.tensor_scalar(both[:, t, :], x_sb[:, t, :], stat[:, 1, t:t + 1], None, ALU.mult).then_inc(S["xn2_ready"], 1)
            for c in range(1, DC, 2):
                bk.wait_full(dve, "h2T", c)
                ins = v.tensor_scalar(hT[:, c, :], bk("h2T", c), cols[:, SCALE2 * 8 + c:SCALE2 * 8 + c + 1],
                                      cols[:, SHIFT2 * 8 + c:SHIFT2 * 8 + c + 1], ALU.mult, ALU.add)
                bk.release(ins, "h2T", c)


RECTS = [(0, 1, 16), (1, 1, 8), (2, 1, 5), (3, 1, 4), (4, 1, 3), (5, 3, 2), (8, 8, 1)]


def query_block(nc, A, keep, s_all):
    hT, ident, hH, hL = keep["hT"], keep["ident"], keep["hH"], keep["hL"]
    with ExitStack() as ctx:
        def sb(name, shape, dt=F32):
            return ctx.enter_context(nc.sbuf_tensor(name, shape, dt))

        def sem(name):
            return ctx.enter_context(nc.semaphore(name))

        M = 2 * PH
        order = [("keys", i) for i in range(4)] + [("q", 0)]
        for m in range(M):
            order += ([("q", m + 1)] if m + 1 < M else []) + [("s", m)]
        psum = ctx.enter_context(nc.psum_tensor("query_psum", [P, 8, 512], F32))
        keys = sb("keys", [P, M, P])
        keysT = sb("keysT", [P, M, P])
        wq = sb("wq", [P, 2, DC, 2 * P])
        wqH = sb("wqH", [P, 2, DC, 2 * P], F32R)
        wqL = sb("wqL", [P, 2, DC, 2 * P], F32R)
        qT = sb("peer_qT", [P, 2, T])
        bank_full = [sem(f"q_bank_full{i}") for i in range(8)]
        bank_free = [sem(f"q_bank_free{i}") for i in range(8)]
        bk = Banks(psum, order, bank_full, bank_free)
        wq_in = [sem(f"wq_in{i}") for i in range(2)]
        keys_in, h_hi, h_lo, wq_hi, wq_lo = (sem(n) for n in ("keys_in", "h_hi", "h_lo", "wq_hi", "wq_lo"))
        block = ctx.enter_context(nc.Block())

        @block.sync
        def _(sp):
            for half, name in enumerate(("peer_keys1", "peer_keys2")):
                sp.dma_start(keys[:].rearrange("p (h two) d -> p h two d", two=2)[:, :, half, :],
                             A[name][0].rearrange("h k d -> k h d")).then_inc(keys_in, 16)
            for s in range(M // 2):
                if s >= 2:
                    sp.wait_ge(wq_lo, s - 1)
                sp.dma_start(wq[:, s % 2, :, :], A["peer_wq"][0, :, s * 2 * P:(s + 1) * 2 * P]
                             .rearrange("(c p) n -> p c n", p=P)).then_inc(wq_in[s % 2], 16)

        @block.scalar
        def _(act):
            func = nc.scalar.activation
            func(hH[:], hT[:], ACT.Copy).then_inc(h_hi, 1)

            def high(s):
                act.wait_ge(wq_in[s % 2], 16 * (s // 2 + 1))
                if s >= 2:
                    bk.wait_full(act, "q", 2 * s - 3)
                func(wqH[:, s % 2, :, :], wq[:, s % 2, :, :], ACT.Copy).then_inc(wq_hi, 1)

            high(0)
            for i in range(4):
                bk.wait_full(act, "keys", i)
                ins = func(keysT[:, 4 * i:4 * i + 4, :], bk("keys", i).rearrange("p (m k) -> p m k", m=4), ACT.Copy)
                bk.release(ins, "keys", i)
            high(1)
            for m in range(M):
                bk.wait_full(act, "q", m)
                if m >= 2:
                    bk.wait_full(act, "s", m - 2)
                bk.release(func(qT[:, m % 2, :], bk("q", m), ACT.Copy), "q", m)
                if m % 2 and m // 2 + 2 < M // 2:
                    high(m // 2 + 2)

        @block.vector
        def _(dve):
            v = nc.vector
            dve.wait_ge(h_hi, 1)
            v.tensor_tensor(hL[:], hT[:], hH[:].bitcast(F32), ALU.subtract).then_inc(h_lo, 1)

            def low(s):
                dve.wait_ge(wq_hi, s + 1)
                v.tensor_tensor(wqL[:, s % 2, :, :], wq[:, s % 2, :, :], wqH[:, s % 2, :, :].bitcast(F32),
                                ALU.subtract).then_inc(wq_lo, 1)

            low(0)
            low(1)
            for m in range(M):
                if m % 2 == 0 and m and m // 2 + 1 < M // 2:
                    low(m // 2 + 1)
                bk.wait_full(dve, "s", m)
                ins = v.tensor_copy(s_all[:, m, :, :], bk("s", m).rearrange("p (t k) -> p t k", t=NT))
                bk.release(ins, "s", m)

        @block.tensor
        def _(pe):
            mm, tr = nc.tensor.matmul, nc.tensor.transpose
            pe.wait_ge(keys_in, 32)
            for i in range(4):
                for k in range(4):
                    last = tr(bk("keys", i)[:, k * P:(k + 1) * P], keys[:, 4 * i + k, :], ident[:])
                bk.done(last, "keys", i)
            pe.wait_ge(h_lo, 1)

            def query(m):
                s = m // 2
                pe.wait_ge(wq_lo, s + 1)
                bk.wait_free(pe, "q", m)
                n = 0
                for c in range(DC):
                    at = slice((m % 2) * P, (m % 2) * P + P)
                    for w, h in ((wqH, hH), (wqH, hL), (wqL, hH)):
                        last = mm(bk("q", m), w[:, s % 2, c, at], h[:, c, :], start=(n == 0), stop=(n == 3 * DC - 1))
                        n += 1
                bk.done(last, "q", m)

            query(0)
            for m in range(M):
                if m + 1 < M:
                    query(m + 1)
                bk.wait_released(pe, "q", m)
                bk.wait_released(pe, "keys", m // 4)
                bk.wait_free(pe, "s", m)
                for t in range(NT):
                    last = mm(bk("s", m)[:, t * P:(t + 1) * P], qT[:, m % 2, t * P:(t + 1) * P], keysT[:, m, :],
                              start=True, stop=True)
                bk.done(last, "s", m)


def expert_block(nc, A, keep, s_all, S_dram, G_dram):
    ident, hH, hL = keep["ident"], keep["hH"], keep["hL"]
    with ExitStack() as ctx:
        def sb(name, shape, dt=F32):
            return ctx.enter_context(nc.sbuf_tensor(name, shape, dt))

        def sem(name):
            return ctx.enter_context(nc.semaphore(name))

        M = 2 * PH
        K = PH * PTOP
        val = sb("val", [P, 2, M, PTOP])
        idx = sb("idx", [P, M, PTOP], U32)
        idxf = sb("idxf", [P, M, PTOP])
        work = sb("work", [P, 4, P])
        cv = sb("cv", [P, PH, NCAND])
        ci = sb("ci", [P, PH, NCAND])
        top = sb("top", [P, NT, PH, PTOP])
        pos = sb("top_pos", [P, PH, PTOP], U32)
        posf = sb("top_posf", [P, PH, PTOP])
        hit = sb("hit", [P, 2, PTOP, NCAND])
        chosen = sb("chosen", [P, PH, PTOP])
        chosen_u = sb("chosen_u", [P, 2, K], U32)
        tsum = sb("tsum", [P, 2, NT, PH])
        sel = sb("sel", [P, NT, 2, K])
        selT = sb("selT", [P, 3, T])
        iota_i = sb("iota_i", [P, P], I32)
        iota = sb("iota", [P, P])
        onehot = sb("onehot", [P, 2, GT, 2, P])
        stage = s_all[:].rearrange("p m t k -> p (m t k)")[:, 0:2 * NBLK * TB].rearrange("p (a i t) -> p a i t", a=2, t=TB)
        ub = sb("ub", [P, 2, D])
        uF = sb("uF", [P, 2, D])
        uH = sb("uH", [P, 2, D], F32R)
        uL = sb("uL", [P, 2, D], F32R)
        act_out = sb("act_out", [P, 2, T])
        uT_ps = ctx.enter_context(nc.psum_tensor("uT_ps", [P, 2, D], F32))
        S_ps = ctx.enter_context(nc.psum_tensor("S_ps", [P, 2, T], F32))
        G_ps = ctx.enter_context(nc.psum_tensor("G_ps", [P, 2, 4, P], F32))

        u_in = [sem(f"u_in{i}") for i in range(2)]
        s_stored = [sem(f"s_stored{i}") for i in range(2)]
        g_stored = [sem(f"g_stored{i}") for i in range(2)]
        (u_turned, u_copied, u_low, u_done, s_ready, dve_chain, iota_ready, iota_done, top_ready, gate_exp, sel_ready, selT_full,
         selT_done, hot_ready, g_full, g_staged) = (sem(n) for n in (
            "u_turned", "u_copied", "u_low", "u_done", "s_ready", "x_dve_chain", "iota_ready", "iota_done", "top_ready", "gate_exp",
            "sel_ready", "selT_full", "selT_done", "hot_ready", "g_full", "g_staged"))
        block = ctx.enter_context(nc.Block())

        def blocks(eng, body):
            with eng.Fori(0, LEAD // 2) as i:
                for b in range(2):
                    body(2 * i + b, i, b, None)
            yield
            with eng.Fori(0, T // GT // 4) as i:
                for b in range(4):
                    body(LEAD + 4 * i + b, LEAD // 2 + 2 * i + b // 2, b % 2, (i, b))
            with eng.Fori((LEAD + T // GT) // 2, NBLK // 2 - 1) as i:
                for b in range(2):
                    body(2 * i + b, i, b, None)
            for b in range(2):
                body(NBLK - 2 + b, NBLK // 2 - 1, b, None)

        @block.sync
        def _(sp):
            for b in range(2):
                sp.sem_inc(s_stored[b], 16)
                sp.sem_inc(g_stored[b], 16)

            def load(n, b):
                sp.dma_start(ub[:, b, :], A["peer_u"][0, bass.ds(n * P, P), :]).then_inc(u_in[b], 16)

            for b in range(2):
                load(b, b)

            def body(n, pair, b, g):
                if not isinstance(n, int):
                    sp.wait_ge(u_turned, n + 3)
                    load(n + 2, b)
                sp.wait_ge(s_ready, n + 3)
                sp.dma_start(S_dram[bass.ds(n, 1), :, :].rearrange("a p t -> p (a t)"), act_out[:, b, :]).then_inc(s_stored[b], 16)
                if g is not None and g[1] % 2:
                    i, k = g
                    sp.wait_ge(g_staged, 4 * i + k + 2)
                    sp.dma_start(G_dram[:, :, bass.ds(2 * i + k // 2, 1), :].rearrange("g p a n -> p g (a n)"),
                                 stage[:, k // 2, :, :].rearrange("p (g i) t -> p g (i t)", g=NBG)).then_inc(g_stored[k // 2], 16)

            for _ in blocks(sp, body):
                pass
            for b in range(2):
                sp.wait_ge(s_stored[b], 16 * (NBLK // 2 + 1))
                sp.wait_ge(g_stored[b], 16 * (NTB // 2 + 1))

        @block.gpsimd
        def _(pool):
            pool.sem_inc(u_low, 2)
            nc.gpsimd.iota(iota_i[:], pattern=[[1, P]], base=0, channel_multiplier=0).then_inc(iota_ready, 1)

            def body(n, pair, b, g):
                pool.wait_ge(u_copied, n + 3)
                pool.wait_ge(u_done, n + 1)
                nc.gpsimd.tensor_tensor(uL[:, b, :], uF[:, b, :], uH[:, b, :].bitcast(F32), ALU.subtract).then_inc(u_low, 1)

            for _ in blocks(pool, body):
                pass

        @block.scalar
        def _(act):
            func = nc.scalar.activation
            act.sem_inc(u_copied, 2)
            act.sem_inc(s_ready, 2)

            def copy(n, b):
                act.wait_ge(u_turned, n + 3)
                act.wait_ge(u_low, n + 1)
                func(uF[:, b, :], uT_ps[:, b, :], ACT.Copy)
                act.wait_ge(u_done, n + 1)
                func(uH[:, b, :], uT_ps[:, b, :], ACT.Copy).then_inc(u_copied, 1)

            def body(n, pair, b, g):
                if not (isinstance(n, int) and n == NBLK - 1):
                    copy(n + 1, 1 - b)
                act.wait_ge(u_done, n + 3)
                act.wait_ge(s_stored[b], 16 * pair + 16)
                func(act_out[:, b, :], S_ps[:, b, :], ACT.Gelu).then_inc(s_ready, 1)

            copy(0, 0)
            for _ in blocks(act, body):
                act.wait_ge(top_ready, 1)
                func(top[:], top[:], ACT.Exp).then_inc(gate_exp, 1)

        @block.tensor
        def _(pe):
            mm, tr = nc.tensor.matmul, nc.tensor.transpose
            pe.sem_inc(u_turned, 2)
            pe.sem_inc(u_done, 2)
            pe.sem_inc(g_full, 2)

            def turn(n, pair, b):
                pe.wait_ge(u_in[b], 16 * pair + 16)
                pe.wait_ge(u_copied, n + 1)
                for c in range(DC):
                    last = tr(uT_ps[:, b, c * P:(c + 1) * P], ub[:, b, c * P:(c + 1) * P], ident[:])
                last.then_inc(u_turned, 1)

            def body(n, pair, b, g):
                if not (isinstance(n, int) and n == NBLK - 1):
                    turn(n + 1, pair + b, 1 - b)
                pe.wait_ge(u_low, n + 3)
                pe.wait_ge(s_ready, n + 1)
                k = 0
                for c in range(DC):
                    for w, h in ((uH, hH), (uH, hL), (uL, hH)):
                        last = mm(S_ps[:, b, :], w[:, b, c * P:(c + 1) * P], h[:, c, :], start=(k == 0), stop=(k == 3 * DC - 1))
                        k += 1
                last.then_inc(u_done, 1)
                if g is not None:
                    m = 4 * g[0] + g[1]
                    pe.wait_ge(hot_ready, m + 1)
                    pe.wait_ge(g_staged, m + 1)
                    for k in range(GT):
                        last = mm(G_ps[:, k // 4, k % 4, :], onehot[:, b, k, 1, :], onehot[:, b, k, 0, :], start=True, stop=True)
                    last.then_inc(g_full, 1)

            turn(0, 0, 0)
            for _ in blocks(pe, body):
                pe.wait_ge(sel_ready, 1)
                for i in range(3):
                    if i == 2:
                        pe.wait_ge(selT_done, 1)
                    for t in range(NT):
                        src = sel[:, t, i, :] if i < 2 else top[:, t, :, :].rearrange("p h k -> p (h k)")
                        last = tr(G_ps[:, i % 2, t, :], src, ident[:])
                    last.then_inc(selT_full, 1)

        @block.vector
        def _(dve):
            v = nc.vector
            step = Chain(dve, dve_chain)
            dve.sem_inc(g_staged, 1)
            dve.wait_ge(iota_ready, 1)
            step(v.tensor_copy(iota[:], iota_i[:]))

            def largest(rows):
                for values, indices, src, spare in rows:
                    step.put(v.max(values[:, 0:8], src))
                step.wait()
                for values, indices, src, spare in rows:
                    step.put(v.match_replace(spare, values[:, 0:8], src, -3.0e38))
                for values, indices, src, spare in rows:
                    step.put(v.max_index(indices[:, 0:8], values[:, 0:8], src))
                step.wait()
                for values, indices, src, spare in rows:
                    step.put(v.max(values[:, 8:16], spare))
                step.wait()
                for values, indices, src, spare in rows:
                    step.put(v.max_index(indices[:, 8:16], values[:, 8:16], spare))
                step.wait()

            for t in range(NT):
                for m in range(0, M, 4):
                    largest([(val[:, t % 2, m + i, :], idx[:, m + i, :], s_all[:, m + i, t, :], work[:, i, :]) for i in range(4)])
                step(v.tensor_copy(idxf[:], idx[:]))
                halves = lambda x, i: x.rearrange("p (h two) k -> p h two k", two=2)[:, :, i, :]
                v1, v2, i1, i2 = halves(val[:, t % 2, :, :], 0), halves(val[:, t % 2, :, :], 1), halves(idxf[:], 0), halves(idxf[:], 1)
                step(v.tensor_scalar(i1, i1, float(PK), None, ALU.mult))
                at = 0
                for a, na, nb in RECTS:
                    for dst, x, y in ((cv, v1, v2), (ci, i1, i2)):
                        step.put(v.tensor_tensor(dst[:, :, at:at + na * nb].rearrange("p h (a b) -> p h a b", a=na),
                                             x[:, :, a:a + na].unsqueeze(3).broadcast_to([P, PH, na, nb]),
                                             y[:, :, 0:nb].unsqueeze(2).broadcast_to([P, PH, na, nb]), ALU.add))
                    at += na * nb
                step.wait()
                for h in range(0, PH, 4):
                    largest([(top[:, t, h + i, :], pos[:, h + i, :], cv[:, h + i, :], work[:, i, 0:NCAND]) for i in range(4)])
                step(v.tensor_copy(posf[:], pos[:]))
                for h in range(0, PH, 2):
                    place = posf[:, h:h + 2, :].unsqueeze(3).broadcast_to([P, 2, PTOP, NCAND])
                    step(v.tensor_tensor(hit[:], iota[:, 0:NCAND].unsqueeze(1).unsqueeze(1).broadcast_to([P, 2, PTOP, NCAND]),
                                         place, ALU.is_equal))
                    step(v.tensor_tensor(hit[:], hit[:], ci[:, h:h + 2, :].unsqueeze(2).broadcast_to([P, 2, PTOP, NCAND]), ALU.mult))
                    step(v.tensor_reduce(chosen[:, h:h + 2, :], hit[:], AX, ALU.add))
                step(v.tensor_copy(chosen_u[:, 0, :], chosen[:].rearrange("p h k -> p (h k)")))
                step(v.tensor_scalar(chosen_u[:, 1, :], chosen_u[:, 0, :], 7, None, ALU.logical_shift_right))
                step(v.tensor_copy(sel[:, t, 0, :], chosen_u[:, 1, :]))
                step(v.tensor_scalar(chosen_u[:, 1, :], chosen_u[:, 0, :], PK - 1, None, ALU.bitwise_and))
                step(v.tensor_copy(sel[:, t, 1, :], chosen_u[:, 1, :]))
            step(v.tensor_copy(tsum[:, 0, :, :], top[:, :, :, 0]))
            flat = top[:].rearrange("p t h k -> p (t h) k")
            sums = lambda i: tsum[:, i, :, :].rearrange("p t h -> p (t h)")
            over = lambda x: x.unsqueeze(2).broadcast_to([P, NT * PH, PTOP])
            v.tensor_tensor(flat, flat, over(sums(0)), ALU.subtract).then_inc(top_ready, 1)
            dve.wait_ge(gate_exp, 1)
            step(v.tensor_reduce(sums(0), flat, AX, ALU.add))
            step(v.reciprocal(sums(1), sums(0)))
            v.tensor_tensor(flat, flat, over(sums(1)), ALU.mult).then_inc(sel_ready, 1)
            for i in range(3):
                dve.wait_ge(selT_full, i + 1)
                v.tensor_copy(selT[:, i, :], G_ps[:, i % 2, :, :].rearrange("p t k -> p (t k)")).then_inc(selT_done, 1)
            dve.wait_ge(selT_done, 3)
            with dve.Fori(0, T // GT // 4) as i:
                for b in range(4):
                    m = 4 * i + b
                    dve.wait_ge(g_full, m + 1)
                    for k in range(GT):
                        t = GT * m + k
                        col = lambda j: selT[:, j, bass.ds(t, 1)]
                        v.tensor_scalar(onehot[:, b % 2, k, 1, :], iota[:], col(1), None, ALU.is_equal)
                        ins = v.tensor_scalar(onehot[:, b % 2, k, 0, :], iota[:], col(0), col(2), ALU.is_equal, ALU.mult)
                    ins.then_inc(hot_ready, 1)
                    if b % 2 == 0:
                        dve.wait_ge(g_stored[b // 2], 16 * i + 16)
                    dve.wait_ge(g_full, m + 3)
                    for q in range(2):
                        t0 = (b % 2) * GT + q * 4
                        ins = v.tensor_copy(stage[:, b // 2, :, t0:t0 + 4].rearrange("p i t -> p t i"), G_ps[:, q, :, :])
                    ins.then_inc(g_staged, 1)


def value_block(nc, A, keep, S_dram, G_dram, out):
    x_sb, gg2 = keep["x"], keep["gg2"]
    with ExitStack() as ctx:
        def sb(name, shape, dt=F32):
            return ctx.enter_context(nc.sbuf_tensor(name, shape, dt))

        def sem(name):
            return ctx.enter_context(nc.semaphore(name))

        y_ps = ctx.enter_context(nc.psum_tensor("y_ps", [P, NT, 2, 512], F32))
        vb = sb("vb", [P, 2, D])
        vH = sb("vH", [P, 2, D], F32R)
        vL = sb("vL", [P, 2, D], F32R)
        sbuf = sb("s_in", [P, 2, T])
        gbuf = sb("g_in", [P, 2, NTB, BG, TB])
        a = sb("a", [P, 2, T])
        aH = sb("aH", [P, 2, T], F32R)
        aL = sb("aL", [P, 2, T], F32R)
        nothing = sb("nothing", [P, 512], F32R)
        y = sb("y", [P, NT, D])
        sq = sb("sq", [P, 512])
        stat = sb("y_stat", [P, 5, 8])
        v_in = [sem(f"v_in{i}") for i in range(2)]
        s_in = [sem(f"s_in_done{i}") for i in range(2)]
        g_in = [sem(f"g_in_done{i}") for i in range(2)]
        out_done = [sem(f"out_done{i}") for i in range(NT)]
        nothing_ready, v_hi, v_lo, a_ready, a_hi, a_lo, v_done, y_done, y_sq, chain, out_ready = (
            sem(n) for n in ("nothing_ready", "v_hi", "v_lo", "a_ready", "a_hi", "a_lo", "v_done", "y_done", "y_sq",
                             "y_dve_chain", "out_ready"))
        block = ctx.enter_context(nc.Block())

        def blocks(eng, body):
            with eng.Fori(0, NBG // 2) as i:
                for gb in range(2):
                    with eng.Fori(0, BG // 2) as j:
                        for b in range(2):
                            body(i * (2 * BG) + gb * BG + 2 * j + b, i * BG + gb * (BG // 2) + j, b, i, gb, j)

        @block.sync
        def _(sp):
            def body(n, pair, b, i, gb, j):
                sp.wait_ge(v_lo, n + 1)
                sp.dma_start(vb[:, b, :], A["peer_v"][0, bass.ds(n * P, P), :]).then_inc(v_in[b], 16)
                sp.wait_ge(a_ready, n + 1)
                sp.dma_start(sbuf[:, b, :], S_dram[bass.ds(n, 1), :, :].rearrange("a p t -> p (a t)")).then_inc(s_in[b], 16)

            blocks(sp, body)
            for t in range(NT):
                sp.wait_ge(out_ready, t + 1)
                sp.dma_start(out[0, t * P:(t + 1) * P, :], y[:, t, :]).then_inc(out_done[t], 16)
            for t in range(NT):
                sp.wait_ge(out_done[t], 16)

        @block.gpsimd
        def _(pool):
            nc.gpsimd.memset(nothing[:].bitcast(F32), 0.0).then_inc(nothing_ready, 1)
            for gb in range(2):
                pool.dma_start(gbuf[:, gb, :, :, :].rearrange("p q b t -> p (q b t)"),
                               G_dram[gb].rearrange("p q n -> p (q n)")).then_inc(g_in[gb], 16)
            with pool.Fori(0, NBG // 2 - 1) as i:
                for gb in range(2):
                    pool.wait_ge(a_ready, i * (2 * BG) + gb * BG + BG + 2)
                    pool.dma_start(gbuf[:, gb, :, :, :].rearrange("p q b t -> p (q b t)"),
                                   G_dram[bass.ds(2 * i + 2 + gb, 1), :, :, :].rearrange("a p q n -> p (a q n)")).then_inc(g_in[gb], 16)

        @block.scalar
        def _(act):
            func = nc.scalar.activation
            act.sem_inc(a_hi, 2)

            def body(n, pair, b, i, gb, j):
                act.wait_ge(v_in[b], 16 * pair + 16)
                act.wait_ge(v_done, n + 1)
                func(vH[:, b, :], vb[:, b, :], ACT.Copy).then_inc(v_hi, 1)
                act.wait_ge(a_ready, n + 3)
                func(aH[:, b, :], a[:, b, :], ACT.Copy).then_inc(a_hi, 1)

            blocks(act, body)
            act.wait_ge(y_done, 1)
            for t in range(NT):
                for h in range(2):
                    func(sq[:], y_ps[:, t, h, :], ACT.Square, accum_out=stat[:, 0, 2 * t + h:2 * t + h + 1]).then_inc(y_sq, 1)
                    act.wait_ge(y_sq, 2 * t + h + 1)

        @block.vector
        def _(dve):
            v = nc.vector
            step = Chain(dve, chain)
            dve.sem_inc(v_lo, 2)
            dve.sem_inc(a_ready, 2)
            dve.sem_inc(a_lo, 2)

            def body(n, pair, b, i, gb, j):
                dve.wait_ge(s_in[b], 16 * pair + 16)
                dve.wait_ge(g_in[gb], 16 * i + 16)
                dve.wait_ge(a_hi, n + 1)
                v.tensor_tensor(a[:, b, :].rearrange("p (q t) -> p q t", t=TB),
                                sbuf[:, b, :].rearrange("p (q t) -> p q t", t=TB),
                                gbuf[:, gb, :, bass.ds(2 * j + b, 1), :].rearrange("p q a t -> p q (a t)"),
                                ALU.mult).then_inc(a_ready, 1)
                dve.wait_ge(v_hi, n + 1)
                v.tensor_tensor(vL[:, b, :], vb[:, b, :], vH[:, b, :].bitcast(F32), ALU.subtract).then_inc(v_lo, 1)
                dve.wait_ge(a_hi, n + 3)
                v.tensor_tensor(aL[:, b, :], a[:, b, :], aH[:, b, :].bitcast(F32), ALU.subtract).then_inc(a_lo, 1)

            blocks(dve, body)
            dve.wait_ge(y_sq, 2 * NT)
            step(v.tensor_reduce(stat[:, 1, 0:NT], stat[:, 0, :].rearrange("p (t h) -> p t h", t=NT), AX, ALU.add))
            step(v.tensor_scalar(stat[:, 2, 0:NT], stat[:, 1, 0:NT], 1.0 / D, EPS, ALU.mult, ALU.add))
            rsqrt(nc, step, stat[:, 1, 0:NT], stat[:, 2, 0:NT], stat[:, 3, 0:NT], stat[:, 4, 0:NT])
            for t in range(NT):
                for h in range(2):
                    step(v.scalar_tensor_tensor(out=y[:, t, h * 512:(h + 1) * 512], in0=y_ps[:, t, h, :],
                                                scalar=stat[:, 1, t:t + 1], in1=gg2[:, h * 512:(h + 1) * 512],
                                                op0=ALU.mult, op1=ALU.mult))
                v.tensor_tensor(y[:, t, :], y[:, t, :], x_sb[:, t, :], ALU.add).then_inc(out_ready, 1)

        @block.tensor
        def _(pe):
            mm = nc.tensor.matmul
            pe.sem_inc(v_done, 2)
            pe.wait_ge(nothing_ready, 1)
            for t in range(NT):
                for h in range(2):
                    mm(y_ps[:, t, h, :], nothing[:, 0:P], nothing[:], start=True, stop=False)

            def body(n, pair, b, i, gb, j):
                pe.wait_ge(a_lo, n + 3)
                pe.wait_ge(v_lo, n + 3)
                for t in range(NT):
                    for x, w in ((aH, vH), (aH, vL), (aL, vH)):
                        for h in range(2):
                            last = mm(y_ps[:, t, h, :], x[:, b, t * P:(t + 1) * P], w[:, b, h * 512:(h + 1) * 512],
                                      start=False, stop=False)
                last.then_inc(v_done, 1)

            blocks(pe, body)
            for t in range(NT):
                for h in range(2):
                    last = mm(y_ps[:, t, h, :], nothing[:, 0:P], nothing[:], start=False, stop=True)
            last.then_inc(y_done, 1)


def build(nc, A, out):
    with ExitStack() as ctx:
        def sb(name, shape, dt=F32):
            return ctx.enter_context(nc.sbuf_tensor(name, shape, dt))

        keep = dict(x=sb("x_sb", [P, NT, D]), hT=sb("hT", [P, DC, T]), ident=sb("ident", [P, P]),
                    cols=sb("cols", [P, 88]), gg2=sb("gg2", [P, D]))
        S_dram = nc.dram_tensor("gelu_table", (NBLK, P, T), F32, kind="Internal").ap()
        G_dram = nc.dram_tensor("gate_table", (NBG, P, NTB, BG * TB), F32, kind="Internal").ap()
        mix_block(nc, A, keep)
        with ExitStack() as peer:
            keep["hH"] = peer.enter_context(nc.sbuf_tensor("hH", [P, DC, T], F32R))
            keep["hL"] = peer.enter_context(nc.sbuf_tensor("hL", [P, DC, T], F32R))
            s_all = peer.enter_context(nc.sbuf_tensor("s_all", [P, 2 * PH, NT, P], F32))
            query_block(nc, A, keep, s_all)
            expert_block(nc, A, keep, s_all, S_dram, G_dram)
        value_block(nc, A, keep, S_dram, G_dram, out)


_INS = ["x", "c", "positions", "w_mod", "b_mod", "g_pre_mix", "g_post_mix", "w_in", "conv_w", "b_igate", "b_fgate",
        "mlstm_norm_g", "att_sinks", "w_out", "g_pre_ffn", "g_post_ffn", "peer_wq", "peer_keys1", "peer_keys2",
        "peer_u", "peer_v"]


def kernel(**inputs):
    import numpy as np
    import concourse.bacc as bacc
    from concourse.bass_utils import run_bass_kernel_spmd

    nc = bacc.Bacc("TRN2", target_bir_lowering=False, num_devices=1)
    arrays, A = {}, {}
    for name in _INS:
        a = np.ascontiguousarray(inputs[name])
        arrays[f"in_{name}"] = a
        A[name] = nc.dram_tensor(f"in_{name}", a.shape, mybir.dt.from_np(a.dtype), kind="ExternalInput").ap()
    inv = np.float32(10000.0) ** (-np.arange(0, DH, 2, dtype=np.float32) / np.float32(DH))
    arrays["in_inv_freq"] = inv.astype(np.float32)
    A["inv_freq"] = nc.dram_tensor("in_inv_freq", inv.shape, F32, kind="ExternalInput").ap()
    out = nc.dram_tensor("out_0", (1, T, D), F32, kind="ExternalOutput").ap()
    build(nc, A, out)
    r = run_bass_kernel_spmd(nc, [arrays], core_ids=[0])
    return r.results[0]["out_0"]
```

```python
from contextlib import ExitStack

import concourse.bass as bass
from concourse import mybir

F32 = mybir.dt.float32
F32R = mybir.dt.float32r
I32 = mybir.dt.int32
U32 = mybir.dt.uint32
ALU = mybir.AluOpType
ACT = mybir.ActivationFunctionType
AX = mybir.AxisListType.X

P = 128
T = 512
NT = T // P
D = 1024
DC = D // P
HEADS, KV, DH = 8, 2, 64
GROUP = HEADS // KV
MH, MV, MQ = 4, 128, 64
TAPS = 4
NEG = -1.0e30
EPS = 1e-6
PI = 3.141592653589793
TWO_PI_HI, TWO_PI_MID = 6.28125, 0.0019350051879882812
TWO_PI_LO = 2 * PI - TWO_PI_HI - TWO_PI_MID
ROUND = 12582912.0

C_AQ, C_AK, C_MQ, C_MV, C_MI, C_MF, C_MO, C_END = 0, 512, 768, 1280, 1792, 1796, 1800, 2312
SHIFT1, SCALE1, GATE1, SHIFT2, SCALE2, GATE2 = range(6)

PH, PK, PTOP = 8, 128, 16
NE = PK * PK
NBLK = NE // P
CAND = [(a, b) for a in range(PTOP) for b in range(PTOP) if (a + 1) * (b + 1) <= PTOP]
NCAND = len(CAND)
K = PH * PTOP
TD = T - P
NTD = TD // P
GT = 6
GSTEPS = TD // GT
TB = 2 * GT
NTB = TD // TB
BG = 16
NBG = NBLK // BG
LEAD = 56
RING = 4
LEAD_ROWS = 48
TAIL = NBLK - LEAD - GSTEPS
assert LEAD_ROWS + GSTEPS + 2 * TAIL == K


class Chain:

    def __init__(self, eng, sem):
        self.eng, self.sem, self.n = eng, sem, 0

    def put(self, ins):
        self.n += 1
        ins.then_inc(self.sem, 1)

    def wait(self):
        self.eng.wait_ge(self.sem, self.n)

    def __call__(self, ins):
        self.put(ins)
        self.wait()


class Banks:

    def __init__(self, psum, order, full, free):
        self.psum, self.full, self.free, self.n = psum, full, free, len(full)
        self.number = {name: i for i, name in enumerate(order)}
        assert len(self.number) == len(order)

    def __call__(self, *name):
        return self.psum[:, self.number[name] % self.n, :]

    def wait_free(self, pe, *name):
        k = self.number[name]
        if k >= self.n:
            pe.wait_ge(self.free[k % self.n], k // self.n)

    def wait_full(self, eng, *name):
        k = self.number[name]
        eng.wait_ge(self.full[k % self.n], k // self.n + 1)

    def wait_released(self, eng, *name):
        k = self.number[name]
        eng.wait_ge(self.free[k % self.n], k // self.n + 1)

    def done(self, ins, *name):
        ins.then_inc(self.full[self.number[name] % self.n], 1)

    def release(self, ins, *name):
        ins.then_inc(self.free[self.number[name] % self.n], 1)


def rsqrt(nc, step, y, a, half_a, t):
    step(nc.vector.tensor_scalar(t.bitcast(U32), a.bitcast(U32), 1, None, ALU.logical_shift_right))
    step(nc.vector.tensor_scalar(y.bitcast(I32), t.bitcast(I32), -1.0, float(0x5F3759DF), ALU.mult, ALU.add))
    step(nc.vector.tensor_scalar(half_a, a, -0.5, None, ALU.mult))
    for _ in range(3):
        step(nc.vector.tensor_tensor(t, y, y, ALU.mult))
        step(nc.vector.tensor_tensor(t, t, half_a, ALU.mult))
        step(nc.vector.scalar_tensor_tensor(out=y, in0=t, scalar=1.5, in1=y, op0=ALU.add, op1=ALU.mult))


def mix_block(nc, A, keep):
    x_sb, hT, ident, cols, gg2 = keep["x"], keep["hT"], keep["ident"], keep["cols"], keep["gg2"]
    with ExitStack() as ctx:
        def sb(name, shape, dt=F32):
            return ctx.enter_context(nc.sbuf_tensor(name, shape, dt))

        def sem(name):
            return ctx.enter_context(nc.semaphore(name))

        slabs = [("mod", s, h) for s in (SCALE1, SHIFT1) for h in range(2)]
        slabs += [("in", C_MQ), ("in", C_AQ), ("in", C_AK), ("in", C_MV), ("in", C_MO)]
        slabs += [("mod", s, h) for s in (GATE1, SCALE2, SHIFT2, GATE2) for h in range(2)]
        slabs += [("out", h) for h in range(2)]
        NW = 3
        slab_no = {s: i for i, s in enumerate(slabs)}

        scores = lambda n: [("sc", n, g, jp) for g in range(KV) for jp in range(2)]
        probsT = lambda n: [("pT", n, i) for i in range(4)]
        mscore = lambda h: [("ms", h, s) for s in range(NT)]
        mvalue = lambda h: [("mv2", h, i) for i in range(2)]
        modr = lambda s: [("modr", s, h) for h in range(2)]
        modg = lambda s: [("modg", s, h) for h in range(2)]
        order = [("rows",)] + [("xT", c) for c in range(DC)] + modr(SCALE1) + modr(SHIFT1)
        order += [("modc", SCALE1), ("modc", SHIFT1)]
        order += [("mq", j) for j in range(4)] + [(k, t) for k in ("aq", "kv") for t in range(NT)]
        order += [("gi",), ("gf",)] + [(k, t) for k in ("mv", "mo") for t in range(NT)]
        order += modg(GATE1) + [("qT", t) for t in range(NT)] + [("kT",)]
        order += [("gcol",)] + [("rb", h) for h in range(MH)]
        order += scores(0) + mscore(0) + modr(SCALE2)
        order += scores(1) + probsT(0) + [("av", 0)] + mvalue(0) + mscore(1)
        order += [("modc", SCALE2)] + modr(SHIFT2)
        order += scores(2) + probsT(1) + [("av", 1)] + mvalue(1) + mscore(2)
        order += [("modc", SHIFT2)] + modg(GATE2)
        order += scores(3) + probsT(2) + [("av", 2)] + mvalue(2) + mscore(3)
        order += probsT(3) + [("av", 3)] + mvalue(3)
        order += [("mixT", c) for c in range(DC)] + [("out", h, t) for h in range(2) for t in range(NT)]
        order += [("h2T", c) for c in range(DC)]
        last_use = {("mod", s, h): ("modr", s, h) for s in (SCALE1, SHIFT1, SCALE2, SHIFT2) for h in range(2)}
        last_use |= {("mod", s, h): ("modg", s, h) for s in (GATE1, GATE2) for h in range(2)}
        last_use |= {("in", C_MQ): ("mq", 3), ("in", C_AQ): ("aq", 3), ("in", C_AK): ("kv", 3),
                     ("in", C_MV): ("mv", 3), ("in", C_MO): ("mo", 3)}
        last_use |= {("out", h): ("out", h, 3) for h in range(2)}

        psum = ctx.enter_context(nc.psum_tensor("mix_psum", [P, 8, 512], F32))
        slab = sb("slab", [P, NW, DC, 520])
        rows = sb("rows", [88, P])
        c_rep = sb("c_rep", [P, DC, P])
        bias_if = sb("bias_if", [MH, 2])
        pos_i = sb("pos_i", [P, NT], I32)
        pos = sb("pos", [P, NT])
        inv_freq = sb("inv_freq", [P, DH // 2])
        sinks = sb("sinks", [P, HEADS])
        g_post = sb("g_post", [P, D])
        gg1 = sb("gg1", [P, D])
        m_norm = sb("m_norm", [P, MH * MV])
        mod_r = sb("mod_r", [1, D])
        stat = sb("stat", [P, 5, 16])
        angle = sb("angle", [P, 3, NT, DH // 2])
        trig = sb("trig", [P, 2, NT, DH // 2])
        cos_sin = sb("cos_sin", [P, NT, 2, DH])
        band = sb("band", [P, 2 * P])
        pick = sb("pick", [MH, MH, P])
        late = sb("late", [P, 2048 + 2 * 10 * P])
        gate = late[0:MH, 0:8 * T].rearrange("h (i t) -> h i t", i=8)
        I_, F_, E_, LF, B_, M_, R_, CS = range(8)
        zeros = late[0:MH, 8 * T:9 * T]
        gcol = sb("gcol", [P, NT, 8])
        em = sb("em", [P, NT, MH])
        both = sb("both", [P, NT, D])
        q_rot = both[:, :, 0:512]
        wide = both[:, :, 512:1024]
        k_rot = sb("k_rot", [P, NT, KV * DH])
        v_att = sb("v_att", [P, NT, KV * DH])
        qT = sb("qT", [P, NT, GROUP, P])
        mod_place = lambda s: qT[0:1, :, :, :].rearrange("a t g q -> a (t g q)")[:, 0:D] if s == SHIFT1 else mod_r[:]
        kT = sb("kT", [P, T])
        v_ext = sb("v_ext", [P, NT, MH, MV + 1])
        o_gate = sb("o_gate", [P, NT, MH * MV])
        mqk = sb("mqk", [P, 4, T])
        rr = hT
        r_all = rr[:, 0:4, :]
        r_diag = rr[:, 4:8, :].rearrange("p h (b t) -> p h b t", b=NT)
        decay = sb("decay", [P, 2, T])
        TRI = [0, 4, 7, 9]
        pm = late[:, 2048:2048 + 20 * P].rearrange("p (a n) -> p a n", a=2)
        sc = sb("sc", [P, 2, HEADS, 2 * P])
        conv_in = sc[:, :, :, :].rearrange("p a b c -> p (a b c)")[:, 0:4 * 515].rearrange("p (j t) -> p j t", j=4)
        junk = sc[:, :, :, :].rearrange("p a b c -> p (a b c)")[:, 0:2048]
        pT = late[:, 0:2048].rearrange("p (h b q) -> p h b q", h=HEADS, b=2)
        mx = sb("mx", [P, 2, 6, HEADS])
        den = sb("den", [P, 4])

        bank_full = [sem(f"bank_full{i}") for i in range(8)]
        bank_free = [sem(f"bank_free{i}") for i in range(8)]
        bk = Banks(psum, order, bank_full, bank_free)
        slab_in = [sem(f"slab_in{i}") for i in range(NW)]
        x_in = [sem(f"x_in{i}") for i in range(NT)]
        names = ("rows_in bc_in small_in dve_chain act_chain pool_chain consts xn_ready c_ready angles trig_done "
                 "hT_ready f_abs f_exp f_ln gates_done diag_done em_done conv_pad conv_done silu_e mqk_ready "
                 "g_post2_in decay_done qrot_done krot_done v_done att_max att_exp mh_done mix_sq xn2_ready").split()
        S = {n: sem(n) for n in names}

        block = ctx.enter_context(nc.Block())

        def slab_of(name):
            return slab[:, slab_no[name] % NW, :, :]

        def wait_slab(pe, name):
            n = slab_no[name]
            pe.wait_ge(slab_in[n % NW], 16 * (n // NW + 1))

        @block.sync
        def _(sp):
            for t in range(NT):
                sp.dma_start(x_sb[:, t, :], A["x"][0, t * P:(t + 1) * P, :]).then_inc(x_in[t], 16)
            sp.dma_start(rows[0:48, :], A["b_mod"][0].rearrange("(r p) -> r p", p=P)).then_inc(S["rows_in"], 16)
            sp.dma_start(rows[48:56, :], A["g_pre_mix"][0].rearrange("(r p) -> r p", p=P)).then_inc(S["rows_in"], 16)
            sp.dma_start(rows[56:64, :], A["g_pre_ffn"][0].rearrange("(r p) -> r p", p=P)).then_inc(S["rows_in"], 16)
            sp.dma_start(rows[64:80, :], A["conv_w"][0].rearrange("j (r p) -> (j r) p", p=P)).then_inc(S["rows_in"], 16)
            sp.dma_start(rows[80:88, :], A["c"][0].rearrange("(r p) -> r p", p=P)).then_inc(S["rows_in"], 16)
            for n, name in enumerate(slabs):
                if n >= NW:
                    bk.wait_full(sp, *last_use[slabs[n - NW]])
                if name[0] == "mod":
                    src, c0, w = A["w_mod"], name[1] * D + name[2] * 512, 512
                elif name[0] == "in":
                    src, c0 = A["w_in"], name[1]
                    w = {C_MQ: 512, C_AQ: 512, C_AK: 256, C_MV: 520, C_MO: 512}[c0]
                else:
                    src, c0, w = A["w_out"], name[1] * 512, 512
                sp.dma_start(slab_of(name)[:, :, 0:w],
                             src[0, :, c0:c0 + w].rearrange("(c p) n -> p c n", p=P)).then_inc(slab_in[n % NW], 16)

        @block.gpsimd
        def _(pool):
            step = Chain(pool, S["pool_chain"])
            pool.dma_start(pos_i[:], A["positions"][0].rearrange("(t p) -> p t", p=P), allow_slow_non_contiguous=True).then_inc(S["small_in"], 16)
            pool.dma_start(bias_if[:, 0:1], A["b_igate"].rearrange("a h -> h a"), allow_slow_non_contiguous=True).then_inc(S["small_in"], 16)
            pool.dma_start(bias_if[:, 1:2], A["b_fgate"].rearrange("a h -> h a"), allow_slow_non_contiguous=True).then_inc(S["small_in"], 16)
            step(nc.gpsimd.memset(ident[:], 0.0))
            nc.gpsimd.affine_select(out=ident[:], in_=ident[:], compare_op=ALU.not_equal, fill=1.0, base=0,
                                    pattern=[[-1, P]], channel_multiplier=1).then_inc(S["consts"], 1)
            nc.gpsimd.memset(conv_in[:, :, 0:3], 0.0).then_inc(S["conv_pad"], 1)
            nc.gpsimd.memset(zeros, 0.0).then_inc(S["consts"], 1)
            nc.gpsimd.memset(v_ext[:, :, :, MV:MV + 1], 1.0).then_inc(S["consts"], 1)
            step(nc.gpsimd.memset(pick[:], 1.0))
            nc.gpsimd.affine_select(out=pick[:], in_=pick[:], compare_op=ALU.is_equal, fill=0.0, base=0,
                                    pattern=[[-1, MH], [0, P]], channel_multiplier=1).then_inc(S["consts"], 1)
            step(nc.gpsimd.memset(band[:], 0.0))
            step(nc.gpsimd.affine_select(out=band[:], in_=band[:], compare_op=ALU.is_gt, fill=NEG, base=0,
                                         pattern=[[1, 2 * P]], channel_multiplier=-1))
            nc.gpsimd.affine_select(out=band[:], in_=band[:], compare_op=ALU.is_ge, fill=NEG, base=P,
                                    pattern=[[-1, 2 * P]], channel_multiplier=1).then_inc(S["consts"], 1)
            for h in range(MH):
                bk.wait_released(pool, "rb", h)
                nc.gpsimd.affine_select(out=r_diag[:, h, :, :], in_=r_all[:, h, :].rearrange("p (b t) -> p b t", b=NT),
                                        compare_op=ALU.is_ge, fill=NEG, base=0, pattern=[[0, NT], [1, P]],
                                        channel_multiplier=-1).then_inc(S["diag_done"], 1)

        CONSTS = 5

        @block.tensor
        def _(pe):
            mm, tr = nc.tensor.matmul, nc.tensor.transpose
            pe.wait_ge(S["consts"], 1)
            pe.wait_ge(S["rows_in"], 80)
            bk.done(tr(bk("rows")[:, 0:88], rows[:], ident[0:88, 0:88]), "rows")
            pe.wait_ge(S["xn_ready"], NT)
            for c in range(DC):
                bk.wait_free(pe, "xT", c)
                for t in range(NT):
                    last = tr(bk("xT", c)[:, t * P:(t + 1) * P], both[:, t, c * P:(c + 1) * P], ident[:])
                bk.done(last, "xT", c)

            def mod_row1(s, h):
                wait_slab(pe, ("mod", s, h))
                bk.wait_free(pe, "modr", s, h)
                for c in range(DC):
                    last = mm(bk("modr", s, h)[0:1, :], cols[:, 80 + c:81 + c], slab_of(("mod", s, h))[:, c, 0:512],
                              start=(c == 0), stop=(c == DC - 1))
                bk.done(last, "modr", s, h)

            def mod_columns(s):
                for h in range(2):
                    bk.wait_released(pe, "modr", s, h)
                bk.wait_free(pe, "modc", s)
                for j in range(8):
                    last = mm(bk("modc", s)[:, j:j + 1], mod_place(s)[:, j * P:(j + 1) * P], ident[0:1, 0:1],
                              start=True, stop=True)
                bk.done(last, "modc", s)

            def mod_rows(s):
                for h in range(2):
                    wait_slab(pe, ("mod", s, h))
                    bk.wait_free(pe, "modg", s, h)
                    for c in range(DC):
                        last = mm(bk("modg", s, h), c_rep[:, c, :], slab_of(("mod", s, h))[:, c, 0:512],
                                  start=(c == 0), stop=(c == DC - 1))
                    bk.done(last, "modg", s, h)

            pe.wait_ge(S["c_ready"], 1)
            for s in (SCALE1, SHIFT1):
                for h in range(2):
                    mod_row1(s, h)
            mod_columns(SCALE1)
            mod_columns(SHIFT1)
            pe.wait_ge(S["hT_ready"], DC)
            w = slab_of(("in", C_MQ))
            wait_slab(pe, ("in", C_MQ))
            order_of_gates = (("gi", C_MI), ("gf", C_MF))
            for j in range(4):
                bk.wait_free(pe, "mq", j)
                for c in range(DC):
                    last = mm(bk("mq", j), w[:, c, j * P:(j + 1) * P], hT[:, c, :], start=(c == 0), stop=(c == DC - 1))
                bk.done(last, "mq", j)
            for kind, c0, width in (("aq", C_AQ, 512), ("kv", C_AK, 256)):
                w = slab_of(("in", c0))
                wait_slab(pe, ("in", c0))
                for t in range(NT):
                    bk.wait_free(pe, kind, t)
                    for c in range(DC):
                        last = mm(bk(kind, t)[:, 0:width], hT[:, c, t * P:(t + 1) * P], w[:, c, 0:width],
                                  start=(c == 0), stop=(c == DC - 1))
                    bk.done(last, kind, t)
            w = slab_of(("in", C_MV))
            wait_slab(pe, ("in", C_MV))
            for name, col in order_of_gates:
                bk.wait_free(pe, name)
                for c in range(DC):
                    last = mm(bk(name)[0:MH, :], w[:, c, col - C_MV:col - C_MV + MH], hT[:, c, :],
                              start=(c == 0), stop=(c == DC - 1))
                bk.done(last, name)
            for kind, c0, width in (("mv", C_MV, 512), ("mo", C_MO, 512)):
                w = slab_of(("in", c0))
                wait_slab(pe, ("in", c0))
                for t in range(NT):
                    bk.wait_free(pe, kind, t)
                    for c in range(DC):
                        last = mm(bk(kind, t)[:, 0:width], hT[:, c, t * P:(t + 1) * P], w[:, c, 0:width],
                                  start=(c == 0), stop=(c == DC - 1))
                    bk.done(last, kind, t)
            mod_rows(GATE1)
            for t in range(NT):
                pe.wait_ge(S["qrot_done"], t + 1)
                bk.wait_free(pe, "qT", t)
                for j in range(GROUP):
                    last = tr(bk("qT", t)[:, j * P:(j + 1) * P], q_rot[:, t, j * P:(j + 1) * P], ident[:])
                bk.done(last, "qT", t)
            pe.wait_ge(S["krot_done"], NT)
            bk.wait_free(pe, "kT")
            for t in range(NT):
                last = tr(bk("kT")[:, t * P:(t + 1) * P], k_rot[:, t, :], ident[:])
            bk.done(last, "kT")
            pe.wait_ge(S["gates_done"], 1)
            bk.wait_free(pe, "gcol")
            for t in range(NT):
                for i, row in enumerate((CS, M_)):
                    last = tr(bk("gcol")[:, t * 8 + i * 4:t * 8 + i * 4 + 4], gate[:, row, t * P:(t + 1) * P], ident[0:MH, 0:MH])
            bk.done(last, "gcol")
            pe.wait_ge(S["consts"], CONSTS)
            for h in range(MH):
                bk.wait_free(pe, "rb", h)
                bk.done(mm(bk("rb", h), pick[:, h, :], gate[:, R_, :], start=True, stop=True), "rb", h)

            def att_scores(n):
                k0 = max(n - 1, 0) * P
                wide_ = (n + 1) * P - k0
                bk.wait_released(pe, "qT", n)
                bk.wait_released(pe, "kT")
                for name in scores(n):
                    _, _, g, jp = name
                    bk.wait_free(pe, *name)
                    for i in range(2):
                        last = mm(bk(*name)[:, i * wide_:(i + 1) * wide_], qT[g * DH:(g + 1) * DH, n, jp * 2 + i, :],
                                  kT[g * DH:(g + 1) * DH, k0:k0 + wide_], start=True, stop=True)
                    bk.done(last, *name)

            def att_values(n):
                pe.wait_ge(S["att_exp"], n + 1)
                blocks = 1 if n == 0 else 2
                for i, name in enumerate(probsT(n)):
                    bk.wait_free(pe, *name)
                    for hh in range(2):
                        for b in range(blocks):
                            at = (hh * blocks + b) * P
                            last = tr(bk(*name)[:, at:at + P], sc[:, n % 2, 2 * i + hh, b * P:(b + 1) * P], ident[:])
                    bk.done(last, *name)
                for name in probsT(n):
                    bk.wait_released(pe, *name)
                pe.wait_ge(S["v_done"], NT)
                bk.wait_free(pe, "av", n)
                for h in range(HEADS):
                    for b in range(blocks):
                        last = mm(bk("av", n)[:, h * DH:(h + 1) * DH], pT[:, h, b, :],
                                  v_att[:, n - blocks + 1 + b, (h // GROUP) * DH:(h // GROUP + 1) * DH],
                                  start=(b == 0), stop=(b == blocks - 1))
                bk.done(last, "av", n)

            def mlstm_scores(h):
                pe.wait_ge(S["mqk_ready"], 1)
                p0 = (h % 2) * MQ
                for s in range(NT):
                    bk.wait_free(pe, "ms", h, s)
                    bk.done(mm(bk("ms", h, s)[:, 0:T - s * P], mqk[p0:p0 + MQ, 2 + h // 2, s * P:(s + 1) * P],
                               mqk[p0:p0 + MQ, h // 2, s * P:T], start=True, stop=True), "ms", h, s)

            def mlstm_values(h):
                for s in range(NT):
                    bk.wait_released(pe, "ms", h, s)
                    bk.wait_released(pe, "mv", s)
                for i in range(2):
                    bk.wait_free(pe, "mv2", h, i)
                    for tt in range(2):
                        t = 2 * i + tt
                        for s in range(t + 1):
                            at = (TRI[s] + t - s) * P
                            last = mm(bk("mv2", h, i)[:, tt * (MV + 1):(tt + 1) * (MV + 1)], pm[:, h % 2, at:at + P],
                                      v_ext[:, s, h, :], start=(s == 0), stop=(s == t))
                    bk.done(last, "mv2", h, i)

            att_scores(0)
            mlstm_scores(0)
            mod_row1(SCALE2, 0)
            mod_row1(SCALE2, 1)
            att_scores(1)
            att_values(0)
            mlstm_values(0)
            mlstm_scores(1)
            mod_columns(SCALE2)
            mod_row1(SHIFT2, 0)
            mod_row1(SHIFT2, 1)
            att_scores(2)
            att_values(1)
            mlstm_values(1)
            mlstm_scores(2)
            mod_columns(SHIFT2)
            mod_rows(GATE2)
            att_scores(3)
            att_values(2)
            mlstm_values(2)
            mlstm_scores(3)
            att_values(3)
            mlstm_values(3)
            for c in range(DC):
                if c < 4:
                    for n in range(NT):
                        bk.wait_released(pe, "av", n)
                else:
                    pe.wait_ge(S["mh_done"], 1)
                bk.wait_free(pe, "mixT", c)
                for t in range(NT):
                    last = tr(bk("mixT", c)[:, t * P:(t + 1) * P], both[:, t, c * P:(c + 1) * P], ident[:])
                bk.done(last, "mixT", c)
            for c in range(DC):
                bk.wait_released(pe, "mixT", c)
            for h in range(2):
                wait_slab(pe, ("out", h))
                for t in range(NT):
                    bk.wait_free(pe, "out", h, t)
                    for c in range(DC):
                        last = mm(bk("out", h, t), rr[:, c, t * P:(t + 1) * P], slab_of(("out", h))[:, c, 0:512],
                                  start=(c == 0), stop=(c == DC - 1))
                    bk.done(last, "out", h, t)
            pe.wait_ge(S["xn2_ready"], NT)
            for c in range(DC):
                bk.wait_free(pe, "h2T", c)
                for t in range(NT):
                    last = tr(bk("h2T", c)[:, t * P:(t + 1) * P], both[:, t, c * P:(c + 1) * P], ident[:])
                bk.done(last, "h2T", c)

        @block.scalar
        def _(act):
            func = nc.scalar.activation
            step = Chain(act, S["act_chain"])
            for dst, src in ((inv_freq, A["inv_freq"]), (sinks, A["att_sinks"][0]), (gg1, A["b_mod"][0, GATE1 * D:(GATE1 + 1) * D]),
                             (g_post, A["g_post_mix"][0]), (gg2, A["b_mod"][0, GATE2 * D:(GATE2 + 1) * D]),
                             (m_norm, A["mlstm_norm_g"][0].rearrange("h v -> (h v)"))):
                act.dma_start(dst[:], src.partition_broadcast(P)).then_inc(S["bc_in"], 16)
            act.wait_ge(S["angles"], 1)
            func(trig[:].rearrange("p a t f -> p (a t f)"), angle[:, 1:3, :, :].rearrange("p a t f -> p (a t f)"),
                 ACT.Sin).then_inc(S["trig_done"], 1)
            for c in range(DC):
                bk.wait_full(act, "xT", c)
                ins = func(hT[:, c, :], bk("xT", c), ACT.Copy)
                bk.release(ins, "xT", c)
            act.wait_ge(S["conv_pad"], 1)
            act.wait_ge(S["xn_ready"], NT)
            for j in range(4):
                bk.wait_full(act, "mq", j)
                bk.release(func(conv_in[:, j, 3:3 + T], bk("mq", j), ACT.Copy), "mq", j)
            act.wait_ge(S["conv_done"], 1)
            func(wide, mqk[:], ACT.Sigmoid).then_inc(S["silu_e"], 1)
            act.wait_ge(S["f_abs"], 1)
            func(gate[:, E_, :], gate[:, E_, :], ACT.Exp, scale=-1.0).then_inc(S["f_exp"], 1)
            act.wait_ge(S["f_exp"], 1)
            func(gate[:, E_, :], gate[:, E_, :], ACT.Ln, bias=1.0).then_inc(S["f_ln"], 1)
            act.wait_ge(S["consts"], CONSTS)
            for t in range(NT):
                bk.wait_full(act, "mv", t)
                ins = func(v_ext[:, t, :, 0:MV], bk("mv", t).rearrange("p (h v) -> p h v", h=MH), ACT.Copy)
                bk.release(ins, "mv", t)
            for t in range(NT):
                bk.wait_full(act, "mo", t)
                bk.release(func(o_gate[:, t, :], bk("mo", t), ACT.Sigmoid), "mo", t)
            for h in range(MH):
                bk.wait_full(act, "rb", h)
                bk.release(func(r_all[:, h, :], bk("rb", h), ACT.Copy), "rb", h)
            bk.wait_released(act, "gcol")
            act.dma_start(g_post[:], A["g_post_ffn"][0].partition_broadcast(P)).then_inc(S["g_post2_in"], 16)
            func(em[:], gcol[:, :, 4:8], ACT.Exp, scale=-1.0).then_inc(S["em_done"], 1)

            def att_exp(n):
                act.wait_ge(S["att_max"], n + 1)
                keys = P if n == 0 else 2 * P
                for h in range(HEADS):
                    func(sc[:, n % 2, h, 0:keys], sc[:, n % 2, h, 0:keys], ACT.Exp, bias=mx[:, n % 2, 1, h:h + 1],
                         accum_out=mx[:, n % 2, 3, h:h + 1])
                func(mx[:, n % 2, 4, :], mx[:, n % 2, 2, :], ACT.Exp).then_inc(S["att_exp"], 1)

            def probs_T(n):
                blocks = 1 if n == 0 else 2
                for i in range(2):
                    name = ("pT", n, i)
                    bk.wait_full(act, *name)
                    if n and i == 0:
                        bk.wait_full(act, "av", n - 1)
                    ins = func(pT[:, 2 * i:2 * i + 2, 0:blocks, :],
                               bk(*name)[:, 0:2 * blocks * P].rearrange("p (h b q) -> p h b q", h=2, b=blocks), ACT.Copy)
                    bk.release(ins, *name)

            def decays(h):
                act.wait_ge(S["diag_done"], h + 1)
                for s in range(NT):
                    k = h * NT + s - 2
                    if k >= 0:
                        bk.wait_released(act, "ms", k // NT, k % NT)
                    bias = gcol[:, s, h:h + 1]
                    ins = func(decay[:, s % 2, 0:P], r_diag[:, h, s, :], ACT.Exp, bias=bias)
                    if s < NT - 1:
                        ins = func(decay[:, s % 2, P:T - s * P], r_all[:, h, (s + 1) * P:T], ACT.Exp, bias=bias)
                    ins.then_inc(S["decay_done"], 1)

            decays(0)
            att_exp(0)
            att_exp(1)
            probs_T(0)
            decays(1)
            att_exp(2)
            probs_T(1)
            decays(2)
            att_exp(3)
            probs_T(2)
            decays(3)
            probs_T(3)
            for c in range(DC):
                bk.wait_full(act, "mixT", c)
                bk.release(func(rr[:, c, :], bk("mixT", c), ACT.Copy), "mixT", c)
            for h in range(2):
                for t in range(NT):
                    bk.wait_full(act, "out", h, t)
                    func(sc[:, 0, 0:2, :], bk("out", h, t).rearrange("p (a b) -> p a b", a=2), ACT.Square,
                         accum_out=stat[:, 0, 2 * t + h:2 * t + h + 1]).then_inc(S["mix_sq"], 1)
                    act.wait_ge(S["mix_sq"], NT * h + t + 1)
            for c in range(0, DC, 2):
                bk.wait_full(act, "h2T", c)
                ins = func(hT[:, c, :], bk("h2T", c), ACT.Identity, scale=cols[:, SCALE2 * 8 + c:SCALE2 * 8 + c + 1],
                           bias=cols[:, SHIFT2 * 8 + c:SHIFT2 * 8 + c + 1])
                bk.release(ins, "h2T", c)

        @block.vector
        def _(dve):
            v = nc.vector
            step = Chain(dve, S["dve_chain"])

            def mean_to_rstd(width, n):
                step(v.tensor_scalar(stat[:, 2, 0:n], stat[:, 0, 0:n], 1.0 / width, EPS, ALU.mult, ALU.add))
                rsqrt(nc, step, stat[:, 1, 0:n], stat[:, 2, 0:n], stat[:, 3, 0:n], stat[:, 4, 0:n])

            for t in range(NT):
                dve.wait_ge(x_in[t], 16)
                step(v.tensor_tensor_reduce(out=both[:, t, :], in0=x_sb[:, t, :], in1=x_sb[:, t, :], scale=1.0, scalar=0.0,
                                            op0=ALU.mult, op1=ALU.add, accum_out=stat[:, 0, t:t + 1]))
            mean_to_rstd(D, NT)
            for t in range(NT):
                v.tensor_scalar(both[:, t, :], x_sb[:, t, :], stat[:, 1, t:t + 1], None, ALU.mult).then_inc(S["xn_ready"], 1)
            bk.wait_full(dve, "rows")
            ins = v.tensor_copy(cols[:, 0:88], bk("rows")[:, 0:88])
            bk.release(ins, "rows")
            bk.wait_released(dve, "rows")
            v.tensor_copy(c_rep[:], cols[:, 80:88].unsqueeze(2).broadcast_to([P, DC, P])).then_inc(S["c_ready"], 1)
            dve.wait_ge(S["small_in"], 48)
            dve.wait_ge(S["bc_in"], 6 * 16)
            step(v.tensor_copy(pos[:], pos_i[:]))
            for t in range(NT):
                step(v.tensor_scalar(angle[:, 0, t, :], inv_freq[:], pos[:, t:t + 1], None, ALU.mult))
            for i, quarter in ((2, 0.0), (1, 0.25)):
                a, k = angle[:, i, :, :], trig[:, 0, :, :]
                step(v.tensor_scalar(k, angle[:, 0, :, :], 1.0 / (2 * PI), quarter, ALU.mult, ALU.add))
                step(v.tensor_scalar(k, k, ROUND, None, ALU.add))
                step(v.tensor_scalar(k, k, ROUND, None, ALU.subtract))
                step(v.scalar_tensor_tensor(out=a, in0=k, scalar=-TWO_PI_HI, in1=angle[:, 0, :, :], op0=ALU.mult, op1=ALU.add))
                for part in (TWO_PI_MID, TWO_PI_LO):
                    step(v.scalar_tensor_tensor(out=a, in0=k, scalar=-part, in1=a, op0=ALU.mult, op1=ALU.add))
                if quarter:
                    step(v.tensor_scalar(a, a, PI / 2, None, ALU.add))
                ins = v.tensor_scalar(a, a, 3.1415925, -3.1415925, ALU.min, ALU.max)
                if quarter:
                    ins.then_inc(S["angles"], 1)
                else:
                    step(ins)
            dve.wait_ge(S["trig_done"], 1)
            for half in range(2):
                v.tensor_copy(cos_sin[:, :, 0, half * 32:half * 32 + 32], trig[:, 0, :, :])
            v.tensor_copy(cos_sin[:, :, 1, 32:64], trig[:, 1, :, :])
            step(v.tensor_scalar(cos_sin[:, :, 1, 0:32], trig[:, 1, :, :], -1.0, None, ALU.mult))

            def mod_rowcopy(s):
                for half in range(2):
                    bk.wait_full(dve, "modr", s, half)
                    ins = v.tensor_copy(mod_place(s)[:, half * 512:half * 512 + 512], bk("modr", s, half)[0:1, :])
                    bk.release(ins, "modr", s, half)

            def mod_col(s):
                a = s * 8
                bk.wait_full(dve, "modc", s)
                ins = v.tensor_tensor(cols[:, a:a + 8], bk("modc", s)[:, 0:8], cols[:, a:a + 8], ALU.add)
                bk.release(ins, "modc", s)
                bk.wait_released(dve, "modc", s)

            def mod_scale(s, g0):
                a = s * 8
                step(v.scalar_tensor_tensor(out=cols[:, a:a + 8], in0=cols[:, a:a + 8], scalar=1.0, in1=cols[:, g0:g0 + 8],
                                            op0=ALU.add, op1=ALU.mult))

            def mod_row(s, dst, g):
                for half in range(2):
                    at = slice(half * 512, half * 512 + 512)
                    bk.wait_full(dve, "modg", s, half)
                    ins = v.tensor_tensor(dst[:, at], bk("modg", s, half), dst[:, at], ALU.add)
                    bk.release(ins, "modg", s, half)
                    bk.wait_released(dve, "modg", s, half)
                    step(v.tensor_tensor(dst[:, at], dst[:, at], g[:, at], ALU.mult))

            mod_rowcopy(SCALE1)
            mod_rowcopy(SHIFT1)
            mod_col(SCALE1)
            mod_scale(SCALE1, 48)
            mod_col(SHIFT1)
            for c in range(DC):
                bk.wait_released(dve, "xT", c)
                v.tensor_scalar(hT[:, c, :], hT[:, c, :], cols[:, 8 * SCALE1 + c:8 * SCALE1 + c + 1],
                                cols[:, 8 * SHIFT1 + c:8 * SHIFT1 + c + 1], ALU.mult, ALU.add).then_inc(S["hT_ready"], 1)
            for j in range(4):
                bk.wait_released(dve, "mq", j)
                acc = mqk[:, j, :]
                step(v.tensor_scalar(acc, conv_in[:, j, 0:T], cols[:, 64 + j:65 + j], None, ALU.mult))
                for tap in range(1, TAPS):
                    w = cols[:, 64 + tap * 4 + j:65 + tap * 4 + j]
                    ins = v.scalar_tensor_tensor(out=acc, in0=conv_in[:, j, tap:tap + T], scalar=w, in1=acc,
                                                 op0=ALU.mult, op1=ALU.add)
                    if j == 3 and tap == TAPS - 1:
                        ins.then_inc(S["conv_done"], 1)
                    else:
                        step(ins)
            tmp = junk[:, 0:512].rearrange("p (g j d) -> p g j d", g=KV, j=GROUP)
            dve.wait_ge(S["conv_done"], 1)
            for t in range(NT):
                bk.wait_full(dve, "aq", t)
                src = bk("aq", t).rearrange("p (g j d) -> p g j d", g=KV, j=GROUP)
                dst = q_rot[:, t, :].rearrange("p (j g d) -> p g j d", g=KV, j=GROUP)
                for g in range(KV):
                    cs = lambda i, a, b: cos_sin[:, t, i, a:b].unsqueeze(1).broadcast_to([P, GROUP, b - a])
                    v.tensor_tensor(tmp[:, g, :, 0:32], src[:, g, :, 32:64], cs(1, 0, 32), ALU.mult)
                    v.tensor_tensor(tmp[:, g, :, 32:64], src[:, g, :, 0:32], cs(1, 32, 64), ALU.mult)
                    ins = v.tensor_tensor(dst[:, g, :, :], src[:, g, :, :], cs(0, 0, 64), ALU.mult)
                    if g == KV - 1:
                        bk.release(ins, "aq", t)
                        bk.wait_released(dve, "aq", t)
                    else:
                        step(ins)
                for g in range(KV):
                    ins = v.tensor_tensor(dst[:, g, :, :], dst[:, g, :, :], tmp[:, g, :, :], ALU.add)
                    if g == KV - 1:
                        ins.then_inc(S["qrot_done"], 1)
                        dve.wait_ge(S["qrot_done"], t + 1)
            tmp = junk[:, 0:128].rearrange("p (g d) -> p g d", g=KV)
            for t in range(NT):
                bk.wait_full(dve, "kv", t)
                src = bk("kv", t)[:, 0:P].rearrange("p (g d) -> p g d", g=KV)
                dst = k_rot[:, t, :].rearrange("p (g d) -> p g d", g=KV)
                cs = lambda i, a, b: cos_sin[:, t, i, a:b].unsqueeze(1).broadcast_to([P, KV, b - a])
                v.tensor_tensor(tmp[:, :, 0:32], src[:, :, 32:64], cs(1, 0, 32), ALU.mult)
                v.tensor_tensor(tmp[:, :, 32:64], src[:, :, 0:32], cs(1, 32, 64), ALU.mult)
                v.tensor_copy(v_att[:, t, :], bk("kv", t)[:, P:2 * P]).then_inc(S["v_done"], 1)
                ins = v.tensor_tensor(dst, src, cs(0, 0, 64), ALU.mult)
                bk.release(ins, "kv", t)
                bk.wait_released(dve, "kv", t)
                v.tensor_tensor(dst, dst, tmp, ALU.add).then_inc(S["krot_done"], 1)
                dve.wait_ge(S["krot_done"], t + 1)
            dve.wait_ge(S["silu_e"], 1)
            v.tensor_tensor(mqk[:], mqk[:], wide, ALU.mult).then_inc(S["mqk_ready"], 1)
            bk.wait_full(dve, "gi")
            bk.release(v.tensor_scalar(gate[:, I_, :], bk("gi")[0:MH, :], bias_if[:, 0:1], None, ALU.add), "gi")
            bk.wait_full(dve, "gf")
            ins = v.tensor_scalar(gate[:, F_, :], bk("gf")[0:MH, :], bias_if[:, 1:2], None, ALU.add)
            bk.release(ins, "gf")
            bk.wait_released(dve, "gf")
            v.scalar_tensor_tensor(out=gate[:, E_, :], in0=gate[:, F_, :], scalar=-1.0, in1=gate[:, F_, :],
                                   op0=ALU.mult, op1=ALU.max).then_inc(S["f_abs"], 1)
            dve.wait_ge(S["f_ln"], 1)
            step(v.scalar_tensor_tensor(out=gate[:, LF, :], in0=gate[:, F_, :], scalar=0.0, in1=gate[:, E_, :],
                                        op0=ALU.min, op1=ALU.subtract))
            dve.wait_ge(S["consts"], CONSTS)
            step(v.tensor_tensor_scan(gate[:, B_, :], gate[:, LF, :], zeros, 0.0, ALU.add, ALU.add))
            step(v.tensor_tensor_scan(gate[:, M_, :], gate[:, LF, :], gate[:, I_, :], 0.0, ALU.add, ALU.max))
            step(v.tensor_tensor(gate[:, R_, :], gate[:, B_, :], gate[:, M_, :], ALU.subtract))
            v.tensor_tensor(gate[:, CS, :], gate[:, I_, :], gate[:, B_, :], ALU.subtract).then_inc(S["gates_done"], 1)
            mod_row(GATE1, gg1, g_post)
            for t in range(NT):
                bk.wait_full(dve, "qT", t)
                ins = v.tensor_copy(qT[:, t, :, :], bk("qT", t).rearrange("p (j q) -> p j q", j=GROUP))
                bk.release(ins, "qT", t)
                bk.wait_released(dve, "qT", t)
            bk.wait_full(dve, "kT")
            ins = v.tensor_copy(kT[:], bk("kT"))
            bk.release(ins, "kT")
            bk.wait_released(dve, "kT")
            bk.wait_full(dve, "gcol")
            ins = v.tensor_copy(gcol[:], bk("gcol")[:, 0:NT * 8].rearrange("p (t i) -> p t i", t=NT))
            bk.release(ins, "gcol")
            def att_soft(n):
                keys = P if n == 0 else 2 * P
                if n >= 2:
                    bk.wait_full(dve, "pT", n - 2, 3)
                for name in scores(n):
                    _, _, g, jp = name
                    bk.wait_full(dve, *name)
                    h = g * GROUP + 2 * jp
                    ins = v.scalar_tensor_tensor(
                        out=sc[:, n % 2, h:h + 2, 0:keys], in0=bk(*name)[:, 0:2 * keys].rearrange("p (h s) -> p h s", h=2),
                        scalar=DH ** -0.5, in1=band[:, 2 * P - keys:2 * P].unsqueeze(1).broadcast_to([P, 2, keys]),
                        op0=ALU.mult, op1=ALU.add)
                    bk.release(ins, *name)
                for name in scores(n):
                    bk.wait_released(dve, *name)
                m = mx[:, n % 2, :, :]
                step(v.tensor_reduce(m[:, 0, :], sc[:, n % 2, :, 0:keys], AX, ALU.max))
                step(v.tensor_tensor(m[:, 0, :], m[:, 0, :], sinks[:], ALU.max))
                step(v.tensor_scalar(m[:, 1, :], m[:, 0, :], -1.0, None, ALU.mult))
                v.tensor_tensor(m[:, 2, :], sinks[:], m[:, 0, :], ALU.subtract).then_inc(S["att_max"], 1)

            def att_out(n):
                blocks = 1 if n == 0 else 2
                m = mx[:, n % 2, :, :]
                dve.wait_ge(S["att_exp"], n + 1)
                step(v.tensor_tensor(m[:, 5, :], m[:, 3, :], m[:, 4, :], ALU.add))
                step(v.reciprocal(m[:, 5, :], m[:, 5, :]))
                for i in range(2, 4):
                    name = ("pT", n, i)
                    bk.wait_full(dve, *name)
                    if n and i == 2:
                        bk.wait_full(dve, "av", n - 1)
                    ins = v.tensor_copy(pT[:, 2 * i:2 * i + 2, 0:blocks, :],
                                        bk(*name)[:, 0:2 * blocks * P].rearrange("p (h b q) -> p h b q", h=2, b=blocks))
                    bk.release(ins, *name)
                bk.wait_full(dve, "av", n)
                ins = v.tensor_tensor(both[:, n, 0:512].rearrange("p (h d) -> p h d", h=HEADS),
                                      bk("av", n).rearrange("p (h d) -> p h d", h=HEADS),
                                      m[:, 5, :].unsqueeze(2).broadcast_to([P, HEADS, DH]), ALU.mult)
                bk.release(ins, "av", n)

            def mlstm_weights(h):
                if h >= 2:
                    bk.wait_full(dve, "mv2", h - 2, 1)
                for s in range(NT):
                    n = T - s * P
                    bk.wait_full(dve, "ms", h, s)
                    dve.wait_ge(S["decay_done"], NT * h + s + 1)
                    ins = v.scalar_tensor_tensor(out=pm[:, h % 2, TRI[s] * P:TRI[s] * P + n], in0=bk("ms", h, s)[:, 0:n],
                                                 scalar=MQ ** -0.5, in1=decay[:, s % 2, 0:n], op0=ALU.mult, op1=ALU.mult)
                    bk.release(ins, "ms", h, s)

            def mlstm_out(h):
                dve.wait_ge(S["em_done"], 1)
                for i in range(2):
                    bk.wait_full(dve, "mv2", h, i)
                    src = bk("mv2", h, i)[:, 0:2 * (MV + 1)].rearrange("p (t v) -> p t v", t=2)
                    d = den[:, 2 * i:2 * i + 2].unsqueeze(2)
                    step(v.scalar_tensor_tensor(out=d, in0=src[:, :, MV:MV + 1], scalar=-1.0,
                                                in1=em[:, 2 * i:2 * i + 2, h:h + 1], op0=ALU.mult, op1=ALU.max))
                    step(v.tensor_tensor(d, src[:, :, MV:MV + 1], d, ALU.max))
                    step(v.reciprocal(d, d))
                    ins = v.tensor_tensor(wide[:, 2 * i:2 * i + 2, h * MV:(h + 1) * MV], src[:, :, 0:MV],
                                          d.broadcast_to([P, 2, MV]), ALU.mult)
                    bk.release(ins, "mv2", h, i)

            att_soft(0)
            mlstm_weights(0)
            mod_rowcopy(SCALE2)
            att_soft(1)
            att_out(0)
            mlstm_out(0)
            mlstm_weights(1)
            mod_col(SCALE2)
            mod_scale(SCALE2, 56)
            mod_rowcopy(SHIFT2)
            att_soft(2)
            att_out(1)
            mlstm_out(1)
            mlstm_weights(2)
            mod_col(SHIFT2)
            dve.wait_ge(S["g_post2_in"], 16)
            mod_row(GATE2, gg2, g_post)
            att_soft(3)
            att_out(2)
            mlstm_out(2)
            mlstm_weights(3)
            att_out(3)
            mlstm_out(3)
            bk.wait_released(dve, "mv2", 3, 1)
            heads = wide.rearrange("p t (h v) -> p t h v", h=MH)
            sq = junk.rearrange("p (t h v) -> p t h v", t=NT, h=MH)
            step(v.tensor_tensor(sq, heads, heads, ALU.mult))
            step(v.tensor_reduce(stat[:, 0, :].rearrange("p (t h) -> p t h", t=NT), sq, AX, ALU.add))
            mean_to_rstd(MV, 16)
            step(v.tensor_tensor(heads, heads, stat[:, 1, :].rearrange("p (t h) -> p t h", t=NT).unsqueeze(3)
                                 .broadcast_to([P, NT, MH, MV]), ALU.mult))
            step(v.tensor_tensor(wide, wide, m_norm[:].unsqueeze(1).broadcast_to([P, NT, MH * MV]), ALU.mult))
            for t in range(NT):
                bk.wait_released(dve, "mo", t)
            v.tensor_tensor(wide, wide, o_gate[:], ALU.mult).then_inc(S["mh_done"], 1)
            dve.wait_ge(S["mix_sq"], 2 * NT)
            step(v.tensor_reduce(stat[:, 0, 8:12], stat[:, 0, 0:8].rearrange("p (t h) -> p t h", t=NT), AX, ALU.add))
            step(v.tensor_copy(stat[:, 0, 0:4], stat[:, 0, 8:12]))
            mean_to_rstd(D, NT)
            for h in range(2):
                at = slice(h * 512, h * 512 + 512)
                for t in range(NT):
                    ins = v.scalar_tensor_tensor(out=both[:, t, at], in0=bk("out", h, t), scalar=stat[:, 1, t:t + 1],
                                                 in1=gg1[:, at], op0=ALU.mult, op1=ALU.mult)
                    bk.release(ins, "out", h, t)
                    bk.wait_released(dve, "out", h, t)
                    step(v.tensor_tensor(x_sb[:, t, at], x_sb[:, t, at], both[:, t, at], ALU.add))
            for t in range(NT):
                step(v.tensor_tensor_reduce(out=both[:, t, :], in0=x_sb[:, t, :], in1=x_sb[:, t, :], scale=1.0, scalar=0.0,
                                            op0=ALU.mult, op1=ALU.add, accum_out=stat[:, 0, t:t + 1]))
            mean_to_rstd(D, NT)
            for t in range(NT):
                v.tensor_scalar(both[:, t, :], x_sb[:, t, :], stat[:, 1, t:t + 1], None, ALU.mult).then_inc(S["xn2_ready"], 1)
            for c in range(1, DC, 2):
                bk.wait_full(dve, "h2T", c)
                ins = v.tensor_scalar(hT[:, c, :], bk("h2T", c), cols[:, SCALE2 * 8 + c:SCALE2 * 8 + c + 1],
                                      cols[:, SHIFT2 * 8 + c:SHIFT2 * 8 + c + 1], ALU.mult, ALU.add)
                bk.release(ins, "h2T", c)


RECTS = [(0, 1, 16), (1, 1, 8), (2, 1, 5), (3, 1, 4), (4, 1, 3), (5, 3, 2), (8, 8, 1)]


def query_block(nc, A, keep, s_all):
    hT, ident, hH, hL, h_rows = keep["hT"], keep["ident"], keep["hH"], keep["hL"], keep["h_rows"]
    with ExitStack() as ctx:
        def sb(name, shape, dt=F32):
            return ctx.enter_context(nc.sbuf_tensor(name, shape, dt))

        def sem(name):
            return ctx.enter_context(nc.semaphore(name))

        M = 2 * PH
        order = [("h", i) for i in range(2)] + [("keys", i) for i in range(4)] + [("q", 0)]
        for m in range(M):
            order += ([("q", m + 1)] if m + 1 < M else []) + [("s", m)]
        psum = ctx.enter_context(nc.psum_tensor("query_psum", [P, 8, 512], F32))
        keys = sb("keys", [P, M, P])
        keysT = sb("keysT", [P, M, P])
        wq = sb("wq", [P, 2, DC, 2 * P])
        wqH = sb("wqH", [P, 2, DC, 2 * P], F32R)
        wqL = sb("wqL", [P, 2, DC, 2 * P], F32R)
        qT = sb("peer_qT", [P, 2, T])
        bank_full = [sem(f"q_bank_full{i}") for i in range(8)]
        bank_free = [sem(f"q_bank_free{i}") for i in range(8)]
        bk = Banks(psum, order, bank_full, bank_free)
        wq_in = [sem(f"wq_in{i}") for i in range(2)]
        keys_in, h_hi, h_lo, wq_hi, wq_lo = (sem(n) for n in ("keys_in", "h_hi", "h_lo", "wq_hi", "wq_lo"))
        block = ctx.enter_context(nc.Block())

        @block.sync
        def _(sp):
            for half, name in enumerate(("peer_keys1", "peer_keys2")):
                sp.dma_start(keys[:].rearrange("p (h two) d -> p h two d", two=2)[:, :, half, :],
                             A[name][0].rearrange("h k d -> k h d")).then_inc(keys_in, 16)
            for s in range(M // 2):
                if s >= 2:
                    sp.wait_ge(wq_lo, s - 1)
                sp.dma_start(wq[:, s % 2, :, :], A["peer_wq"][0, :, s * 2 * P:(s + 1) * 2 * P]
                             .rearrange("(c p) n -> p c n", p=P)).then_inc(wq_in[s % 2], 16)

        @block.scalar
        def _(act):
            func = nc.scalar.activation
            func(hH[:], hT[:], ACT.Copy).then_inc(h_hi, 1)

            def high(s):
                act.wait_ge(wq_in[s % 2], 16 * (s // 2 + 1))
                if s >= 2:
                    bk.wait_full(act, "q", 2 * s - 3)
                func(wqH[:, s % 2, :, :], wq[:, s % 2, :, :], ACT.Copy).then_inc(wq_hi, 1)

            high(0)
            for i in range(2):
                bk.wait_full(act, "h", i)
                bk.release(func(h_rows[:, i * 512:(i + 1) * 512], bk("h", i), ACT.Copy), "h", i)
            for i in range(4):
                bk.wait_full(act, "keys", i)
                ins = func(keysT[:, 4 * i:4 * i + 4, :], bk("keys", i).rearrange("p (m k) -> p m k", m=4), ACT.Copy)
                bk.release(ins, "keys", i)
            high(1)
            for m in range(M):
                bk.wait_full(act, "q", m)
                if m >= 2:
                    bk.wait_full(act, "s", m - 2)
                bk.release(func(qT[:, m % 2, :], bk("q", m), ACT.Copy), "q", m)
                if m % 2 and m // 2 + 2 < M // 2:
                    high(m // 2 + 2)

        @block.vector
        def _(dve):
            v = nc.vector
            dve.wait_ge(h_hi, 1)
            v.tensor_tensor(hL[:], hT[:], hH[:].bitcast(F32), ALU.subtract).then_inc(h_lo, 1)

            def low(s):
                dve.wait_ge(wq_hi, s + 1)
                v.tensor_tensor(wqL[:, s % 2, :, :], wq[:, s % 2, :, :], wqH[:, s % 2, :, :].bitcast(F32),
                                ALU.subtract).then_inc(wq_lo, 1)

            low(0)
            low(1)
            for m in range(M):
                if m % 2 == 0 and m and m // 2 + 1 < M // 2:
                    low(m // 2 + 1)
                bk.wait_full(dve, "s", m)
                ins = v.tensor_copy(s_all[:, m, :, :], bk("s", m).rearrange("p (t k) -> p t k", t=NT))
                bk.release(ins, "s", m)

        @block.tensor
        def _(pe):
            mm, tr = nc.tensor.matmul, nc.tensor.transpose
            for i in range(2):
                for k in range(4):
                    last = tr(bk("h", i)[:, k * P:(k + 1) * P], hT[:, 4 * i + k, 0:P], ident[:])
                bk.done(last, "h", i)
            pe.wait_ge(keys_in, 32)
            for i in range(4):
                for k in range(4):
                    last = tr(bk("keys", i)[:, k * P:(k + 1) * P], keys[:, 4 * i + k, :], ident[:])
                bk.done(last, "keys", i)
            pe.wait_ge(h_lo, 1)

            def query(m):
                s = m // 2
                pe.wait_ge(wq_lo, s + 1)
                bk.wait_free(pe, "q", m)
                n = 0
                for c in range(DC):
                    at = slice((m % 2) * P, (m % 2) * P + P)
                    for w, h in ((wqH, hH), (wqH, hL), (wqL, hH)):
                        last = mm(bk("q", m), w[:, s % 2, c, at], h[:, c, :], start=(n == 0), stop=(n == 3 * DC - 1))
                        n += 1
                bk.done(last, "q", m)

            query(0)
            for m in range(M):
                if m + 1 < M:
                    query(m + 1)
                bk.wait_released(pe, "q", m)
                bk.wait_released(pe, "keys", m // 4)
                bk.wait_free(pe, "s", m)
                for t in range(NT):
                    last = mm(bk("s", m)[:, t * P:(t + 1) * P], qT[:, m % 2, t * P:(t + 1) * P], keysT[:, m, :],
                              start=True, stop=True)
                bk.done(last, "s", m)


def expert_block(nc, A, keep, s_all, S_dram, G_dram):
    ident, hH, hL, h_rows, eidx, coef = (keep[n] for n in ("ident", "hH", "hL", "h_rows", "eidx", "coef"))
    with ExitStack() as ctx:
        def sb(name, shape, dt=F32):
            return ctx.enter_context(nc.sbuf_tensor(name, shape, dt))

        def sem(name):
            return ctx.enter_context(nc.semaphore(name))

        M = 2 * PH
        u_rows = keep["hT"].rearrange("p (q a) t -> p q (a t)", q=RING)
        row_no = sb("row_no", [P, RING], U32)
        dot4 = sb("dot4", [P, RING])
        dots = sb("dots", [P, K])
        val = sb("val", [P, 2, M, PTOP])
        idx = sb("idx", [P, M, PTOP], U32)
        idxf = sb("idxf", [P, M, PTOP])
        work = sb("work", [P, 4, P])
        cv = sb("cv", [P, PH, NCAND])
        ci = sb("ci", [P, PH, NCAND])
        top = sb("top", [P, NT, PH, PTOP])
        pos = sb("top_pos", [P, PH, PTOP], U32)
        posf = sb("top_posf", [P, PH, PTOP])
        hit = sb("hit", [P, 2, PTOP, NCAND])
        chosen = sb("chosen", [P, PH, PTOP])
        chosen_u = sb("chosen_u", [P, 2, K], U32)
        tsum = sb("tsum", [P, 2, NT, PH])
        sel = sb("sel", [P, NTD, 2, K])
        selT = sb("selT", [P, 3, TD])
        iota_i = sb("iota_i", [P, P], I32)
        iota = sb("iota", [P, P])
        onehot = sb("onehot", [P, 2, GT, 2, P])
        stage = s_all[:].rearrange("p m t k -> p (m t k)")[:, 0:2 * NBLK * TB].rearrange("p (a i t) -> p a i t", a=2, t=TB)
        ub = sb("ub", [P, RING, D])
        uF = sb("uF", [P, 2, D])
        uH = sb("uH", [P, 2, D], F32R)
        uL = sb("uL", [P, 2, D], F32R)
        act_out = sb("act_out", [P, 2, TD])
        uT_ps = ctx.enter_context(nc.psum_tensor("uT_ps", [P, 2, D], F32))
        S_ps = ctx.enter_context(nc.psum_tensor("S_ps", [P, 2, T], F32))
        G_ps = ctx.enter_context(nc.psum_tensor("G_ps", [P, 2, 4, P], F32))

        u_in = [sem(f"u_in{i}") for i in range(RING)]
        rows_in = [sem(f"u_rows_in{i}") for i in range(RING)]
        s_stored = [sem(f"s_stored{i}") for i in range(2)]
        g_stored = [sem(f"g_stored{i}") for i in range(2)]
        (u_turned, u_high, u_copied, u_low, u_done, s_ready, dve_chain, iota_ready, iota_done, top_ready, gate_exp, sel_ready, selT_full,
         selT_done, hot_ready, g_full, g_staged, eidx_ready, dot_done, dots_gelu, row_no_ready, dots_copied) = (sem(n) for n in (
            "u_turned", "u_high", "u_copied", "u_low", "u_done", "s_ready", "x_dve_chain", "iota_ready", "iota_done", "top_ready", "gate_exp",
            "sel_ready", "selT_full", "selT_done", "hot_ready", "g_full", "g_staged",
            "eidx_ready", "dot_done", "dots_gelu", "row_no_ready", "dots_copied"))
        block = ctx.enter_context(nc.Block())

        def blocks(eng, body):
            n0 = LEAD - LEAD_ROWS
            with eng.Fori(0, n0 // 4) as i:
                for r in range(4):
                    body(4 * i + r, i, r, None, [])
            with eng.Fori(0, LEAD_ROWS // 4) as i:
                for r in range(4):
                    body(n0 + 4 * i + r, n0 // 4 + i, r, None, [(4 * i + r, r, i)])
            yield
            with eng.Fori(0, GSTEPS // 4) as i:
                for r in range(4):
                    body(LEAD + 4 * i + r, LEAD // 4 + i, r, (i, r), [(LEAD_ROWS + 4 * i + r, r, LEAD_ROWS // 4 + i)])
            n0, k0 = NBLK - TAIL, LEAD_ROWS + GSTEPS

            def tail(i):
                for r in range(4):
                    body(n0 + 4 * i + r, n0 // 4 + i, r, None,
                         [(k0 + 8 * i + 2 * r + e, (2 * r + e) % 4, k0 // 4 + 2 * i + (2 * r + e) // 4) for e in range(2)])

            with eng.Fori(0, TAIL // 4 - 1) as i:
                tail(i)
            tail(TAIL // 4 - 1)

        @block.sync
        def _(sp):
            for b in range(2):
                sp.sem_inc(s_stored[b], 16)
                sp.sem_inc(g_stored[b], 16)

            def load(n, r):
                sp.dma_start(ub[:, r, :], A["peer_u"][0, bass.ds(n * P, P), :]).then_inc(u_in[r], 16)

            for r in range(RING):
                load(r, r)

            def body(n, four, r, g, d):
                b = r % 2
                if not (isinstance(n, int) and n >= NBLK - RING):
                    sp.wait_ge(u_turned, n + 3)
                    load(n + RING, r)
                sp.wait_ge(s_ready, n + 3)
                sp.dma_start(S_dram[bass.ds(n, 1), :, :].rearrange("a p t -> p (a t)"), act_out[:, b, :]).then_inc(s_stored[b], 16)
                if g is not None and g[1] % 2:
                    i, k = g
                    sp.wait_ge(g_staged, 4 * i + k + 2)
                    sp.dma_start(G_dram[:, :, bass.ds(2 * i + k // 2, 1), :].rearrange("g p a n -> p g (a n)"),
                                 stage[:, k // 2, :, :].rearrange("p (g i) t -> p g (i t)", g=NBG)).then_inc(g_stored[k // 2], 16)

            for _ in blocks(sp, body):
                pass
            for b in range(2):
                sp.wait_ge(s_stored[b], 16 * (NBLK // 2 + 1))
                sp.wait_ge(g_stored[b], 16 * (NTB // 2 + 1))

        @block.gpsimd
        def _(pool):
            pool.sem_inc(u_low, 2)
            nc.gpsimd.iota(iota_i[:], pattern=[[1, P]], base=0, channel_multiplier=0).then_inc(iota_ready, 1)

            def body(n, four, r, g, d):
                b = r % 2
                if d:
                    pool.wait_ge(eidx_ready, 1)
                for k, q, turn in d:
                    pool.wait_ge(dot_done, k + 1)
                    nc.gpsimd.tensor_copy(row_no[:, q:q + 1], eidx[:, bass.ds(k, 1)]).then_inc(row_no_ready, 1)
                if d:
                    pool.wait_ge(row_no_ready, d[-1][0] + 1)
                pool.wait_ge(u_copied, n + 3)
                pool.wait_ge(u_done, n + 1)
                nc.gpsimd.tensor_tensor(uL[:, b, :], uF[:, b, :], uH[:, b, :].bitcast(F32), ALU.subtract).then_inc(u_low, 1)
                for k, q, turn in d:
                    pool.indirect_dma_start(u_rows[:, q, :], None, A["peer_u"][0],
                                            bass.IndirectOffsetOnAxis(row_no[:, q:q + 1], 0)).then_inc(rows_in[q], 16)

            for _ in blocks(pool, body):
                pass

        @block.scalar
        def _(act):
            func = nc.scalar.activation
            act.sem_inc(u_copied, 2)
            act.sem_inc(u_high, 2)
            act.sem_inc(s_ready, 2)

            def copy(n, b):
                act.wait_ge(u_turned, n + 3)
                act.wait_ge(u_done, n + 1)
                func(uH[:, b, :], uT_ps[:, b, :], ACT.Copy).then_inc(u_high, 1)
                act.wait_ge(u_low, n + 1)
                func(uF[:, b, :], uT_ps[:, b, :], ACT.Copy).then_inc(u_copied, 1)

            def body(n, four, r, g, d):
                b = r % 2
                if not (isinstance(n, int) and n == NBLK - 1):
                    copy(n + 1, 1 - b)
                act.wait_ge(u_done, n + 3)
                act.wait_ge(s_stored[b], 32 * four + 16 * (r // 2) + 16)
                func(act_out[:, b, :], S_ps[:, b, 0:TD], ACT.Gelu).then_inc(s_ready, 1)

            copy(0, 0)
            for _ in blocks(act, body):
                act.wait_ge(top_ready, 1)
                func(top[:], top[:], ACT.Exp).then_inc(gate_exp, 1)
            act.wait_ge(dots_copied, K // RING)
            func(coef[:], dots[:], ACT.Gelu).then_inc(dots_gelu, 1)

        @block.tensor
        def _(pe):
            mm, tr = nc.tensor.matmul, nc.tensor.transpose
            pe.sem_inc(u_turned, 2)
            pe.sem_inc(u_done, 2)
            pe.sem_inc(g_full, 2)

            def turn(n, four, r):
                b = r % 2
                pe.wait_ge(u_in[r], 16 * four + 16)
                pe.wait_ge(u_copied, n + 1)
                for c in range(DC):
                    last = tr(uT_ps[:, b, c * P:(c + 1) * P], ub[:, r, c * P:(c + 1) * P], ident[:])
                last.then_inc(u_turned, 1)

            def body(n, four, r, g, d):
                b = r % 2
                if not (isinstance(n, int) and n == NBLK - 1):
                    turn(n + 1, four + (r + 1) // 4, (r + 1) % 4)
                pe.wait_ge(u_high, n + 3)
                pe.wait_ge(s_ready, n + 1)
                for c in range(DC):
                    for h in (hH, hL):
                        mm(S_ps[:, b, 0:TD], uH[:, b, c * P:(c + 1) * P], h[:, c, P:T], start=(c == 0 and h is hH), stop=False)
                pe.wait_ge(u_low, n + 3)
                for c in range(DC):
                    last = mm(S_ps[:, b, 0:TD], uL[:, b, c * P:(c + 1) * P], hH[:, c, P:T], start=False, stop=(c == DC - 1))
                last.then_inc(u_done, 1)
                if g is not None:
                    m = 4 * g[0] + g[1]
                    pe.wait_ge(hot_ready, m + 1)
                    pe.wait_ge(g_staged, m + 1)
                    for k in range(GT):
                        last = mm(G_ps[:, k // 3, k % 3, :], onehot[:, b, k, 1, :], onehot[:, b, k, 0, :], start=True, stop=True)
                    last.then_inc(g_full, 1)

            turn(0, 0, 0)
            for _ in blocks(pe, body):
                pe.wait_ge(sel_ready, 1)
                for i in range(3):
                    if i == 2:
                        pe.wait_ge(selT_done, 1)
                    for t in range(NTD):
                        src = sel[:, t, i, :] if i < 2 else top[:, t + 1, :, :].rearrange("p h k -> p (h k)")
                        last = tr(G_ps[:, i % 2, t, :], src, ident[:])
                    last.then_inc(selT_full, 1)

        @block.vector
        def _(dve):
            v = nc.vector
            step = Chain(dve, dve_chain)
            dve.sem_inc(g_staged, 1)
            dve.sem_inc(dot_done, RING)
            dve.wait_ge(iota_ready, 1)
            step(v.tensor_copy(iota[:], iota_i[:]))

            def largest(rows):
                for values, indices, src, spare in rows:
                    step.put(v.max(values[:, 0:8], src))
                step.wait()
                for values, indices, src, spare in rows:
                    step.put(v.match_replace(spare, values[:, 0:8], src, -3.0e38))
                for values, indices, src, spare in rows:
                    step.put(v.max_index(indices[:, 0:8], values[:, 0:8], src))
                step.wait()
                for values, indices, src, spare in rows:
                    step.put(v.max(values[:, 8:16], spare))
                step.wait()
                for values, indices, src, spare in rows:
                    step.put(v.max_index(indices[:, 8:16], values[:, 8:16], spare))
                step.wait()

            def dot(k, q, turn):
                dve.wait_ge(rows_in[q], 16 * turn + 16)
                v.tensor_tensor_reduce(out=u_rows[:, q, :], in0=u_rows[:, q, :], in1=h_rows[:], scale=1.0, scalar=0.0,
                                       op0=ALU.mult, op1=ALU.add, accum_out=dot4[:, q:q + 1]).then_inc(dot_done, 1)
                if q == RING - 1:
                    dve.wait_ge(dot_done, k + 1 + RING)
                    v.tensor_copy(dots[:, bass.ds(RING * turn, RING)], dot4[:]).then_inc(dots_copied, 1)
                    dve.wait_ge(dots_copied, turn + 1)

            dots_made = 0

            def dots_beside(n):
                nonlocal dots_made
                for k in range(dots_made, dots_made + n):
                    dot(k, k % RING, k // RING)
                dots_made += n

            for t in range(NT):
                for m in range(0, M, 4):
                    largest([(val[:, t % 2, m + i, :], idx[:, m + i, :], s_all[:, m + i, t, :], work[:, i, :]) for i in range(4)])
                    dots_beside(2 if t else 0)
                step(v.tensor_copy(idxf[:], idx[:]))
                halves = lambda x, i: x.rearrange("p (h two) k -> p h two k", two=2)[:, :, i, :]
                v1, v2, i1, i2 = halves(val[:, t % 2, :, :], 0), halves(val[:, t % 2, :, :], 1), halves(idxf[:], 0), halves(idxf[:], 1)
                step(v.tensor_scalar(i1, i1, float(PK), None, ALU.mult))
                at = 0
                for a, na, nb in RECTS:
                    for dst, x, y in ((cv, v1, v2), (ci, i1, i2)):
                        step.put(v.tensor_tensor(dst[:, :, at:at + na * nb].rearrange("p h (a b) -> p h a b", a=na),
                                             x[:, :, a:a + na].unsqueeze(3).broadcast_to([P, PH, na, nb]),
                                             y[:, :, 0:nb].unsqueeze(2).broadcast_to([P, PH, na, nb]), ALU.add))
                    at += na * nb
                step.wait()
                for h in range(0, PH, 4):
                    largest([(top[:, t, h + i, :], pos[:, h + i, :], cv[:, h + i, :], work[:, i, 0:NCAND]) for i in range(4)])
                    dots_beside(2 if t else 0)
                step(v.tensor_copy(posf[:], pos[:]))
                for h in range(0, PH, 2):
                    place = posf[:, h:h + 2, :].unsqueeze(3).broadcast_to([P, 2, PTOP, NCAND])
                    step(v.tensor_tensor(hit[:], iota[:, 0:NCAND].unsqueeze(1).unsqueeze(1).broadcast_to([P, 2, PTOP, NCAND]),
                                         place, ALU.is_equal))
                    step(v.tensor_tensor(hit[:], hit[:], ci[:, h:h + 2, :].unsqueeze(2).broadcast_to([P, 2, PTOP, NCAND]), ALU.mult))
                    step(v.tensor_reduce(chosen[:, h:h + 2, :], hit[:], AX, ALU.add))
                dots_beside(1 if t else 0)
                if t == 0:
                    v.tensor_copy(eidx[:], chosen[:].rearrange("p h k -> p (h k)")).then_inc(eidx_ready, 1)
                    dve.wait_ge(eidx_ready, 1)
                    continue
                step(v.tensor_copy(chosen_u[:, 0, :], chosen[:].rearrange("p h k -> p (h k)")))
                step(v.tensor_scalar(chosen_u[:, 1, :], chosen_u[:, 0, :], 7, None, ALU.logical_shift_right))
                step(v.tensor_copy(sel[:, t - 1, 0, :], chosen_u[:, 1, :]))
                step(v.tensor_scalar(chosen_u[:, 1, :], chosen_u[:, 0, :], PK - 1, None, ALU.bitwise_and))
                step(v.tensor_copy(sel[:, t - 1, 1, :], chosen_u[:, 1, :]))
            dots_beside(LEAD_ROWS - dots_made)
            step(v.tensor_copy(tsum[:, 0, :, :], top[:, :, :, 0]))
            flat = top[:].rearrange("p t h k -> p (t h) k")
            sums = lambda i: tsum[:, i, :, :].rearrange("p t h -> p (t h)")
            over = lambda x: x.unsqueeze(2).broadcast_to([P, NT * PH, PTOP])
            v.tensor_tensor(flat, flat, over(sums(0)), ALU.subtract).then_inc(top_ready, 1)
            dve.wait_ge(gate_exp, 1)
            step(v.tensor_reduce(sums(0), flat, AX, ALU.add))
            step(v.reciprocal(sums(1), sums(0)))
            v.tensor_tensor(flat, flat, over(sums(1)), ALU.mult).then_inc(sel_ready, 1)
            for i in range(3):
                dve.wait_ge(selT_full, i + 1)
                v.tensor_copy(selT[:, i, :], G_ps[:, i % 2, 0:NTD, :].rearrange("p t k -> p (t k)")).then_inc(selT_done, 1)
            dve.wait_ge(selT_done, 3)

            def one_hot(m, b):
                dve.wait_ge(g_full, m + 1)
                for k in range(GT):
                    col = lambda j: selT[:, j, bass.ds(GT * m + k, 1)]
                    v.tensor_scalar(onehot[:, b, k, 1, :], iota[:], col(1), None, ALU.is_equal)
                    ins = v.tensor_scalar(onehot[:, b, k, 0, :], iota[:], col(0), col(2), ALU.is_equal, ALU.mult)
                ins.then_inc(hot_ready, 1)

            def four_steps(i, final):
                for b in range(4):
                    m = 4 * i + b
                    if not (final and b == 3):
                        one_hot(m + 1, (b + 1) % 2)
                    if b % 2 == 0:
                        dve.wait_ge(g_stored[b // 2], 16 * i + 16)
                    dve.wait_ge(g_full, m + 3)
                    for q in range(2):
                        t0 = (b % 2) * GT + q * 3
                        ins = v.tensor_copy(stage[:, b // 2, :, t0:t0 + 3].rearrange("p i t -> p t i"), G_ps[:, q, 0:3, :])
                    ins.then_inc(g_staged, 1)
                    dot(LEAD_ROWS + m, b, LEAD_ROWS // 4 + i)

            one_hot(0, 0)
            with dve.Fori(0, GSTEPS // 4 - 1) as i:
                four_steps(i, False)
            four_steps(GSTEPS // 4 - 1, True)
            with dve.Fori(0, 2 * TAIL // RING) as i:
                for q in range(RING):
                    dot(LEAD_ROWS + GSTEPS + RING * i + q, q, (LEAD_ROWS + GSTEPS) // RING + i)
            dve.wait_ge(dots_gelu, 1)
            v.tensor_tensor(coef[:], coef[:], top[:, 0, :, :].rearrange("p h k -> p (h k)"), ALU.mult)


def value_block(nc, A, keep, S_dram, G_dram, out):
    x_sb, gg2, eidx, coef = keep["x"], keep["gg2"], keep["eidx"], keep["coef"]
    with ExitStack() as ctx:
        def sb(name, shape, dt=F32):
            return ctx.enter_context(nc.sbuf_tensor(name, shape, dt))

        def sem(name):
            return ctx.enter_context(nc.semaphore(name))

        y_ps = ctx.enter_context(nc.psum_tensor("y_ps", [P, NTD, 2, 512], F32))
        vb = sb("vb", [P, RING, D])
        vH = sb("vH", [P, RING, D], F32R)
        vL = sb("vL", [P, RING, D], F32R)
        sbuf = sb("s_in", [P, RING, TD])
        gbuf = sb("g_in", [P, 2, NTB, BG, TB])
        a = sb("a", [P, RING, TD])
        aH = sb("aH", [P, RING, TD], F32R)
        aL = sb("aL", [P, RING, TD], F32R)
        nothing = sb("nothing", [P, 512], F32R)
        y = sb("y", [P, NT, D])
        v_rows = keep["hT"].rearrange("p (q a) t -> p q (a t)", q=RING)
        row_no = sb("v_row_no", [P, RING], U32)
        y0 = sb("y0", [P, 2, D])
        sq = sb("sq", [P, 512])
        stat = sb("y_stat", [P, 5, 8])
        v_in = [sem(f"v_in{i}") for i in range(RING)]
        s_in = [sem(f"s_in_done{i}") for i in range(RING)]
        g_in = [sem(f"g_in_done{i}") for i in range(2)]
        out_done = [sem(f"out_done{i}") for i in range(NT)]
        rows_in = [sem(f"v_rows_in{i}") for i in range(RING)]
        row_no_ready, row_done, y0_clear, y0_done = sem("v_row_no_ready"), sem("row_done"), sem("y0_clear"), sem("y0_done")
        nothing_ready, v_hi, v_lo, a_ready, a_hi, a_lo, v_done, y_done, y_sq, chain, out_ready = (
            sem(n) for n in ("nothing_ready", "v_hi", "v_lo", "a_ready", "a_hi", "a_lo", "v_done", "y_done", "y_sq",
                             "y_dve_chain", "out_ready"))
        GP = BG // 4
        block = ctx.enter_context(nc.Block())

        def blocks(eng, body):
            with eng.Fori(0, NBG // 2) as i:
                for gb in range(2):
                    with eng.Fori(0, BG // 4) as j:
                        for q in range(4):
                            body(i * (2 * BG) + gb * BG + 4 * j + q, q, i * (BG // 2) + gb * (BG // 4) + j,
                                 i, gb, 4 * j + q)

        def y_of(t, h):
            return y0[:, 0, h * 512:(h + 1) * 512] if t == 0 else y_ps[:, t - 1, h, :]

        @block.sync
        def _(sp):
            def body(n, q, turn, i, gb, k):
                sp.wait_ge(v_lo, n + 1)
                sp.dma_start(vb[:, q, :], A["peer_v"][0, bass.ds(n * P, P), :]).then_inc(v_in[q], 16)
                sp.wait_ge(a_ready, n + 1)
                sp.dma_start(sbuf[:, q, :], S_dram[bass.ds(n, 1), :, :].rearrange("a p t -> p (a t)")).then_inc(s_in[q], 16)

            blocks(sp, body)
            for t in range(NT):
                sp.wait_ge(out_ready, t + 1)
                sp.dma_start(out[0, t * P:(t + 1) * P, :], y[:, t, :]).then_inc(out_done[t], 16)
            for t in range(NT):
                sp.wait_ge(out_done[t], 16)

        @block.gpsimd
        def _(pool):
            nc.gpsimd.memset(nothing[:].bitcast(F32), 0.0).then_inc(nothing_ready, 1)
            nc.gpsimd.memset(y0[:], 0.0).then_inc(y0_clear, 1)
            pool.sem_inc(v_lo, RING)
            pool.dma_start(gbuf[:, 0, :, :, :].rearrange("p q b t -> p (q b t)"),
                           G_dram[0].rearrange("p q n -> p (q n)")).then_inc(g_in[0], 16 * GP)

            def gather(q, at):
                pool.indirect_dma_start(v_rows[:, q, :], None, A["peer_v"][0],
                                        bass.IndirectOffsetOnAxis(at, 0)).then_inc(rows_in[q], 16)

            for q in range(2):
                gather(q, eidx[:, q:q + 1])

            def body(n, q, last):
                q2 = (q + 2) % 4
                if not last:
                    pool.wait_ge(row_done, n + 3)
                    nc.gpsimd.tensor_copy(row_no[:, q2:q2 + 1], eidx[:, bass.ds(n + 2, 1)]).then_inc(row_no_ready, 1)
                    pool.wait_ge(row_no_ready, n + 1)
                pool.wait_ge(v_done, n + 1)
                pool.wait_ge(v_hi, n + 1)
                nc.gpsimd.tensor_tensor(vL[:, q, :], vb[:, q, :], vH[:, q, :].bitcast(F32), ALU.subtract).then_inc(v_lo, 1)
                if not last:
                    gather(q2, row_no[:, q2:q2 + 1])

            def group(i, gb, more):
                with pool.Fori(0, GP if more else GP - 1) as j:
                    for q in range(4):
                        body(i * (2 * BG) + gb * BG + 4 * j + q, q, False)
                        if q == 0 and more:
                            pool.wait_ge(a_ready, i * (2 * BG) + gb * BG + RING)
                            pool.dma_start(gbuf[:, 1 - gb, bass.ds(j * (NTB // GP), NTB // GP), :, :].rearrange("p q b t -> p (q b t)"),
                                           G_dram[bass.ds(2 * i + gb + 1, 1), :, bass.ds(j * (NTB // GP), NTB // GP), :]
                                           .rearrange("a p q n -> p (a q n)")).then_inc(g_in[1 - gb], 16)

            with pool.Fori(0, NBG // 2 - 1) as i:
                for gb in range(2):
                    group(i, gb, True)
            group(NBG // 2 - 1, 0, True)
            group(NBG // 2 - 1, 1, False)
            for q in range(4):
                body(NBLK - 4 + q, q, q >= 2)

        @block.scalar
        def _(act):
            func = nc.scalar.activation
            act.sem_inc(a_hi, RING)

            def body(n, q, turn, i, gb, k):
                act.wait_ge(v_in[q], 16 * turn + 16)
                act.wait_ge(v_done, n + 1)
                func(vH[:, q, :], vb[:, q, :], ACT.Copy).then_inc(v_hi, 1)
                act.wait_ge(a_ready, n + 1 + RING)
                func(aH[:, q, :], a[:, q, :], ACT.Copy).then_inc(a_hi, 1)

            blocks(act, body)
            act.wait_ge(y0_done, 1)
            for t in range(NT):
                if t == 1:
                    act.wait_ge(y_done, 1)
                for h in range(2):
                    func(sq[:], y_of(t, h), ACT.Square, accum_out=stat[:, 0, 2 * t + h:2 * t + h + 1]).then_inc(y_sq, 1)
                    act.wait_ge(y_sq, 2 * t + h + 1)

        @block.vector
        def _(dve):
            v = nc.vector
            step = Chain(dve, chain)
            dve.sem_inc(row_done, RING)
            dve.sem_inc(a_ready, RING)
            dve.sem_inc(a_lo, RING)

            def body(n, q, turn, i, gb, k):
                dve.wait_ge(s_in[q], 16 * turn + 16)
                dve.wait_ge(g_in[gb], 16 * GP * (i + 1))
                dve.wait_ge(a_hi, n + 1)
                v.tensor_tensor(a[:, q, :].rearrange("p (q t) -> p q t", t=TB),
                                sbuf[:, q, :].rearrange("p (q t) -> p q t", t=TB),
                                gbuf[:, gb, :, bass.ds(k, 1), :].rearrange("p q a t -> p q (a t)"),
                                ALU.mult).then_inc(a_ready, 1)
                dve.wait_ge(a_hi, n + 1 + RING)
                v.tensor_tensor(aL[:, q, :], a[:, q, :], aH[:, q, :].bitcast(F32), ALU.subtract).then_inc(a_lo, 1)
                dve.wait_ge(rows_in[q], 16 * turn + 16)
                dve.wait_ge(row_done, n + 3)
                v.scalar_tensor_tensor(out=y0[:, q % 2, :], in0=v_rows[:, q, :], scalar=coef[:, bass.ds(n, 1)], in1=y0[:, q % 2, :],
                                       op0=ALU.mult, op1=ALU.add).then_inc(row_done, 1)

            dve.wait_ge(y0_clear, 1)
            blocks(dve, body)
            dve.wait_ge(row_done, K + RING)
            v.tensor_tensor(y0[:, 0, :], y0[:, 0, :], y0[:, 1, :], ALU.add).then_inc(y0_done, 1)
            dve.wait_ge(y_sq, 2 * NT)
            step(v.tensor_reduce(stat[:, 1, 0:NT], stat[:, 0, :].rearrange("p (t h) -> p t h", t=NT), AX, ALU.add))
            step(v.tensor_scalar(stat[:, 2, 0:NT], stat[:, 1, 0:NT], 1.0 / D, EPS, ALU.mult, ALU.add))
            rsqrt(nc, step, stat[:, 1, 0:NT], stat[:, 2, 0:NT], stat[:, 3, 0:NT], stat[:, 4, 0:NT])
            for t in range(NT):
                for h in range(2):
                    step(v.scalar_tensor_tensor(out=y[:, t, h * 512:(h + 1) * 512], in0=y_of(t, h),
                                                scalar=stat[:, 1, t:t + 1], in1=gg2[:, h * 512:(h + 1) * 512],
                                                op0=ALU.mult, op1=ALU.mult))
                v.tensor_tensor(y[:, t, :], y[:, t, :], x_sb[:, t, :], ALU.add).then_inc(out_ready, 1)

        @block.tensor
        def _(pe):
            mm = nc.tensor.matmul
            pe.sem_inc(v_done, RING)
            pe.wait_ge(nothing_ready, 1)
            for t in range(NTD):
                for h in range(2):
                    mm(y_ps[:, t, h, :], nothing[:, 0:P], nothing[:], start=True, stop=False)

            def body(n, q, turn, i, gb, k):
                pe.wait_ge(a_lo, n + 1 + RING)
                pe.wait_ge(v_lo, n + 1 + RING)
                for t in range(NTD):
                    for x, w in ((aH, vH), (aH, vL), (aL, vH)):
                        for h in range(2):
                            last = mm(y_ps[:, t, h, :], x[:, q, t * P:(t + 1) * P], w[:, q, h * 512:(h + 1) * 512],
                                      start=False, stop=False)
                last.then_inc(v_done, 1)

            blocks(pe, body)
            for t in range(NTD):
                for h in range(2):
                    last = mm(y_ps[:, t, h, :], nothing[:, 0:P], nothing[:], start=False, stop=True)
            last.then_inc(y_done, 1)


def build(nc, A, out):
    with ExitStack() as ctx:
        def sb(name, shape, dt=F32):
            return ctx.enter_context(nc.sbuf_tensor(name, shape, dt))

        keep = dict(x=sb("x_sb", [P, NT, D]), hT=sb("hT", [P, DC, T]), ident=sb("ident", [P, P]),
                    cols=sb("cols", [P, 88]), gg2=sb("gg2", [P, D]))
        keep["eidx"] = sb("eidx", [P, K], U32)
        keep["coef"] = sb("coef", [P, K])
        S_dram = nc.dram_tensor("gelu_table", (NBLK, P, TD), F32, kind="Internal").ap()
        G_dram = nc.dram_tensor("gate_table", (NBG, P, NTB, BG * TB), F32, kind="Internal").ap()
        mix_block(nc, A, keep)
        with ExitStack() as peer:
            keep["hH"] = peer.enter_context(nc.sbuf_tensor("hH", [P, DC, T], F32R))
            keep["hL"] = peer.enter_context(nc.sbuf_tensor("hL", [P, DC, T], F32R))
            keep["h_rows"] = peer.enter_context(nc.sbuf_tensor("h_rows", [P, D], F32))
            s_all = peer.enter_context(nc.sbuf_tensor("s_all", [P, 2 * PH, NT, P], F32))
            query_block(nc, A, keep, s_all)
            expert_block(nc, A, keep, s_all, S_dram, G_dram)
        value_block(nc, A, keep, S_dram, G_dram, out)


_INS = ["x", "c", "positions", "w_mod", "b_mod", "g_pre_mix", "g_post_mix", "w_in", "conv_w", "b_igate", "b_fgate",
        "mlstm_norm_g", "att_sinks", "w_out", "g_pre_ffn", "g_post_ffn", "peer_wq", "peer_keys1", "peer_keys2",
        "peer_u", "peer_v"]


def kernel(**inputs):
    import numpy as np
    import concourse.bacc as bacc
    from concourse.bass_utils import run_bass_kernel_spmd

    nc = bacc.Bacc("TRN2", target_bir_lowering=False, num_devices=1)
    arrays, A = {}, {}
    for name in _INS:
        a = np.ascontiguousarray(inputs[name])
        arrays[f"in_{name}"] = a
        A[name] = nc.dram_tensor(f"in_{name}", a.shape, mybir.dt.from_np(a.dtype), kind="ExternalInput").ap()
    inv = np.float32(10000.0) ** (-np.arange(0, DH, 2, dtype=np.float32) / np.float32(DH))
    arrays["in_inv_freq"] = inv.astype(np.float32)
    A["inv_freq"] = nc.dram_tensor("in_inv_freq", inv.shape, F32, kind="ExternalInput").ap()
    out = nc.dram_tensor("out_0", (1, T, D), F32, kind="ExternalOutput").ap()
    build(nc, A, out)
    r = run_bass_kernel_spmd(nc, [arrays], core_ids=[0])
    return r.results[0]["out_0"]
```

```python
from contextlib import ExitStack

import concourse.bass as bass
from concourse import mybir

F32 = mybir.dt.float32
F32R = mybir.dt.float32r
I32 = mybir.dt.int32
U32 = mybir.dt.uint32
ALU = mybir.AluOpType
ACT = mybir.ActivationFunctionType
AX = mybir.AxisListType.X

P = 128
T = 512
NT = T // P
D = 1024
DC = D // P
HEADS, KV, DH = 8, 2, 64
GROUP = HEADS // KV
MH, MV, MQ = 4, 128, 64
TAPS = 4
NEG = -1.0e30
EPS = 1e-6
PI = 3.141592653589793
TWO_PI_HI, TWO_PI_MID = 6.28125, 0.0019350051879882812
TWO_PI_LO = 2 * PI - TWO_PI_HI - TWO_PI_MID
ROUND = 12582912.0

C_AQ, C_AK, C_MQ, C_MV, C_MI, C_MF, C_MO, C_END = 0, 512, 768, 1280, 1792, 1796, 1800, 2312
SHIFT1, SCALE1, GATE1, SHIFT2, SCALE2, GATE2 = range(6)

PH, PK, PTOP = 8, 128, 16
NE = PK * PK
NBLK = NE // P
CAND = [(a, b) for a in range(PTOP) for b in range(PTOP) if (a + 1) * (b + 1) <= PTOP]
NCAND = len(CAND)
K = PH * PTOP
TD = T - P
NTD = TD // P
GT = 6
GSTEPS = TD // GT
TB = 2 * GT
NTB = TD // TB
BG = 16
GP = BG // 4
NBG = NBLK // BG
LEAD = 56
RING = 4
LEAD_ROWS = 48
TAIL = NBLK - LEAD - GSTEPS
TWICE = 12
TAIL_ROWS = 4
assert LEAD_ROWS + GSTEPS + TWICE + TAIL_ROWS == K


class Chain:

    def __init__(self, eng, sem):
        self.eng, self.sem, self.n = eng, sem, 0

    def put(self, ins):
        self.n += 1
        ins.then_inc(self.sem, 1)

    def wait(self):
        self.eng.wait_ge(self.sem, self.n)

    def __call__(self, ins):
        self.put(ins)
        self.wait()


class Banks:

    def __init__(self, psum, order, full, free):
        self.psum, self.full, self.free, self.n = psum, full, free, len(full)
        self.number = {name: i for i, name in enumerate(order)}
        assert len(self.number) == len(order)

    def __call__(self, *name):
        return self.psum[:, self.number[name] % self.n, :]

    def wait_free(self, pe, *name):
        k = self.number[name]
        if k >= self.n:
            pe.wait_ge(self.free[k % self.n], k // self.n)

    def wait_full(self, eng, *name):
        k = self.number[name]
        eng.wait_ge(self.full[k % self.n], k // self.n + 1)

    def wait_released(self, eng, *name):
        k = self.number[name]
        eng.wait_ge(self.free[k % self.n], k // self.n + 1)

    def done(self, ins, *name):
        ins.then_inc(self.full[self.number[name] % self.n], 1)

    def release(self, ins, *name):
        ins.then_inc(self.free[self.number[name] % self.n], 1)


def rsqrt(nc, step, y, a, half_a, t):
    step(nc.vector.tensor_scalar(t.bitcast(U32), a.bitcast(U32), 1, None, ALU.logical_shift_right))
    step(nc.vector.tensor_scalar(y.bitcast(I32), t.bitcast(I32), -1.0, float(0x5F3759DF), ALU.mult, ALU.add))
    step(nc.vector.tensor_scalar(half_a, a, -0.5, None, ALU.mult))
    for _ in range(3):
        step(nc.vector.tensor_tensor(t, y, y, ALU.mult))
        step(nc.vector.tensor_tensor(t, t, half_a, ALU.mult))
        step(nc.vector.scalar_tensor_tensor(out=y, in0=t, scalar=1.5, in1=y, op0=ALU.add, op1=ALU.mult))


def mix_block(nc, A, keep):
    x_sb, hT, ident, cols, gg2 = keep["x"], keep["hT"], keep["ident"], keep["cols"], keep["gg2"]
    with ExitStack() as ctx:
        def sb(name, shape, dt=F32):
            return ctx.enter_context(nc.sbuf_tensor(name, shape, dt))

        def sem(name):
            return ctx.enter_context(nc.semaphore(name))

        mods = [("mod", s, h) for h in range(2) for s in (SCALE1, SHIFT1)]
        mods += [("mod", s, h) for s in (GATE1, SCALE2, SHIFT2, GATE2) for h in range(2)]
        mod_no = {m: i for i, m in enumerate(mods)}
        EARLY, BESIDE = 3, 10
        slabs = mods[0:2] + [("in", C_MQ)] + mods[2:EARLY] + [("in", C_AQ), ("in", C_AK), ("in", C_MV), ("in", C_MO)]
        slabs += mods[BESIDE:] + [("out", h) for h in range(2)]
        NW = 3
        slab_no = {s: i for i, s in enumerate(slabs)}

        scores = lambda n: [("sc", n, g, jp) for g in range(KV) for jp in range(2)]
        probsT = lambda n: [("pT", n, i) for i in range(4)]
        mscore = lambda h: [("ms", h, s) for s in range(NT)]
        mvalue = lambda h: [("mv2", h, i) for i in range(2)]
        modg = lambda s: [("modg", s, h) for h in range(2)]
        av_of = lambda n: [("av", n, g) for g in range(KV)]
        order = [("rows",)] + [("xT", c) for c in range(DC)] 
        order += [("modc", SCALE1, 0), ("modc", SHIFT1, 0)]
        order += [("mq", j) for j in range(4)] + [("modc", SCALE1, 1), ("modc", SHIFT1, 1)]
        order += [(k, t) for k in ("aq", "kv") for t in range(NT)]
        order += modg(GATE1) + [("gi",), ("gf",)] + [("mv", t) for t in range(NT)] + [("modc", SCALE2, h) for h in range(2)]
        order += [("qT", t) for t in range(NT)] + [("kT",), ("gcol",)] + [("rb", h) for h in range(MH)]
        order += scores(0) + mscore(0) + [("modc", SHIFT2, h) for h in range(2)] + [("mo", 0)] + scores(1) + [("mo", 1)]
        order += probsT(0) + av_of(0) + mvalue(0) + mscore(1) + [("mo", 2)]
        order += scores(2) + probsT(1) + av_of(1) + mvalue(1) + mscore(2) + [("mo", 3)]
        order += scores(3) + probsT(2) + av_of(2) + mvalue(2) + mscore(3) + modg(GATE2)
        order += probsT(3) + av_of(3) + mvalue(3)
        out_of = lambda t: [("out", h, t) for h in range(2)]
        h2T_of = lambda t: [("h2T", t, i) for i in range(2)]
        order += out_of(0) + out_of(1) + [("mixT", c) for c in range(4, 8)]
        order += out_of(2) + h2T_of(0) + out_of(3) + h2T_of(1) + h2T_of(2) + h2T_of(3)
        last_use = {("in", C_MQ): ("mq", 3), ("in", C_AQ): ("aq", 3), ("in", C_AK): ("kv", 3),
                    ("in", C_MV): ("mv", 3), ("in", C_MO): ("mo", 3)}
        last_use |= {("out", h): ("out", h, 3) for h in range(2)}

        psum = ctx.enter_context(nc.psum_tensor("mix_psum", [P, 8, 512], F32))
        slab = sb("slab", [P, NW, DC, 520])
        ones = sb("ones", [P, P])
        mod_sum = sb("mod_sum", [P, 4, 512])
        bias_if = sb("bias_if", [MH, 2])
        pos_i = sb("pos_i", [P, NT], I32)
        pos = sb("pos", [P, NT])
        inv_freq = sb("inv_freq", [P, DH // 2])
        sinks = sb("sinks", [P, HEADS])
        g_post = sb("g_post", [P, D])
        gg1 = sb("gg1", [P, D])
        m_norm = sb("m_norm", [P, MH * MV])
        stat = sb("stat", [P, 5, 16])
        angle = sb("angle", [P, 3, NT, DH // 2])
        trig = sb("trig", [P, 2, NT, DH // 2])
        cos_sin = sb("cos_sin", [P, NT, 2, DH])
        band = sb("band", [P, 2 * P])
        pick = sb("pick", [MH, MH, P])
        late = sb("late", [P, 2048 + 2 * 10 * P])
        gate = late[0:MH, 0:8 * T].rearrange("h (i t) -> h i t", i=8)
        I_, F_, E_, LF, B_, M_, R_, CS = range(8)
        zeros = late[0:MH, 8 * T:9 * T]
        gcol = sb("gcol", [P, NT, 8])
        em = sb("em", [P, NT, MH])
        both = sb("both", [P, NT, D])
        q_rot = both[:, :, 0:512]
        wide = both[:, :, 512:1024]
        k_rot = sb("k_rot", [P, NT, KV * DH])
        v_att = sb("v_att", [P, NT, KV, 2, DH])
        att_T = q_rot
        qT = sb("qT", [P, NT, GROUP, P])
        kT = sb("kT", [P, T])
        rows = kT[0:88, 0:P]
        v_ext = sb("v_ext", [P, NT, MH, MV + 1])
        o_gate = sb("o_gate", [P, NT, MH * MV])
        mqk = sb("mqk", [P, 4, T])
        rr = hT
        x_halves = x_sb[:].rearrange("p t (i n) -> p (t i) n", i=2)
        r_all = x_halves[:, 0:4, :]
        r_diag = x_halves[:, 4:8, :].rearrange("p h (b t) -> p h b t", b=NT)
        decay = sb("decay", [P, 2, T])
        TRI = [0, 4, 7, 9]
        pm = late[:, 2048:2048 + 20 * P].rearrange("p (a n) -> p a n", a=2)
        sc = sb("sc", [P, 2, HEADS, 2 * P])
        conv_in = sc[:, :, :, :].rearrange("p a b c -> p (a b c)")[:, 0:4 * 515].rearrange("p (j t) -> p j t", j=4)
        junk = sc[:, :, :, :].rearrange("p a b c -> p (a b c)")[:, 0:2048]
        pT = late[:, 0:2048].rearrange("p (h b q) -> p h b q", h=HEADS, b=2)
        mx = sb("mx", [P, 2, 6, HEADS])
        den = sb("den", [P, 4])

        bank_full = [sem(f"bank_full{i}") for i in range(8)]
        bank_free = [sem(f"bank_free{i}") for i in range(8)]
        bk = Banks(psum, order, bank_full, bank_free)
        slab_in = [sem(f"slab_in{i}") for i in range(NW)]
        x_in = [sem(f"x_in{i}") for i in range(NT)]
        names = ("rows_in bc_in small_in dve_chain act_chain pool_chain consts xn_ready mods_made beside_in angles trig_done "
                 "hT_ready f_abs f_exp f_ln gates_done diag_done em_done conv_pad conv_done silu_e mqk_ready "
                 "g_post2_in decay_done qrot_done krot_done v_done att_max att_exp att_normed mh_done o_gate_done mix_sq xn2_ready").split()
        S = {n: sem(n) for n in names}

        block = ctx.enter_context(nc.Block())

        def slab_of(name):
            if name[0] == "mod" and EARLY <= mod_no[name] < BESIDE:
                return x_sb[:].rearrange("p t (i n) -> p (t i) n", i=2)
            return slab[:, slab_no[name] % NW, :, :]

        def wait_slab(pe, name):
            n = slab_no[name]
            pe.wait_ge(slab_in[n % NW], 16 * (n // NW + 1))

        def att_turned(copy, eng, n, g):
            bk.wait_full(eng, "av", n, g)
            src = bk("av", n, g).rearrange("p (c i q) -> p c i q", i=2, q=P)
            for i in range(2):
                rows_ = slice(i * DH, (i + 1) * DH)
                ins = copy(att_T[rows_, 2 * g:2 * g + 2, n * P:(n + 1) * P], src[rows_, :, i, :])
            bk.release(ins, "av", n, g)

        def x_new(t):
            return late[:, t * D:(t + 1) * D]

        @block.sync
        def _(sp):
            for t in range(NT):
                sp.dma_start(x_sb[:, t, :], A["x"][0, t * P:(t + 1) * P, :]).then_inc(x_in[t], 16)
            sp.dma_start(rows[0:48, :], A["b_mod"][0].rearrange("(r p) -> r p", p=P)).then_inc(S["rows_in"], 16)
            sp.dma_start(rows[48:56, :], A["g_pre_mix"][0].rearrange("(r p) -> r p", p=P)).then_inc(S["rows_in"], 16)
            sp.dma_start(rows[56:64, :], A["g_pre_ffn"][0].rearrange("(r p) -> r p", p=P)).then_inc(S["rows_in"], 16)
            sp.dma_start(rows[64:80, :], A["conv_w"][0].rearrange("j (r p) -> (j r) p", p=P)).then_inc(S["rows_in"], 16)
            sp.dma_start(rows[80:88, :], A["c"][0].rearrange("(r p) -> r p", p=P)).then_inc(S["rows_in"], 16)
            for n, name in enumerate(slabs):
                if n >= NW:
                    old = slabs[n - NW]
                    if old[0] != "mod":
                        bk.wait_full(sp, *last_use[old])
                    else:
                        sp.wait_ge(S["mods_made"], mod_no[old] + 1)
                if name[0] == "mod":
                    src, c0, w = A["w_mod"], name[1] * D + name[2] * 512, 512
                elif name[0] == "in":
                    src, c0 = A["w_in"], name[1]
                    w = {C_MQ: 512, C_AQ: 512, C_AK: 256, C_MV: 520, C_MO: 512}[c0]
                else:
                    src, c0, w = A["w_out"], name[1] * 512, 512
                sp.dma_start(slab_of(name)[:, :, 0:w],
                             src[0, :, c0:c0 + w].rearrange("(c p) n -> p c n", p=P)).then_inc(slab_in[n % NW], 16)
            sp.wait_ge(S["decay_done"], MH * NT)
            for t in range(NT):
                sp.dma_start(x_sb[:, t, :], A["x"][0, t * P:(t + 1) * P, :]).then_inc(x_in[t], 16)

        @block.gpsimd
        def _(pool):
            step = Chain(pool, S["pool_chain"])
            pool.dma_start(pos_i[:], A["positions"][0].rearrange("(t p) -> p t", p=P), allow_slow_non_contiguous=True).then_inc(S["small_in"], 16)
            pool.dma_start(bias_if[:, 0:1], A["b_igate"].rearrange("a h -> h a"), allow_slow_non_contiguous=True).then_inc(S["small_in"], 16)
            pool.dma_start(bias_if[:, 1:2], A["b_fgate"].rearrange("a h -> h a"), allow_slow_non_contiguous=True).then_inc(S["small_in"], 16)
            step(nc.gpsimd.memset(ident[:], 0.0))
            nc.gpsimd.affine_select(out=ident[:], in_=ident[:], compare_op=ALU.not_equal, fill=1.0, base=0,
                                    pattern=[[-1, P]], channel_multiplier=1).then_inc(S["consts"], 1)
            nc.gpsimd.memset(conv_in[:, :, 0:3], 0.0).then_inc(S["conv_pad"], 1)
            nc.gpsimd.memset(ones[:], 1.0).then_inc(S["consts"], 1)
            nc.gpsimd.memset(zeros, 0.0).then_inc(S["consts"], 1)
            nc.gpsimd.memset(v_ext[:, :, :, MV:MV + 1], 1.0).then_inc(S["consts"], 1)
            step(nc.gpsimd.memset(pick[:], 1.0))
            nc.gpsimd.affine_select(out=pick[:], in_=pick[:], compare_op=ALU.is_equal, fill=0.0, base=0,
                                    pattern=[[-1, MH], [0, P]], channel_multiplier=1).then_inc(S["consts"], 1)
            step(nc.gpsimd.memset(band[:], 0.0))
            step(nc.gpsimd.affine_select(out=band[:], in_=band[:], compare_op=ALU.is_gt, fill=NEG, base=0,
                                         pattern=[[1, 2 * P]], channel_multiplier=-1))
            nc.gpsimd.affine_select(out=band[:], in_=band[:], compare_op=ALU.is_ge, fill=NEG, base=P,
                                    pattern=[[-1, 2 * P]], channel_multiplier=1).then_inc(S["consts"], 1)
            pool.wait_ge(S["xn_ready"], NT)
            for name in mods[EARLY:BESIDE]:
                if mod_no[name] > EARLY:
                    pool.wait_ge(S["mods_made"], mod_no[name])
                c0 = name[1] * D + name[2] * 512
                pool.dma_start(slab_of(name), A["w_mod"][0, :, c0:c0 + 512].rearrange("(c p) n -> p c n", p=P)
                               ).then_inc(S["beside_in"], 16)
            for h in range(MH):
                bk.wait_released(pool, "rb", h)
                nc.gpsimd.affine_select(out=r_diag[:, h, :, :], in_=r_all[:, h, :].rearrange("p (b t) -> p b t", b=NT),
                                        compare_op=ALU.is_ge, fill=NEG, base=0, pattern=[[0, NT], [1, P]],
                                        channel_multiplier=-1).then_inc(S["diag_done"], 1)

        CONSTS = 6

        @block.tensor
        def _(pe):
            mm, tr = nc.tensor.matmul, nc.tensor.transpose
            pe.wait_ge(S["consts"], 1)
            pe.wait_ge(S["rows_in"], 80)
            bk.done(tr(bk("rows")[:, 0:88], rows, ident[0:88, 0:88]), "rows")
            pe.wait_ge(S["xn_ready"], NT)
            for c in range(DC):
                bk.wait_free(pe, "xT", c)
                for t in range(NT):
                    last = tr(bk("xT", c)[:, t * P:(t + 1) * P], both[:, t, c * P:(c + 1) * P], ident[:])
                bk.done(last, "xT", c)

            def mod_columns(s, h):
                bk.wait_free(pe, "modc", s, h)
                pe.wait_ge(S["mods_made"], mod_no[("mod", s, h)] + 1)
                for j in range(4):
                    last = mm(bk("modc", s, h)[:, j:j + 1], mod_sum[:, mod_no[("mod", s, h)] % 4, j * P:(j + 1) * P],
                              ones[:, 0:1], start=True, stop=True)
                bk.done(last, "modc", s, h)

            def mod_rows(s):
                for h in range(2):
                    pe.wait_ge(S["mods_made"], mod_no[("mod", s, h)] + 1)
                    bk.wait_free(pe, "modg", s, h)
                    bk.done(mm(bk("modg", s, h), ones[:], mod_sum[:, mod_no[("mod", s, h)] % 4, :], start=True, stop=True), "modg", s, h)

            pe.wait_ge(S["consts"], CONSTS)
            mod_columns(SCALE1, 0)
            mod_columns(SHIFT1, 0)
            w = slab_of(("in", C_MQ))
            wait_slab(pe, ("in", C_MQ))
            order_of_gates = (("gi", C_MI), ("gf", C_MF))
            for half in range(2):
                if half == 1:
                    mod_columns(SCALE1, 1)
                    mod_columns(SHIFT1, 1)
                pe.wait_ge(S["hT_ready"], 4 * half + 4)
                for j in range(4):
                    if half == 0:
                        bk.wait_free(pe, "mq", j)
                    for c in range(4 * half, 4 * half + 4):
                        last = mm(bk("mq", j), w[:, c, j * P:(j + 1) * P], hT[:, c, :], start=(c == 0), stop=(c == DC - 1))
                    if half == 1:
                        bk.done(last, "mq", j)
            for kind, c0, width in (("aq", C_AQ, 512), ("kv", C_AK, 256)):
                w = slab_of(("in", c0))
                wait_slab(pe, ("in", c0))
                for t in range(NT):
                    bk.wait_free(pe, kind, t)
                    for c in range(DC):
                        last = mm(bk(kind, t)[:, 0:width], hT[:, c, t * P:(t + 1) * P], w[:, c, 0:width],
                                  start=(c == 0), stop=(c == DC - 1))
                    bk.done(last, kind, t)
            mod_rows(GATE1)
            w = slab_of(("in", C_MV))
            wait_slab(pe, ("in", C_MV))
            for name, col in order_of_gates:
                bk.wait_free(pe, name)
                for c in range(DC):
                    last = mm(bk(name)[0:MH, :], w[:, c, col - C_MV:col - C_MV + MH], hT[:, c, :],
                              start=(c == 0), stop=(c == DC - 1))
                bk.done(last, name)
            def wide_product(kind, c0, t):
                w = slab_of(("in", c0))
                if t == 0:
                    wait_slab(pe, ("in", c0))
                bk.wait_free(pe, kind, t)
                for c in range(DC):
                    last = mm(bk(kind, t), hT[:, c, t * P:(t + 1) * P], w[:, c, 0:512], start=(c == 0), stop=(c == DC - 1))
                bk.done(last, kind, t)

            for t in range(NT):
                wide_product("mv", C_MV, t)
            for h in range(2):
                mod_columns(SCALE2, h)
            for t in range(NT):
                pe.wait_ge(S["qrot_done"], t + 1)
                bk.wait_free(pe, "qT", t)
                for j in range(GROUP):
                    last = tr(bk("qT", t)[:, j * P:(j + 1) * P], q_rot[:, t, j * P:(j + 1) * P], ident[:])
                bk.done(last, "qT", t)
            pe.wait_ge(S["krot_done"], NT)
            bk.wait_free(pe, "kT")
            for t in range(NT):
                last = tr(bk("kT")[:, t * P:(t + 1) * P], k_rot[:, t, :], ident[:])
            bk.done(last, "kT")
            pe.wait_ge(S["gates_done"], 1)
            bk.wait_free(pe, "gcol")
            for t in range(NT):
                for i, row in enumerate((CS, M_)):
                    last = tr(bk("gcol")[:, t * 8 + i * 4:t * 8 + i * 4 + 4], gate[:, row, t * P:(t + 1) * P], ident[0:MH, 0:MH])
            bk.done(last, "gcol")
            pe.wait_ge(S["consts"], CONSTS)
            for h in range(MH):
                bk.wait_free(pe, "rb", h)
                bk.done(mm(bk("rb", h), pick[:, h, :], gate[:, R_, :], start=True, stop=True), "rb", h)

            def att_scores(n):
                k0 = max(n - 1, 0) * P
                wide_ = (n + 1) * P - k0
                bk.wait_released(pe, "qT", n)
                bk.wait_released(pe, "kT")
                for name in scores(n):
                    _, _, g, jp = name
                    bk.wait_free(pe, *name)
                    for i in range(2):
                        last = mm(bk(*name)[:, i * wide_:(i + 1) * wide_], qT[g * DH:(g + 1) * DH, n, jp * 2 + i, :],
                                  kT[g * DH:(g + 1) * DH, k0:k0 + wide_], start=True, stop=True)
                    bk.done(last, *name)

            def att_values(n):
                pe.wait_ge(S["att_normed"], n + 1)
                blocks = 1 if n == 0 else 2
                for i, name in enumerate(probsT(n)):
                    bk.wait_free(pe, *name)
                    for hh in range(2):
                        for b in range(blocks):
                            at = (hh * blocks + b) * P
                            last = tr(bk(*name)[:, at:at + P], sc[:, n % 2, 2 * i + hh, b * P:(b + 1) * P], ident[:])
                    bk.done(last, *name)
                for name in probsT(n):
                    bk.wait_released(pe, *name)
                pe.wait_ge(S["v_done"], NT)
                for g in range(KV):
                    bk.wait_free(pe, "av", n, g)
                    for b in range(blocks):
                        last = mm(bk("av", n, g).rearrange("p (h q) -> p h q", h=GROUP),
                                  v_att[:, n - blocks + 1 + b, g, :, :].rearrange("p a d -> p (a d)"),
                                  pT[:, g * GROUP:(g + 1) * GROUP, b, :], start=(b == 0), stop=(b == blocks - 1))
                    bk.done(last, "av", n, g)

            def mlstm_scores(h):
                pe.wait_ge(S["mqk_ready"], 1)
                p0 = (h % 2) * MQ
                for s in range(NT):
                    bk.wait_free(pe, "ms", h, s)
                    bk.done(mm(bk("ms", h, s)[:, 0:T - s * P], mqk[p0:p0 + MQ, 2 + h // 2, s * P:(s + 1) * P],
                               mqk[p0:p0 + MQ, h // 2, s * P:T], start=True, stop=True), "ms", h, s)

            def mlstm_values(h):
                for s in range(NT):
                    bk.wait_released(pe, "ms", h, s)
                    bk.wait_released(pe, "mv", s)
                for i in range(2):
                    bk.wait_free(pe, "mv2", h, i)
                    for tt in range(2):
                        t = 2 * i + tt
                        for s in range(t + 1):
                            at = (TRI[s] + t - s) * P
                            last = mm(bk("mv2", h, i)[:, tt * (MV + 1):(tt + 1) * (MV + 1)], pm[:, h % 2, at:at + P],
                                      v_ext[:, s, h, :], start=(s == 0), stop=(s == t))
                    bk.done(last, "mv2", h, i)

            att_scores(0)
            mlstm_scores(0)
            for h in range(2):
                mod_columns(SHIFT2, h)
            wide_product("mo", C_MO, 0)
            att_scores(1)
            wide_product("mo", C_MO, 1)
            att_values(0)
            mlstm_values(0)
            mlstm_scores(1)
            wide_product("mo", C_MO, 2)
            att_scores(2)
            att_values(1)
            mlstm_values(1)
            mlstm_scores(2)
            wide_product("mo", C_MO, 3)
            att_scores(3)
            att_values(2)
            mlstm_values(2)
            mlstm_scores(3)
            mod_rows(GATE2)
            att_values(3)
            mlstm_values(3)
            def mix_T(c):
                bk.wait_free(pe, "mixT", c)
                for t in range(NT):
                    last = tr(bk("mixT", c)[:, t * P:(t + 1) * P], both[:, t, c * P:(c + 1) * P], ident[:])
                bk.done(last, "mixT", c)

            def out_product(t, chunks):
                for h in range(2):
                    if chunks[0] == 0:
                        bk.wait_free(pe, "out", h, t)
                    for c in chunks:
                        mixed = att_T[:, c, t * P:(t + 1) * P] if c < 4 else rr[:, c, t * P:(t + 1) * P]
                        last = mm(bk("out", h, t), mixed, slab_of(("out", h))[:, c, 0:512],
                                  start=(c == 0), stop=(c == DC - 1))
                    if chunks[-1] == DC - 1:
                        bk.done(last, "out", h, t)

            def h2_T(t):
                pe.wait_ge(S["xn2_ready"], t + 1)
                for i in range(2):
                    bk.wait_free(pe, "h2T", t, i)
                    for k in range(4):
                        c = 4 * i + k
                        last = tr(bk("h2T", t, i)[:, k * P:(k + 1) * P], x_new(t)[:, c * P:(c + 1) * P], ident[:])
                    bk.done(last, "h2T", t, i)

            for n in range(NT):
                for g in range(KV):
                    bk.wait_released(pe, "av", n, g)
            for h in range(2):
                wait_slab(pe, ("out", h))
            for t in range(2):
                out_product(t, range(4))
            pe.wait_ge(S["mh_done"], 1)
            for c in range(4, DC):
                mix_T(c)
            for c in range(4, DC):
                bk.wait_released(pe, "mixT", c)
            for t in range(2):
                out_product(t, range(4, DC))
            out_product(2, range(DC))
            h2_T(0)
            out_product(3, range(DC))
            for t in range(1, NT):
                h2_T(t)

        @block.scalar
        def _(act):
            func = nc.scalar.activation
            step = Chain(act, S["act_chain"])
            for dst, src in ((inv_freq, A["inv_freq"]), (sinks, A["att_sinks"][0]), (gg1, A["b_mod"][0, GATE1 * D:(GATE1 + 1) * D]),
                             (g_post, A["g_post_mix"][0]), (gg2, A["b_mod"][0, GATE2 * D:(GATE2 + 1) * D]),
                             (m_norm, A["mlstm_norm_g"][0].rearrange("h v -> (h v)"))):
                act.dma_start(dst[:], src.partition_broadcast(P)).then_inc(S["bc_in"], 16)
            for c in range(DC):
                bk.wait_full(act, "xT", c)
                ins = func(hT[:, c, :], bk("xT", c), ACT.Copy)
                bk.release(ins, "xT", c)
            act.wait_ge(S["angles"], 1)
            func(trig[:].rearrange("p a t f -> p (a t f)"), angle[:, 1:3, :, :].rearrange("p a t f -> p (a t f)"),
                 ACT.Sin).then_inc(S["trig_done"], 1)
            act.wait_ge(S["conv_pad"], 1)
            act.wait_ge(S["xn_ready"], NT)
            for j in range(4):
                bk.wait_full(act, "mq", j)
                bk.release(func(conv_in[:, j, 3:3 + T], bk("mq", j), ACT.Copy), "mq", j)
            act.wait_ge(S["conv_done"], 1)
            func(wide, mqk[:], ACT.Sigmoid).then_inc(S["silu_e"], 1)
            act.wait_ge(S["f_abs"], 1)
            func(gate[:, E_, :], gate[:, E_, :], ACT.Exp, scale=-1.0).then_inc(S["f_exp"], 1)
            act.wait_ge(S["f_exp"], 1)
            func(gate[:, E_, :], gate[:, E_, :], ACT.Ln, bias=1.0).then_inc(S["f_ln"], 1)
            act.wait_ge(S["consts"], CONSTS)
            for t in range(NT):
                bk.wait_full(act, "mv", t)
                ins = func(v_ext[:, t, :, 0:MV], bk("mv", t).rearrange("p (h v) -> p h v", h=MH), ACT.Copy)
                bk.release(ins, "mv", t)
            act.wait_ge(S["mods_made"], BESIDE)
            for h in range(MH):
                bk.wait_full(act, "rb", h)
                bk.release(func(r_all[:, h, :], bk("rb", h), ACT.Copy), "rb", h)
            bk.wait_released(act, "gcol")
            act.dma_start(g_post[:], A["g_post_ffn"][0].partition_broadcast(P)).then_inc(S["g_post2_in"], 16)
            func(em[:], gcol[:, :, 4:8], ACT.Exp, scale=-1.0).then_inc(S["em_done"], 1)

            def att_exp(n):
                act.wait_ge(S["att_max"], n + 1)
                keys = P if n == 0 else 2 * P
                for h in range(HEADS):
                    func(sc[:, n % 2, h, 0:keys], sc[:, n % 2, h, 0:keys], ACT.Exp, bias=mx[:, n % 2, 1, h:h + 1],
                         accum_out=mx[:, n % 2, 3, h:h + 1])
                func(mx[:, n % 2, 4, :], mx[:, n % 2, 2, :], ACT.Exp).then_inc(S["att_exp"], 1)

            def probs_T(n):
                blocks = 1 if n == 0 else 2
                for i in range(2):
                    name = ("pT", n, i)
                    bk.wait_full(act, *name)
                    if n and i == 0:
                        for g in range(KV):
                            bk.wait_full(act, "av", n - 1, g)
                    ins = func(pT[:, 2 * i:2 * i + 2, 0:blocks, :],
                               bk(*name)[:, 0:2 * blocks * P].rearrange("p (h b q) -> p h b q", h=2, b=blocks), ACT.Copy)
                    bk.release(ins, *name)
                att_turned(lambda out, in_: func(out, in_, ACT.Copy), act, n, 0)

            def decays(h):
                act.wait_ge(S["diag_done"], h + 1)
                for s in range(NT):
                    k = h * NT + s - 2
                    if k >= 0:
                        bk.wait_released(act, "ms", k // NT, k % NT)
                    bias = gcol[:, s, h:h + 1]
                    ins = func(decay[:, s % 2, 0:P], r_diag[:, h, s, :], ACT.Exp, bias=bias)
                    if s < NT - 1:
                        ins = func(decay[:, s % 2, P:T - s * P], r_all[:, h, (s + 1) * P:T], ACT.Exp, bias=bias)
                    ins.then_inc(S["decay_done"], 1)

            def out_gate(t):
                bk.wait_full(act, "mo", t)
                bk.release(func(o_gate[:, t, :], bk("mo", t), ACT.Copy), "mo", t)

            decays(0)
            att_exp(0)
            out_gate(0)
            att_exp(1)
            out_gate(1)
            probs_T(0)
            decays(1)
            out_gate(2)
            probs_T(1)
            att_exp(2)
            decays(2)
            out_gate(3)
            probs_T(2)
            att_exp(3)
            decays(3)
            for t in range(NT):
                bk.wait_released(act, "mo", t)
            func(o_gate[:], o_gate[:], ACT.Sigmoid).then_inc(S["o_gate_done"], 1)
            probs_T(3)
            for c in range(4, DC):
                bk.wait_full(act, "mixT", c)
                bk.release(func(rr[:, c, :], bk("mixT", c), ACT.Copy), "mixT", c)

            def mix_squares(t):
                for h in range(2):
                    bk.wait_full(act, "out", h, t)
                    func(sc[:, 0, 0:2, :], bk("out", h, t).rearrange("p (a b) -> p a b", a=2), ACT.Square,
                         accum_out=stat[:, 0, 2 * t + h:2 * t + h + 1]).then_inc(S["mix_sq"], 1)
                    act.wait_ge(S["mix_sq"], 2 * t + h + 1)

            def h2_modulated(t, i):
                bk.wait_full(act, "h2T", t, i)
                for k in range(4):
                    c = 4 * i + k
                    ins = func(hT[:, c, t * P:(t + 1) * P], bk("h2T", t, i)[:, k * P:(k + 1) * P], ACT.Identity,
                               scale=cols[:, SCALE2 * 8 + c:SCALE2 * 8 + c + 1], bias=cols[:, SHIFT2 * 8 + c:SHIFT2 * 8 + c + 1])
                bk.release(ins, "h2T", t, i)

            for t in range(3):
                mix_squares(t)
            for t in range(3):
                for i in range(2):
                    h2_modulated(t, i)
                if t == 0:
                    mix_squares(3)
            h2_modulated(3, 0)

        @block.vector
        def _(dve):
            v = nc.vector
            step = Chain(dve, S["dve_chain"])

            def mean_to_rstd(width, n, at=0):
                row = lambda i: stat[:, i, at:at + n]
                step(v.tensor_scalar(row(2), row(0), 1.0 / width, EPS, ALU.mult, ALU.add))
                rsqrt(nc, step, row(1), row(2), row(3), row(4))

            for t in range(NT):
                dve.wait_ge(x_in[t], 16)
                step(v.tensor_tensor_reduce(out=both[:, t, :], in0=x_sb[:, t, :], in1=x_sb[:, t, :], scale=1.0, scalar=0.0,
                                            op0=ALU.mult, op1=ALU.add, accum_out=stat[:, 0, t:t + 1]))
            mean_to_rstd(D, NT)
            for t in range(NT):
                v.tensor_scalar(both[:, t, :], x_sb[:, t, :], stat[:, 1, t:t + 1], None, ALU.mult).then_inc(S["xn_ready"], 1)
            bk.wait_full(dve, "rows")
            ins = v.tensor_copy(cols[:, 0:88], bk("rows")[:, 0:88])
            bk.release(ins, "rows")
            bk.wait_released(dve, "rows")

            def mod_sum_of(k):
                name, dst = mods[k], mod_sum[:, k % 4, :]
                w = slab_of(name)
                if EARLY <= k < BESIDE:
                    dve.wait_ge(S["beside_in"], 16 * (k - EARLY + 1))
                else:
                    wait_slab(dve, name)
                if k >= 4:
                    _, s, h = mods[k - 4]
                    bk.wait_full(dve, "modg" if s in (GATE1, GATE2) else "modc", s, h)
                step(v.tensor_scalar(dst, w[:, 0, 0:512], cols[:, 80:81], None, ALU.mult))
                for c in range(1, DC):
                    ins = v.scalar_tensor_tensor(out=dst, in0=w[:, c, 0:512], scalar=cols[:, 80 + c:81 + c], in1=dst,
                                                 op0=ALU.mult, op1=ALU.add)
                    if c < DC - 1:
                        step(ins)
                    else:
                        ins.then_inc(S["mods_made"], 1)

            def mod_col(s, h):
                a = s * 8 + 4 * h
                bk.wait_full(dve, "modc", s, h)
                ins = v.tensor_tensor(cols[:, a:a + 4], bk("modc", s, h)[:, 0:4], cols[:, a:a + 4], ALU.add)
                bk.release(ins, "modc", s, h)
                bk.wait_released(dve, "modc", s, h)

            def mod_scale(s, h, g0):
                a, g0 = s * 8 + 4 * h, g0 + 4 * h
                step(v.scalar_tensor_tensor(out=cols[:, a:a + 4], in0=cols[:, a:a + 4], scalar=1.0, in1=cols[:, g0:g0 + 4],
                                            op0=ALU.add, op1=ALU.mult))

            def mod_row(s, dst, g):
                for half in range(2):
                    at = slice(half * 512, half * 512 + 512)
                    bk.wait_full(dve, "modg", s, half)
                    ins = v.tensor_tensor(dst[:, at], bk("modg", s, half), dst[:, at], ALU.add)
                    bk.release(ins, "modg", s, half)
                    bk.wait_released(dve, "modg", s, half)
                    step(v.tensor_tensor(dst[:, at], dst[:, at], g[:, at], ALU.mult))

            for h in range(2):
                mod_sum_of(2 * h)
                mod_sum_of(2 * h + 1)
                mod_col(SCALE1, h)
                mod_scale(SCALE1, h, 48)
                mod_col(SHIFT1, h)
                for c in range(4 * h, 4 * h + 4):
                    bk.wait_released(dve, "xT", c)
                    v.tensor_scalar(hT[:, c, :], hT[:, c, :], cols[:, 8 * SCALE1 + c:8 * SCALE1 + c + 1],
                                    cols[:, 8 * SHIFT1 + c:8 * SHIFT1 + c + 1], ALU.mult, ALU.add).then_inc(S["hT_ready"], 1)
            dve.wait_ge(S["small_in"], 48)
            dve.wait_ge(S["bc_in"], 6 * 16)
            step(v.tensor_copy(pos[:], pos_i[:]))
            for t in range(NT):
                step(v.tensor_scalar(angle[:, 0, t, :], inv_freq[:], pos[:, t:t + 1], None, ALU.mult))
            for i, quarter in ((2, 0.0), (1, 0.25)):
                a, k = angle[:, i, :, :], trig[:, 0, :, :]
                step(v.tensor_scalar(k, angle[:, 0, :, :], 1.0 / (2 * PI), quarter, ALU.mult, ALU.add))
                step(v.tensor_scalar(k, k, ROUND, None, ALU.add))
                step(v.tensor_scalar(k, k, ROUND, None, ALU.subtract))
                step(v.scalar_tensor_tensor(out=a, in0=k, scalar=-TWO_PI_HI, in1=angle[:, 0, :, :], op0=ALU.mult, op1=ALU.add))
                for part in (TWO_PI_MID, TWO_PI_LO):
                    step(v.scalar_tensor_tensor(out=a, in0=k, scalar=-part, in1=a, op0=ALU.mult, op1=ALU.add))
                if quarter:
                    step(v.tensor_scalar(a, a, PI / 2, None, ALU.add))
                ins = v.tensor_scalar(a, a, 3.1415925, -3.1415925, ALU.min, ALU.max)
                if quarter:
                    ins.then_inc(S["angles"], 1)
                else:
                    step(ins)
            dve.wait_ge(S["trig_done"], 1)
            for half in range(2):
                v.tensor_copy(cos_sin[:, :, 0, half * 32:half * 32 + 32], trig[:, 0, :, :])
            v.tensor_copy(cos_sin[:, :, 1, 32:64], trig[:, 1, :, :])
            step(v.tensor_scalar(cos_sin[:, :, 1, 0:32], trig[:, 1, :, :], -1.0, None, ALU.mult))
            mod_sum_of(4)
            for j in range(4):
                bk.wait_released(dve, "mq", j)
                acc = mqk[:, j, :]
                step(v.tensor_scalar(acc, conv_in[:, j, 0:T], cols[:, 64 + j:65 + j], None, ALU.mult))
                for tap in range(1, TAPS):
                    w = cols[:, 64 + tap * 4 + j:65 + tap * 4 + j]
                    ins = v.scalar_tensor_tensor(out=acc, in0=conv_in[:, j, tap:tap + T], scalar=w, in1=acc,
                                                 op0=ALU.mult, op1=ALU.add)
                    if j == 3 and tap == TAPS - 1:
                        ins.then_inc(S["conv_done"], 1)
                    else:
                        step(ins)
            tmp = junk[:, 0:512].rearrange("p (g j d) -> p g j d", g=KV, j=GROUP)
            dve.wait_ge(S["conv_done"], 1)
            mod_sum_of(5)
            for t in range(NT):
                bk.wait_full(dve, "aq", t)
                src = bk("aq", t).rearrange("p (g j d) -> p g j d", g=KV, j=GROUP)
                dst = q_rot[:, t, :].rearrange("p (j g d) -> p g j d", g=KV, j=GROUP)
                for g in range(KV):
                    cs = lambda i, a, b: cos_sin[:, t, i, a:b].unsqueeze(1).broadcast_to([P, GROUP, b - a])
                    v.tensor_tensor(tmp[:, g, :, 0:32], src[:, g, :, 32:64], cs(1, 0, 32), ALU.mult)
                    v.tensor_tensor(tmp[:, g, :, 32:64], src[:, g, :, 0:32], cs(1, 32, 64), ALU.mult)
                    ins = v.tensor_tensor(dst[:, g, :, :], src[:, g, :, :], cs(0, 0, 64), ALU.mult)
                    if g == KV - 1:
                        bk.release(ins, "aq", t)
                        bk.wait_released(dve, "aq", t)
                    else:
                        step(ins)
                for g in range(KV):
                    ins = v.tensor_tensor(dst[:, g, :, :], dst[:, g, :, :], tmp[:, g, :, :], ALU.add)
                    if g == KV - 1:
                        ins.then_inc(S["qrot_done"], 1)
                        dve.wait_ge(S["qrot_done"], t + 1)
                if t % 2:
                    mod_sum_of(6 + t // 2)
            tmp = junk[:, 0:128].rearrange("p (g d) -> p g d", g=KV)
            for t in range(NT):
                bk.wait_full(dve, "kv", t)
                src = bk("kv", t)[:, 0:P].rearrange("p (g d) -> p g d", g=KV)
                dst = k_rot[:, t, :].rearrange("p (g d) -> p g d", g=KV)
                cs = lambda i, a, b: cos_sin[:, t, i, a:b].unsqueeze(1).broadcast_to([P, KV, b - a])
                v.tensor_tensor(tmp[:, :, 0:32], src[:, :, 32:64], cs(1, 0, 32), ALU.mult)
                v.tensor_tensor(tmp[:, :, 32:64], src[:, :, 0:32], cs(1, 32, 64), ALU.mult)
                v.tensor_copy(v_att[:, t, :, :, :], bk("kv", t)[:, P:2 * P].rearrange("p (g d) -> p g d", g=KV).unsqueeze(2)
                              .broadcast_to([P, KV, 2, DH])).then_inc(S["v_done"], 1)
                ins = v.tensor_tensor(dst, src, cs(0, 0, 64), ALU.mult)
                bk.release(ins, "kv", t)
                bk.wait_released(dve, "kv", t)
                v.tensor_tensor(dst, dst, tmp, ALU.add).then_inc(S["krot_done"], 1)
                dve.wait_ge(S["krot_done"], t + 1)
            mod_row(GATE1, gg1, g_post)
            mod_sum_of(8)
            dve.wait_ge(S["silu_e"], 1)
            v.tensor_tensor(mqk[:], mqk[:], wide, ALU.mult).then_inc(S["mqk_ready"], 1)
            mod_sum_of(9)
            bk.wait_full(dve, "gi")
            bk.release(v.tensor_scalar(gate[:, I_, :], bk("gi")[0:MH, :], bias_if[:, 0:1], None, ALU.add), "gi")
            bk.wait_full(dve, "gf")
            ins = v.tensor_scalar(gate[:, F_, :], bk("gf")[0:MH, :], bias_if[:, 1:2], None, ALU.add)
            bk.release(ins, "gf")
            bk.wait_released(dve, "gf")
            v.scalar_tensor_tensor(out=gate[:, E_, :], in0=gate[:, F_, :], scalar=-1.0, in1=gate[:, F_, :],
                                   op0=ALU.mult, op1=ALU.max).then_inc(S["f_abs"], 1)
            dve.wait_ge(S["f_ln"], 1)
            step(v.scalar_tensor_tensor(out=gate[:, LF, :], in0=gate[:, F_, :], scalar=0.0, in1=gate[:, E_, :],
                                        op0=ALU.min, op1=ALU.subtract))
            dve.wait_ge(S["consts"], CONSTS)
            step(v.tensor_tensor_scan(gate[:, B_, :], gate[:, LF, :], zeros, 0.0, ALU.add, ALU.add))
            step(v.tensor_tensor_scan(gate[:, M_, :], gate[:, LF, :], gate[:, I_, :], 0.0, ALU.add, ALU.max))
            step(v.tensor_tensor(gate[:, R_, :], gate[:, B_, :], gate[:, M_, :], ALU.subtract))
            v.tensor_tensor(gate[:, CS, :], gate[:, I_, :], gate[:, B_, :], ALU.subtract).then_inc(S["gates_done"], 1)
            for h in range(2):
                mod_col(SCALE2, h)
                mod_scale(SCALE2, h, 56)
            for t in range(NT):
                bk.wait_full(dve, "qT", t)
                ins = v.tensor_copy(qT[:, t, :, :], bk("qT", t).rearrange("p (j q) -> p j q", j=GROUP))
                bk.release(ins, "qT", t)
                bk.wait_released(dve, "qT", t)
            bk.wait_full(dve, "kT")
            ins = v.tensor_copy(kT[:], bk("kT"))
            bk.release(ins, "kT")
            bk.wait_released(dve, "kT")
            bk.wait_full(dve, "gcol")
            ins = v.tensor_copy(gcol[:], bk("gcol")[:, 0:NT * 8].rearrange("p (t i) -> p t i", t=NT))
            bk.release(ins, "gcol")
            def att_soft(n):
                keys = P if n == 0 else 2 * P
                if n >= 2:
                    bk.wait_full(dve, "pT", n - 2, 3)
                for name in scores(n):
                    _, _, g, jp = name
                    bk.wait_full(dve, *name)
                    h = g * GROUP + 2 * jp
                    ins = v.scalar_tensor_tensor(
                        out=sc[:, n % 2, h:h + 2, 0:keys], in0=bk(*name)[:, 0:2 * keys].rearrange("p (h s) -> p h s", h=2),
                        scalar=DH ** -0.5, in1=band[:, 2 * P - keys:2 * P].unsqueeze(1).broadcast_to([P, 2, keys]),
                        op0=ALU.mult, op1=ALU.add)
                    bk.release(ins, *name)
                for name in scores(n):
                    bk.wait_released(dve, *name)
                m = mx[:, n % 2, :, :]
                step(v.tensor_reduce(m[:, 0, :], sc[:, n % 2, :, 0:keys], AX, ALU.max))
                step(v.tensor_tensor(m[:, 0, :], m[:, 0, :], sinks[:], ALU.max))
                step(v.tensor_scalar(m[:, 1, :], m[:, 0, :], -1.0, None, ALU.mult))
                v.tensor_tensor(m[:, 2, :], sinks[:], m[:, 0, :], ALU.subtract).then_inc(S["att_max"], 1)

            def att_norm(n):
                keys = P if n == 0 else 2 * P
                m = mx[:, n % 2, :, :]
                dve.wait_ge(S["att_exp"], n + 1)
                step(v.tensor_tensor(m[:, 5, :], m[:, 3, :], m[:, 4, :], ALU.add))
                step(v.reciprocal(m[:, 5, :], m[:, 5, :]))
                v.tensor_tensor(sc[:, n % 2, :, 0:keys], sc[:, n % 2, :, 0:keys],
                                m[:, 5, :].unsqueeze(2).broadcast_to([P, HEADS, keys]), ALU.mult).then_inc(S["att_normed"], 1)

            def att_out(n):
                blocks = 1 if n == 0 else 2
                for i in range(2, 4):
                    name = ("pT", n, i)
                    bk.wait_full(dve, *name)
                    if n and i == 2:
                        for g in range(KV):
                            bk.wait_full(dve, "av", n - 1, g)
                    ins = v.tensor_copy(pT[:, 2 * i:2 * i + 2, 0:blocks, :],
                                        bk(*name)[:, 0:2 * blocks * P].rearrange("p (h b q) -> p h b q", h=2, b=blocks))
                    bk.release(ins, *name)
                att_turned(v.tensor_copy, dve, n, 1)

            def mlstm_weights(h):
                if h >= 2:
                    bk.wait_full(dve, "mv2", h - 2, 1)
                for s in range(NT):
                    n = T - s * P
                    bk.wait_full(dve, "ms", h, s)
                    dve.wait_ge(S["decay_done"], NT * h + s + 1)
                    ins = v.scalar_tensor_tensor(out=pm[:, h % 2, TRI[s] * P:TRI[s] * P + n], in0=bk("ms", h, s)[:, 0:n],
                                                 scalar=MQ ** -0.5, in1=decay[:, s % 2, 0:n], op0=ALU.mult, op1=ALU.mult)
                    bk.release(ins, "ms", h, s)

            def mlstm_out(h):
                dve.wait_ge(S["em_done"], 1)
                for i in range(2):
                    bk.wait_full(dve, "mv2", h, i)
                    src = bk("mv2", h, i)[:, 0:2 * (MV + 1)].rearrange("p (t v) -> p t v", t=2)
                    d = den[:, 2 * i:2 * i + 2].unsqueeze(2)
                    step(v.scalar_tensor_tensor(out=d, in0=src[:, :, MV:MV + 1], scalar=-1.0,
                                                in1=em[:, 2 * i:2 * i + 2, h:h + 1], op0=ALU.mult, op1=ALU.max))
                    step(v.tensor_tensor(d, src[:, :, MV:MV + 1], d, ALU.max))
                    step(v.reciprocal(d, d))
                    ins = v.tensor_tensor(wide[:, 2 * i:2 * i + 2, h * MV:(h + 1) * MV], src[:, :, 0:MV],
                                          d.broadcast_to([P, 2, MV]), ALU.mult)
                    bk.release(ins, "mv2", h, i)

            mod_sum_of(10)
            att_soft(0)
            mlstm_weights(0)
            for h in range(2):
                mod_col(SHIFT2, h)
            mod_sum_of(11)
            att_soft(1)
            att_norm(0)
            att_out(0)
            mlstm_out(0)
            mlstm_weights(1)
            att_norm(1)
            att_soft(2)
            att_out(1)
            mlstm_out(1)
            mlstm_weights(2)
            att_norm(2)
            att_soft(3)
            att_out(2)
            mlstm_out(2)
            mlstm_weights(3)
            att_norm(3)
            dve.wait_ge(S["g_post2_in"], 16)
            mod_row(GATE2, gg2, g_post)
            att_out(3)
            mlstm_out(3)
            bk.wait_released(dve, "mv2", 3, 1)
            heads = wide.rearrange("p t (h v) -> p t h v", h=MH)
            sq = junk.rearrange("p (t h v) -> p t h v", t=NT, h=MH)
            step(v.tensor_tensor(sq, heads, heads, ALU.mult))
            step(v.tensor_reduce(stat[:, 0, :].rearrange("p (t h) -> p t h", t=NT), sq, AX, ALU.add))
            mean_to_rstd(MV, 16)
            step(v.tensor_tensor(heads, heads, stat[:, 1, :].rearrange("p (t h) -> p t h", t=NT).unsqueeze(3)
                                 .broadcast_to([P, NT, MH, MV]), ALU.mult))
            step(v.tensor_tensor(wide, wide, m_norm[:].unsqueeze(1).broadcast_to([P, NT, MH * MV]), ALU.mult))
            dve.wait_ge(S["o_gate_done"], 1)
            v.tensor_tensor(wide, wide, o_gate[:], ALU.mult).then_inc(S["mh_done"], 1)
            for t in range(NT):
                dve.wait_ge(S["mix_sq"], 2 * t + 2)
                step(v.tensor_tensor(stat[:, 0, 8 + t:9 + t], stat[:, 0, 2 * t:2 * t + 1], stat[:, 0, 2 * t + 1:2 * t + 2], ALU.add))
                mean_to_rstd(D, 1, 8 + t)
                for h in range(2):
                    at = slice(h * 512, h * 512 + 512)
                    ins = v.scalar_tensor_tensor(out=x_new(t)[:, at], in0=bk("out", h, t), scalar=stat[:, 1, 8 + t:9 + t],
                                                 in1=gg1[:, at], op0=ALU.mult, op1=ALU.mult)
                    bk.release(ins, "out", h, t)
                dve.wait_ge(x_in[t], 32)
                for h in range(2):
                    bk.wait_released(dve, "out", h, t)
                step(v.tensor_tensor(x_sb[:, t, :], x_sb[:, t, :], x_new(t), ALU.add))
                step(v.tensor_tensor_reduce(out=x_new(t), in0=x_sb[:, t, :], in1=x_sb[:, t, :], scale=1.0, scalar=0.0,
                                            op0=ALU.mult, op1=ALU.add, accum_out=stat[:, 0, 12 + t:13 + t]))
                mean_to_rstd(D, 1, 12 + t)
                v.tensor_scalar(x_new(t), x_sb[:, t, :], stat[:, 1, 12 + t:13 + t], None, ALU.mult).then_inc(S["xn2_ready"], 1)
            bk.wait_full(dve, "h2T", 3, 1)
            for c in range(4, DC):
                ins = v.tensor_scalar(hT[:, c, 3 * P:T], bk("h2T", 3, 1)[:, (c - 4) * P:(c - 3) * P],
                                      cols[:, SCALE2 * 8 + c:SCALE2 * 8 + c + 1], cols[:, SHIFT2 * 8 + c:SHIFT2 * 8 + c + 1],
                                      ALU.mult, ALU.add)
            bk.release(ins, "h2T", 3, 1)


RECTS = [(0, 1, 16), (1, 1, 8), (2, 1, 5), (3, 1, 4), (4, 1, 3), (5, 3, 2), (8, 8, 1)]


def query_block(nc, A, keep, s_all):
    hT, ident, hH, hL, h_rows = keep["hT"], keep["ident"], keep["hH"], keep["hL"], keep["h_rows"]
    with ExitStack() as ctx:
        def sb(name, shape, dt=F32):
            return ctx.enter_context(nc.sbuf_tensor(name, shape, dt))

        def sem(name):
            return ctx.enter_context(nc.semaphore(name))

        M = 2 * PH
        order = [("h", i) for i in range(2)] + [("q", 0)] + [("keys", i) for i in range(4)]
        for m in range(M):
            order += ([("q", m + 1)] if m + 1 < M else []) + [("s", m)]
        psum = ctx.enter_context(nc.psum_tensor("query_psum", [P, 8, 512], F32))
        keys = sb("keys", [P, M, P])
        keysT = sb("keysT", [P, M, P])
        wq = sb("wq", [P, 2, DC, 2 * P])
        wqH = sb("wqH", [P, 2, DC, 2 * P], F32R)
        wqL = sb("wqL", [P, 2, DC, 2 * P], F32R)
        qT = sb("peer_qT", [P, 2, T])
        bank_full = [sem(f"q_bank_full{i}") for i in range(8)]
        bank_free = [sem(f"q_bank_free{i}") for i in range(8)]
        bk = Banks(psum, order, bank_full, bank_free)
        wq_in = [sem(f"wq_in{i}") for i in range(2)]
        keys_in, h_hi, h_lo, wq_hi, wq_lo = (sem(n) for n in ("keys_in", "h_hi", "h_lo", "wq_hi", "wq_lo"))
        block = ctx.enter_context(nc.Block())

        @block.sync
        def _(sp):
            for s in range(M // 2):
                if s == 1:
                    for half, name in enumerate(("peer_keys1", "peer_keys2")):
                        sp.dma_start(keys[:].rearrange("p (h two) d -> p h two d", two=2)[:, :, half, :],
                                     A[name][0].rearrange("h k d -> k h d")).then_inc(keys_in, 16)
                if s >= 2:
                    sp.wait_ge(wq_lo, s - 1)
                sp.dma_start(wq[:, s % 2, :, :], A["peer_wq"][0, :, s * 2 * P:(s + 1) * 2 * P]
                             .rearrange("(c p) n -> p c n", p=P)).then_inc(wq_in[s % 2], 16)

        @block.scalar
        def _(act):
            func = nc.scalar.activation
            for c in range(0, DC, 2):
                func(hH[:, c:c + 2, :], hT[:, c:c + 2, :], ACT.Copy).then_inc(h_hi, 1)

            def high(s):
                act.wait_ge(wq_in[s % 2], 16 * (s // 2 + 1))
                if s >= 2:
                    bk.wait_full(act, "q", 2 * s - 3)
                func(wqH[:, s % 2, :, :], wq[:, s % 2, :, :], ACT.Copy).then_inc(wq_hi, 1)

            high(0)
            for i in range(2):
                bk.wait_full(act, "h", i)
                bk.release(func(h_rows[:, i * 512:(i + 1) * 512], bk("h", i), ACT.Copy), "h", i)
            for i in range(4):
                bk.wait_full(act, "keys", i)
                ins = func(keysT[:, 4 * i:4 * i + 4, :], bk("keys", i).rearrange("p (m k) -> p m k", m=4), ACT.Copy)
                bk.release(ins, "keys", i)
            high(1)
            for m in range(M):
                bk.wait_full(act, "q", m)
                if m >= 2:
                    bk.wait_full(act, "s", m - 2)
                bk.release(func(qT[:, m % 2, :], bk("q", m), ACT.Copy), "q", m)
                if m % 2 and m // 2 + 2 < M // 2:
                    high(m // 2 + 2)

        @block.vector
        def _(dve):
            v = nc.vector
            for c in range(0, DC, 2):
                dve.wait_ge(h_hi, c // 2 + 1)
                v.tensor_tensor(hL[:, c:c + 2, :], hT[:, c:c + 2, :], hH[:, c:c + 2, :].bitcast(F32), ALU.subtract).then_inc(h_lo, 1)

            def low(s):
                dve.wait_ge(wq_hi, s + 1)
                v.tensor_tensor(wqL[:, s % 2, :, :], wq[:, s % 2, :, :], wqH[:, s % 2, :, :].bitcast(F32),
                                ALU.subtract).then_inc(wq_lo, 1)

            low(0)
            low(1)
            for m in range(M):
                if m % 2 == 0 and m and m // 2 + 1 < M // 2:
                    low(m // 2 + 1)
                bk.wait_full(dve, "s", m)
                ins = v.tensor_copy(s_all[:, m, :, :], bk("s", m).rearrange("p (t k) -> p t k", t=NT))
                bk.release(ins, "s", m)

        @block.tensor
        def _(pe):
            mm, tr = nc.tensor.matmul, nc.tensor.transpose
            for i in range(2):
                for k in range(4):
                    last = tr(bk("h", i)[:, k * P:(k + 1) * P], hT[:, 4 * i + k, 0:P], ident[:])
                bk.done(last, "h", i)
            def query(m):
                s = m // 2
                pe.wait_ge(wq_lo, s + 1)
                bk.wait_free(pe, "q", m)
                n = 0
                for c in range(DC):
                    if m == 0:
                        pe.wait_ge(h_lo, c // 2 + 1)
                    at = slice((m % 2) * P, (m % 2) * P + P)
                    for w, h in ((wqH, hH), (wqH, hL), (wqL, hH)):
                        last = mm(bk("q", m), w[:, s % 2, c, at], h[:, c, :], start=(n == 0), stop=(n == 3 * DC - 1))
                        n += 1
                bk.done(last, "q", m)

            query(0)
            pe.wait_ge(keys_in, 32)
            for i in range(4):
                for k in range(4):
                    last = tr(bk("keys", i)[:, k * P:(k + 1) * P], keys[:, 4 * i + k, :], ident[:])
                bk.done(last, "keys", i)


            for m in range(M):
                if m + 1 < M:
                    query(m + 1)
                bk.wait_released(pe, "q", m)
                bk.wait_released(pe, "keys", m // 4)
                bk.wait_free(pe, "s", m)
                for t in range(NT):
                    last = mm(bk("s", m)[:, t * P:(t + 1) * P], qT[:, m % 2, t * P:(t + 1) * P], keysT[:, m, :],
                              start=True, stop=True)
                bk.done(last, "s", m)


def expert_block(nc, A, keep, s_all, S_dram, G_dram):
    ident, hH, hL, h_rows, eidx, coef = (keep[n] for n in ("ident", "hH", "hL", "h_rows", "eidx", "coef"))
    with ExitStack() as ctx:
        def sb(name, shape, dt=F32):
            return ctx.enter_context(nc.sbuf_tensor(name, shape, dt))

        def sem(name):
            return ctx.enter_context(nc.semaphore(name))

        M = 2 * PH
        u_rows = keep["hT"].rearrange("p (q a) t -> p q (a t)", q=RING)
        row_no = sb("row_no", [P, RING], U32)
        dot4 = sb("dot4", [P, RING])
        dots = sb("dots", [P, K])
        val = sb("val", [P, 2, M, PTOP])
        idx = sb("idx", [P, M, PTOP], U32)
        idxf = sb("idxf", [P, M, PTOP])
        stage = sb("stage", [P, 2, NBLK, TB])
        spare = stage[:].rearrange("p a i t -> p (a i t)")
        hit = spare[:, 0:2 * PTOP * NCAND].rearrange("p (a k n) -> p a k n", a=2, k=PTOP)
        work = spare[:, 2 * PTOP * NCAND:2 * PTOP * NCAND + 4 * P].rearrange("p (a n) -> p a n", a=4)
        cv = sb("cv", [P, PH, NCAND])
        ci = sb("ci", [P, PH, NCAND])
        top = sb("top", [P, NT, PH, PTOP])
        pos = sb("top_pos", [P, PH, PTOP], U32)
        posf = sb("top_posf", [P, PH, PTOP])
        chosen = sb("chosen", [P, PH, PTOP])
        chosen_u = sb("chosen_u", [P, 2, K], U32)
        tsum = sb("tsum", [P, 2, NT, PH])
        sel = sb("sel", [P, NTD, 2, K])
        selT = sb("selT", [P, 4, TD])
        first = sb("first", [P, GT, P])
        iota_i = sb("iota_i", [P, P], I32)
        iota = sb("iota", [P, P])
        gate_hi = sb("gate_hi", [P, TD], F32R)
        onehot = sb("onehot", [P, 2, GT, 3, P], F32R)
        ub, v_in, g_in, gbuf = (keep[n] for n in ("ring", "v_in", "g_in", "gbuf"))
        uF = sb("uF", [P, 2, D])
        uH = sb("uH", [P, 2, D], F32R)
        uL = sb("uL", [P, 2, D], F32R)
        act_out = sb("act_out", [P, 2, TD])
        uT_ps = ctx.enter_context(nc.psum_tensor("uT_ps", [P, 2, D], F32))
        S_ps = ctx.enter_context(nc.psum_tensor("S_ps", [P, 2, T], F32))
        G_ps = ctx.enter_context(nc.psum_tensor("G_ps", [P, 2, 4, P], F32))

        u_in = [sem(f"u_in{i}") for i in range(RING)]
        rows_in = [sem(f"u_rows_in{i}") for i in range(RING)]
        s_stored = [sem(f"s_stored{i}") for i in range(2)]
        g_stored = [sem(f"g_stored{i}") for i in range(2)]
        (u_turned, u_high, u_copied, u_low, u_done, s_ready, dve_chain, iota_ready, iota_done, top_ready, gate_exp, sel_ready, selT_full,
         selT_done, hot_ready, g_full, g_staged, eidx_ready, dot_done, dots_gelu, row_no_ready, dots_copied, first_ready) = (sem(n) for n in (
            "u_turned", "u_high", "u_copied", "u_low", "u_done", "s_ready", "x_dve_chain", "iota_ready", "iota_done", "top_ready", "gate_exp",
            "sel_ready", "selT_full", "selT_done", "hot_ready", "g_full", "g_staged",
            "eidx_ready", "dot_done", "dots_gelu", "row_no_ready", "dots_copied", "first_ready"))
        block = ctx.enter_context(nc.Block())

        def rows_of_two(i, r):
            k = LEAD_ROWS + (GSTEPS - TWICE) + 8 * (i - (GSTEPS - TWICE) // 4) + 2 * r
            return [(k, k % 4, k // 4), (k + 1, (k + 1) % 4, (k + 1) // 4)]

        def blocks(eng, body):
            n0 = LEAD - LEAD_ROWS
            with eng.Fori(0, n0 // 4) as i:
                for r in range(4):
                    body(4 * i + r, i, r, None, [])
            def lead(i):
                for r in range(4):
                    body(n0 + 4 * i + r, n0 // 4 + i, r, None, [(4 * i + r, r, i)])

            with eng.Fori(0, LEAD_ROWS // 4 - 1) as i:
                lead(i)
            yield "near"
            lead(LEAD_ROWS // 4 - 1)
            yield "lead"
            with eng.Fori(0, (GSTEPS - TWICE) // 4) as i:
                for r in range(4):
                    body(LEAD + 4 * i + r, LEAD // 4 + i, r, (i, r), [(LEAD_ROWS + 4 * i + r, r, LEAD_ROWS // 4 + i)])
            for i in range((GSTEPS - TWICE) // 4, GSTEPS // 4):
                for r in range(4):
                    body(LEAD + 4 * i + r, LEAD // 4 + i, r, (i, r), rows_of_two(i, r))
            n0, k0 = NBLK - TAIL, K - TAIL_ROWS
            for i in range(TAIL // 4):
                for r in range(4):
                    body(n0 + 4 * i + r, n0 // 4 + i, r, None, [(k0 + 4 * i + r, r, k0 // 4 + i)] if 4 * i < TAIL_ROWS else [])

        @block.sync
        def _(sp):
            for b in range(2):
                sp.sem_inc(s_stored[b], 16)
                sp.sem_inc(g_stored[b], 16)

            def load(n, r):
                sp.dma_start(ub[:, r, :], A["peer_u"][0, bass.ds(n * P, P), :]).then_inc(u_in[r], 16)

            for r in range(RING):
                load(r, r)

            def body(n, four, r, g, d):
                b = r % 2
                sp.wait_ge(u_turned, n + 3)
                if not (isinstance(n, int) and n >= NBLK - RING):
                    load(n + RING, r)
                else:
                    k = n - (NBLK - RING)
                    sp.dma_start(ub[:, r, :], A["peer_v"][0, k * P:(k + 1) * P, :]).then_inc(v_in[r], 16)
                sp.wait_ge(s_ready, n + 3)
                sp.dma_start(S_dram[bass.ds(n, 1), :, :].rearrange("a p t -> p (a t)"), act_out[:, b, :]).then_inc(s_stored[b], 16)
                if g is not None and g[1] % 2:
                    i, k = g
                    sp.wait_ge(g_staged, 4 * i + k + 2)
                    sp.dma_start(G_dram[:, :, bass.ds(2 * i + k // 2, 1), :].rearrange("g p a n -> p g (a n)"),
                                 stage[:, k // 2, :, :].rearrange("p (g i) t -> p g (i t)", g=NBG)).then_inc(g_stored[k // 2], 16)

            for _ in blocks(sp, body):
                pass
            for b in range(2):
                sp.wait_ge(s_stored[b], 16 * (NBLK // 2 + 1))
                sp.wait_ge(g_stored[b], 16 * (NTB // 2 + 1))

        @block.gpsimd
        def _(pool):
            pool.sem_inc(u_low, 2)
            nc.gpsimd.iota(iota_i[:], pattern=[[1, P]], base=0, channel_multiplier=0).then_inc(iota_ready, 1)

            def body(n, four, r, g, d):
                b = r % 2
                if d:
                    pool.wait_ge(eidx_ready, 1)
                for k, q, turn in d:
                    pool.wait_ge(dot_done, k + 1)
                    nc.gpsimd.tensor_copy(row_no[:, q:q + 1], eidx[:, bass.ds(k, 1)]).then_inc(row_no_ready, 1)
                if d:
                    pool.wait_ge(row_no_ready, d[-1][0] + 1)
                pool.wait_ge(u_copied, n + 3)
                pool.wait_ge(u_done, n + 1)
                nc.gpsimd.tensor_tensor(uL[:, b, :], uF[:, b, :], uH[:, b, :].bitcast(F32), ALU.subtract).then_inc(u_low, 1)
                for k, q, turn in d:
                    pool.indirect_dma_start(u_rows[:, q, :], None, A["peer_u"][0],
                                            bass.IndirectOffsetOnAxis(row_no[:, q:q + 1], 0)).then_inc(rows_in[q], 16)
                k = n - (NBLK - TAIL + 2) if isinstance(n, int) else -1
                if 0 <= k < GP:
                    for i in range(2):
                        pool.wait_ge(g_stored[i], 16 * (NTB // 2 + 1))
                    part = slice(k * (NTB // GP), (k + 1) * (NTB // GP))
                    pool.dma_start(gbuf[0][:, part, :, :].rearrange("p q b t -> p (q b t)"),
                                   G_dram[0][:, part, :].rearrange("p q n -> p (q n)")).then_inc(g_in[0], 16)

            for _ in blocks(pool, body):
                pass

        @block.scalar
        def _(act):
            func = nc.scalar.activation
            act.sem_inc(u_copied, 2)
            act.sem_inc(u_high, 2)
            act.sem_inc(s_ready, 2)
            act.sem_inc(g_staged, 1)

            def copy(n, b):
                act.wait_ge(u_turned, n + 3)
                act.wait_ge(u_done, n + 1)
                func(uH[:, b, :], uT_ps[:, b, :], ACT.Copy).then_inc(u_high, 1)
                act.wait_ge(u_low, n + 1)
                func(uF[:, b, :], uT_ps[:, b, :], ACT.Copy).then_inc(u_copied, 1)

            def body(n, four, r, g, d):
                b = r % 2
                if not (isinstance(n, int) and n == NBLK - 1):
                    copy(n + 1, 1 - b)
                act.wait_ge(u_done, n + 3)
                act.wait_ge(s_stored[b], 32 * four + 16 * (r // 2) + 16)
                func(act_out[:, b, :], S_ps[:, b, 0:TD], ACT.Gelu).then_inc(s_ready, 1)
                if g is not None:
                    i, k = g
                    if k % 2 == 0:
                        act.wait_ge(g_stored[k // 2], 16 * i + 16)
                    act.wait_ge(g_full, 4 * i + k + 3)
                    for q in range(2):
                        t0 = (k % 2) * GT + q * 3
                        ins = func(stage[:, k // 2, :, t0:t0 + 3].rearrange("p i t -> p t i"), G_ps[:, q, 0:3, :], ACT.Copy)
                    ins.then_inc(g_staged, 1)

            copy(0, 0)
            for stop in blocks(act, body):
                if stop == "near":
                    act.wait_ge(top_ready, 1)
                    func(top[:], top[:], ACT.Exp).then_inc(gate_exp, 1)
            act.wait_ge(dots_copied, K // RING)
            func(coef[:], dots[:], ACT.Gelu).then_inc(dots_gelu, 1)

        @block.tensor
        def _(pe):
            mm, tr = nc.tensor.matmul, nc.tensor.transpose
            pe.sem_inc(u_turned, 2)
            pe.sem_inc(u_done, 2)
            pe.sem_inc(g_full, 2)

            def turn(n, four, r):
                b = r % 2
                pe.wait_ge(u_in[r], 16 * four + 16)
                pe.wait_ge(u_copied, n + 1)
                for c in range(DC):
                    last = tr(uT_ps[:, b, c * P:(c + 1) * P], ub[:, r, c * P:(c + 1) * P], ident[:])
                last.then_inc(u_turned, 1)

            def body(n, four, r, g, d):
                b = r % 2
                if not (isinstance(n, int) and n == NBLK - 1):
                    turn(n + 1, four + (r + 1) // 4, (r + 1) % 4)
                pe.wait_ge(u_high, n + 3)
                pe.wait_ge(s_ready, n + 1)
                for c in range(DC):
                    for h in (hH, hL):
                        mm(S_ps[:, b, 0:TD], uH[:, b, c * P:(c + 1) * P], h[:, c, P:T], start=(c == 0 and h is hH), stop=False)
                pe.wait_ge(u_low, n + 3)
                for c in range(DC):
                    last = mm(S_ps[:, b, 0:TD], uL[:, b, c * P:(c + 1) * P], hH[:, c, P:T], start=False, stop=(c == DC - 1))
                last.then_inc(u_done, 1)
                if g is not None:
                    m = 4 * g[0] + g[1]
                    pe.wait_ge(hot_ready, m + 1)
                    pe.wait_ge(g_staged, m + 1)
                    for k in range(GT):
                        for part in range(2):
                            last = mm(G_ps[:, k // 3, k % 3, :], onehot[:, b, k, 2, :], onehot[:, b, k, part, :],
                                      start=(part == 0), stop=(part == 1))
                    last.then_inc(g_full, 1)

            turn(0, 0, 0)
            for stop in blocks(pe, body):
                if stop == "near":
                    continue
                pe.wait_ge(sel_ready, 1)
                for i in range(3):
                    if i == 2:
                        pe.wait_ge(selT_done, 1)
                    for t in range(NTD):
                        src = sel[:, t, i, :] if i < 2 else top[:, t + 1, :, :].rearrange("p h k -> p (h k)")
                        last = tr(G_ps[:, i % 2, t, :], src, ident[:])
                    last.then_inc(selT_full, 1)

        @block.vector
        def _(dve):
            v = nc.vector
            step = Chain(dve, dve_chain)
            dve.sem_inc(dot_done, RING)
            dve.wait_ge(iota_ready, 1)
            step(v.tensor_copy(iota[:], iota_i[:]))

            def largest(rows):
                for values, indices, src, spare in rows:
                    step.put(v.max(values[:, 0:8], src))
                step.wait()
                for values, indices, src, spare in rows:
                    step.put(v.match_replace(spare, values[:, 0:8], src, -3.0e38))
                for values, indices, src, spare in rows:
                    step.put(v.max_index(indices[:, 0:8], values[:, 0:8], src))
                step.wait()
                for values, indices, src, spare in rows:
                    step.put(v.max(values[:, 8:16], spare))
                step.wait()
                for values, indices, src, spare in rows:
                    step.put(v.max_index(indices[:, 8:16], values[:, 8:16], spare))
                step.wait()

            def dot(k, q, turn):
                dve.wait_ge(rows_in[q], 16 * turn + 16)
                v.tensor_tensor_reduce(out=u_rows[:, q, :], in0=u_rows[:, q, :], in1=h_rows[:], scale=1.0, scalar=0.0,
                                       op0=ALU.mult, op1=ALU.add, accum_out=dot4[:, q:q + 1]).then_inc(dot_done, 1)
                if q == RING - 1:
                    dve.wait_ge(dot_done, k + 1 + RING)
                    v.tensor_copy(dots[:, bass.ds(RING * turn, RING)], dot4[:]).then_inc(dots_copied, 1)
                    dve.wait_ge(dots_copied, turn + 1)

            dots_made = 0

            def dots_beside(n):
                nonlocal dots_made
                for k in range(dots_made, dots_made + n):
                    dot(k, k % RING, k // RING)
                dots_made += n

            for t in range(NT):
                for m in range(0, M, 4):
                    largest([(val[:, t % 2, m + i, :], idx[:, m + i, :], s_all[:, m + i, t, :], work[:, i, :]) for i in range(4)])
                    dots_beside((1 if m else 2) if t else 0)
                step(v.tensor_copy(idxf[:], idx[:]))
                halves = lambda x, i: x.rearrange("p (h two) k -> p h two k", two=2)[:, :, i, :]
                v1, v2, i1, i2 = halves(val[:, t % 2, :, :], 0), halves(val[:, t % 2, :, :], 1), halves(idxf[:], 0), halves(idxf[:], 1)
                step(v.tensor_scalar(i1, i1, float(PK), None, ALU.mult))
                at = 0
                for a, na, nb in RECTS:
                    for dst, x, y in ((cv, v1, v2), (ci, i1, i2)):
                        step.put(v.tensor_tensor(dst[:, :, at:at + na * nb].rearrange("p h (a b) -> p h a b", a=na),
                                             x[:, :, a:a + na].unsqueeze(3).broadcast_to([P, PH, na, nb]),
                                             y[:, :, 0:nb].unsqueeze(2).broadcast_to([P, PH, na, nb]), ALU.add))
                    at += na * nb
                step.wait()
                dots_beside(2 if t else 0)
                for h in range(0, PH, 4):
                    largest([(top[:, t, h + i, :], pos[:, h + i, :], cv[:, h + i, :], work[:, i, 0:NCAND]) for i in range(4)])
                    dots_beside(1 if t else 0)
                step(v.tensor_copy(posf[:], pos[:]))
                for h in range(0, PH, 2):
                    place = posf[:, h:h + 2, :].unsqueeze(3).broadcast_to([P, 2, PTOP, NCAND])
                    step(v.tensor_tensor(hit, iota[:, 0:NCAND].unsqueeze(1).unsqueeze(1).broadcast_to([P, 2, PTOP, NCAND]),
                                         place, ALU.is_equal))
                    step(v.tensor_tensor(hit, hit, ci[:, h:h + 2, :].unsqueeze(2).broadcast_to([P, 2, PTOP, NCAND]), ALU.mult))
                    step(v.tensor_reduce(chosen[:, h:h + 2, :], hit, AX, ALU.add))
                    dots_beside((2 if h == 2 else 1) if t else 0)
                if t == 0:
                    v.tensor_copy(eidx[:], chosen[:].rearrange("p h k -> p (h k)")).then_inc(eidx_ready, 1)
                    dve.wait_ge(eidx_ready, 1)
                    continue
                step(v.tensor_copy(chosen_u[:, 0, :], chosen[:].rearrange("p h k -> p (h k)")))
                step(v.tensor_scalar(chosen_u[:, 1, :], chosen_u[:, 0, :], 7, None, ALU.logical_shift_right))
                step(v.tensor_copy(sel[:, t - 1, 0, :], chosen_u[:, 1, :]))
                step(v.tensor_scalar(chosen_u[:, 1, :], chosen_u[:, 0, :], PK - 1, None, ALU.bitwise_and))
                step(v.tensor_copy(sel[:, t - 1, 1, :], chosen_u[:, 1, :]))
            step(v.tensor_copy(tsum[:, 0, :, :], top[:, :, :, 0]))
            flat = top[:].rearrange("p t h k -> p (t h) k")
            sums = lambda i: tsum[:, i, :, :].rearrange("p t h -> p (t h)")
            over = lambda x: x.unsqueeze(2).broadcast_to([P, NT * PH, PTOP])
            v.tensor_tensor(flat, flat, over(sums(0)), ALU.subtract).then_inc(top_ready, 1)
            dots_beside(1)
            dve.wait_ge(gate_exp, 1)
            step(v.tensor_reduce(sums(0), flat, AX, ALU.add))
            step(v.reciprocal(sums(1), sums(0)))
            v.tensor_tensor(flat, flat, over(sums(1)), ALU.mult).then_inc(sel_ready, 1)
            assert dots_made <= LEAD_ROWS
            dots_beside(LEAD_ROWS - dots_made)
            for i in range(3):
                dve.wait_ge(selT_full, i + 1)
                v.tensor_copy(selT[:, i, :], G_ps[:, i % 2, 0:NTD, :].rearrange("p t k -> p (t k)")).then_inc(selT_done, 1)
            dve.wait_ge(selT_done, 3)
            step(v.tensor_copy(gate_hi[:], selT[:, 2, :]))
            step(v.tensor_copy(selT[:, 3, :], gate_hi[:].bitcast(F32)))
            step(v.tensor_tensor(selT[:, 2, :], selT[:, 2, :], selT[:, 3, :], ALU.subtract))

            def one_hot(m, b):
                over = lambda x: x.broadcast_to([P, GT, P])
                cols_of = lambda j: selT[:, j, bass.ds(GT * m, GT)].unsqueeze(2)
                keys = iota[:].unsqueeze(1)
                v.tensor_tensor(first[:], over(keys), over(cols_of(0)), ALU.is_equal).then_inc(first_ready, 1)
                dve.wait_ge(g_full, m + 1)
                v.tensor_tensor(onehot[:, b, :, 2, :], over(keys), over(cols_of(1)), ALU.is_equal)
                dve.wait_ge(first_ready, m + 1)
                gates = selT[:, 2:4, bass.ds(GT * m, GT)].rearrange("p j t -> p t j").unsqueeze(3)
                v.tensor_tensor(onehot[:, b, :, 0:2, :], first[:].unsqueeze(2).broadcast_to([P, GT, 2, P]),
                                gates.broadcast_to([P, GT, 2, P]), ALU.mult).then_inc(hot_ready, 1)
                dve.wait_ge(hot_ready, m + 1)

            def four_steps(i, twice, final):
                for b in range(4):
                    m = 4 * i + b
                    if not (final and b == 3):
                        one_hot(m + 1, (b + 1) % 2)
                    for row in rows_of_two(i, b) if twice else [(LEAD_ROWS + m, b, LEAD_ROWS // 4 + i)]:
                        dot(*row)

            one_hot(0, 0)
            with dve.Fori(0, (GSTEPS - TWICE) // 4) as i:
                four_steps(i, False, False)
            for i in range((GSTEPS - TWICE) // 4, GSTEPS // 4):
                four_steps(i, True, i == GSTEPS // 4 - 1)
            for i in range(TAIL_ROWS // RING):
                for q in range(RING):
                    dot(K - TAIL_ROWS + RING * i + q, q, (K - TAIL_ROWS) // RING + i)
            dve.wait_ge(dots_gelu, 1)
            v.tensor_tensor(coef[:], coef[:], top[:, 0, :, :].rearrange("p h k -> p (h k)"), ALU.mult)


def value_block(nc, A, keep, S_dram, G_dram, out):
    x_sb, gg2, eidx, coef = keep["x"], keep["gg2"], keep["eidx"], keep["coef"]
    with ExitStack() as ctx:
        def sb(name, shape, dt=F32):
            return ctx.enter_context(nc.sbuf_tensor(name, shape, dt))

        def sem(name):
            return ctx.enter_context(nc.semaphore(name))

        y_ps = ctx.enter_context(nc.psum_tensor("y_ps", [P, NTD, 2, 512], F32))
        vb, v_in, g_in = keep["ring"], keep["v_in"], keep["g_in"]
        vH = sb("vH", [P, RING, D], F32R)
        vL = sb("vL", [P, RING, D], F32R)
        sbuf = sb("s_in", [P, RING, TD])
        gbuf = [keep["gbuf"][0], sb("gbuf1", [P, NTB, BG, TB])]
        a = sb("a", [P, RING, TD])
        aH = sb("aH", [P, RING, TD], F32R)
        aL = sb("aL", [P, RING, TD], F32R)
        nothing = sb("nothing", [P, 512], F32R)
        y = sb("y", [P, NT, D])
        v_rows = keep["hT"].rearrange("p (q a) t -> p q (a t)", q=RING)
        row_no = sb("v_row_no", [P, RING], U32)
        y0 = sb("y0", [P, 2, D])
        sq = sb("sq", [P, 512])
        stat = sb("y_stat", [P, 5, 8])
        s_in = [sem(f"s_in_done{i}") for i in range(RING)]
        out_done = [sem(f"out_done{i}") for i in range(NT)]
        rows_in = [sem(f"v_rows_in{i}") for i in range(RING)]
        row_no_ready, row_done, y0_clear, y0_done = sem("v_row_no_ready"), sem("row_done"), sem("y0_clear"), sem("y0_done")
        nothing_ready, v_hi, v_lo, a_ready, a_hi, a_lo, v_done, y_done, y_sq, chain, out_ready = (
            sem(n) for n in ("nothing_ready", "v_hi", "v_lo", "a_ready", "a_hi", "a_lo", "v_done", "y_done", "y_sq",
                             "y_dve_chain", "out_ready"))
        block = ctx.enter_context(nc.Block())

        def blocks(eng, body):
            with eng.Fori(0, NBG // 2) as i:
                for gb in range(2):
                    with eng.Fori(0, BG // 4) as j:
                        for q in range(4):
                            body(i * (2 * BG) + gb * BG + 4 * j + q, q, i * (BG // 2) + gb * (BG // 4) + j,
                                 i, gb, 4 * j + q)

        def y_of(t, h):
            return y0[:, 0, h * 512:(h + 1) * 512] if t == 0 else y_ps[:, t - 1, h, :]

        @block.sync
        def _(sp):
            def load_s(n, q):
                sp.dma_start(sbuf[:, q, :], S_dram[bass.ds(n, 1), :, :].rearrange("a p t -> p (a t)")).then_inc(s_in[q], 16)

            for q in range(RING):
                load_s(q, q)
            with sp.Fori(0, NBLK // RING - 1) as i:
                for q in range(RING):
                    n = RING * i + q
                    sp.wait_ge(a_ready, n + 1 + RING)
                    load_s(n + RING, q)
                    sp.wait_ge(v_lo, n + 1 + RING)
                    sp.dma_start(vb[:, q, :], A["peer_v"][0, bass.ds((n + RING) * P, P), :]).then_inc(v_in[q], 16)
            for t in range(NT):
                sp.wait_ge(out_ready, t + 1)
                sp.dma_start(out[0, t * P:(t + 1) * P, :], y[:, t, :]).then_inc(out_done[t], 16)
            for t in range(NT):
                sp.wait_ge(out_done[t], 16)

        @block.gpsimd
        def _(pool):
            nc.gpsimd.memset(nothing[:].bitcast(F32), 0.0).then_inc(nothing_ready, 1)
            pool.sem_inc(v_lo, RING)

            def gather(q, at):
                pool.indirect_dma_start(v_rows[:, q, :], None, A["peer_v"][0],
                                        bass.IndirectOffsetOnAxis(at, 0)).then_inc(rows_in[q], 16)

            for q in range(2):
                gather(q, eidx[:, q:q + 1])

            def body(n, q, last):
                q2 = (q + 2) % 4
                if not last:
                    pool.wait_ge(row_done, n + 3)
                    nc.gpsimd.tensor_copy(row_no[:, q2:q2 + 1], eidx[:, bass.ds(n + 2, 1)]).then_inc(row_no_ready, 1)
                    pool.wait_ge(row_no_ready, n + 1)
                pool.wait_ge(v_done, n + 1)
                pool.wait_ge(v_hi, n + 1)
                nc.gpsimd.tensor_tensor(vL[:, q, :], vb[:, q, :], vH[:, q, :].bitcast(F32), ALU.subtract).then_inc(v_lo, 1)
                if not last:
                    gather(q2, row_no[:, q2:q2 + 1])

            def group(i, gb, more):
                with pool.Fori(0, GP if more else GP - 1) as j:
                    for q in range(4):
                        body(i * (2 * BG) + gb * BG + 4 * j + q, q, False)
                        if q == 0 and more:
                            pool.wait_ge(a_ready, i * (2 * BG) + gb * BG + RING)
                            pool.dma_start(gbuf[1 - gb][:, bass.ds(j * (NTB // GP), NTB // GP), :, :].rearrange("p q b t -> p (q b t)"),
                                           G_dram[bass.ds(2 * i + gb + 1, 1), :, bass.ds(j * (NTB // GP), NTB // GP), :]
                                           .rearrange("a p q n -> p (a q n)")).then_inc(g_in[1 - gb], 16)

            with pool.Fori(0, NBG // 2 - 1) as i:
                for gb in range(2):
                    group(i, gb, True)
            group(NBG // 2 - 1, 0, True)
            group(NBG // 2 - 1, 1, False)
            for q in range(4):
                body(NBLK - 4 + q, q, q >= 2)

        @block.scalar
        def _(act):
            func = nc.scalar.activation
            act.sem_inc(a_hi, RING)

            def body(n, q, turn, i, gb, k):
                act.wait_ge(v_in[q], 16 * turn + 16)
                act.wait_ge(v_done, n + 1)
                func(vH[:, q, :], vb[:, q, :], ACT.Copy).then_inc(v_hi, 1)
                act.wait_ge(a_ready, n + 1 + RING)
                func(aH[:, q, :], a[:, q, :], ACT.Copy).then_inc(a_hi, 1)

            blocks(act, body)
            act.wait_ge(y0_done, 1)
            for t in range(NT):
                if t == 1:
                    act.wait_ge(y_done, 1)
                for h in range(2):
                    func(sq[:], y_of(t, h), ACT.Square, accum_out=stat[:, 0, 2 * t + h:2 * t + h + 1]).then_inc(y_sq, 1)
                    act.wait_ge(y_sq, 2 * t + h + 1)

        @block.vector
        def _(dve):
            v = nc.vector
            step = Chain(dve, chain)
            dve.sem_inc(row_done, RING)
            dve.sem_inc(a_ready, RING)
            dve.sem_inc(a_lo, RING)

            def body(n, q, turn, i, gb, k):
                dve.wait_ge(s_in[q], 16 * turn + 16)
                dve.wait_ge(g_in[gb], 16 * GP * (i + 1))
                dve.wait_ge(a_hi, n + 1)
                v.tensor_tensor(a[:, q, :].rearrange("p (q t) -> p q t", t=TB),
                                sbuf[:, q, :].rearrange("p (q t) -> p q t", t=TB),
                                gbuf[gb][:, :, bass.ds(k, 1), :].rearrange("p q a t -> p q (a t)"),
                                ALU.mult).then_inc(a_ready, 1)
                dve.wait_ge(a_hi, n + 1 + RING)
                v.tensor_tensor(aL[:, q, :], a[:, q, :], aH[:, q, :].bitcast(F32), ALU.subtract).then_inc(a_lo, 1)
                dve.wait_ge(rows_in[q], 16 * turn + 16)
                dve.wait_ge(row_done, n + 3)
                v.scalar_tensor_tensor(out=y0[:, q % 2, :], in0=v_rows[:, q, :], scalar=coef[:, bass.ds(n, 1)], in1=y0[:, q % 2, :],
                                       op0=ALU.mult, op1=ALU.add).then_inc(row_done, 1)

            v.memset(y0[:], 0.0).then_inc(y0_clear, 1)
            dve.wait_ge(y0_clear, 1)
            blocks(dve, body)
            dve.wait_ge(row_done, K + RING)
            v.tensor_tensor(y0[:, 0, :], y0[:, 0, :], y0[:, 1, :], ALU.add).then_inc(y0_done, 1)
            for t in range(NT):
                for h in range(2):
                    dve.wait_ge(y_sq, 2 * t + h + 1)
                    step.put(v.tensor_tensor(y[:, t, h * 512:(h + 1) * 512], y_of(t, h), gg2[:, h * 512:(h + 1) * 512], ALU.mult))
            dve.wait_ge(y_sq, 2 * NT)
            step(v.tensor_reduce(stat[:, 1, 0:NT], stat[:, 0, :].rearrange("p (t h) -> p t h", t=NT), AX, ALU.add))
            step(v.tensor_scalar(stat[:, 2, 0:NT], stat[:, 1, 0:NT], 1.0 / D, EPS, ALU.mult, ALU.add))
            rsqrt(nc, step, stat[:, 1, 0:NT], stat[:, 2, 0:NT], stat[:, 3, 0:NT], stat[:, 4, 0:NT])
            for t in range(NT):
                v.scalar_tensor_tensor(out=y[:, t, :], in0=y[:, t, :], scalar=stat[:, 1, t:t + 1], in1=x_sb[:, t, :],
                                       op0=ALU.mult, op1=ALU.add).then_inc(out_ready, 1)

        @block.tensor
        def _(pe):
            mm = nc.tensor.matmul
            pe.sem_inc(v_done, RING)
            pe.wait_ge(nothing_ready, 1)
            for t in range(NTD):
                for h in range(2):
                    mm(y_ps[:, t, h, :], nothing[:, 0:P], nothing[:], start=True, stop=False)

            def body(n, q, turn, i, gb, k):
                pe.wait_ge(a_lo, n + 1 + RING)
                pe.wait_ge(v_lo, n + 1 + RING)
                for t in range(NTD):
                    for x, w in ((aH, vH), (aH, vL), (aL, vH)):
                        for h in range(2):
                            last = mm(y_ps[:, t, h, :], x[:, q, t * P:(t + 1) * P], w[:, q, h * 512:(h + 1) * 512],
                                      start=False, stop=False)
                last.then_inc(v_done, 1)

            blocks(pe, body)
            for t in range(NTD):
                for h in range(2):
                    last = mm(y_ps[:, t, h, :], nothing[:, 0:P], nothing[:], start=False, stop=True)
            last.then_inc(y_done, 1)


def build(nc, A, out):
    with ExitStack() as ctx:
        def sb(name, shape, dt=F32):
            return ctx.enter_context(nc.sbuf_tensor(name, shape, dt))

        keep = dict(x=sb("x_sb", [P, NT, D]), hT=sb("hT", [P, DC, T]), ident=sb("ident", [P, P]),
                    cols=sb("cols", [P, 88]), gg2=sb("gg2", [P, D]))
        keep["eidx"] = sb("eidx", [P, K], U32)
        keep["coef"] = sb("coef", [P, K])
        S_dram = nc.dram_tensor("gelu_table", (NBLK, P, TD), F32, kind="Internal").ap()
        G_dram = nc.dram_tensor("gate_table", (NBG, P, NTB, BG * TB), F32, kind="Internal").ap()
        mix_block(nc, A, keep)
        s_all = sb("s_all", [P, 2 * PH, NT, P])
        gbuf0 = s_all[:].rearrange("p m t k -> p (m t k)")[:, 0:NTB * BG * TB].rearrange("p (q b t) -> p q b t", q=NTB, b=BG)
        keep["gbuf"] = [gbuf0]
        keep["g_in"] = [ctx.enter_context(nc.semaphore(f"g_in{i}")) for i in range(2)]
        keep["ring"] = sb("ring", [P, RING, D])
        keep["v_in"] = [ctx.enter_context(nc.semaphore(f"v_in{i}")) for i in range(RING)]
        with ExitStack() as peer:
            keep["hH"] = peer.enter_context(nc.sbuf_tensor("hH", [P, DC, T], F32R))
            keep["hL"] = peer.enter_context(nc.sbuf_tensor("hL", [P, DC, T], F32R))
            keep["h_rows"] = peer.enter_context(nc.sbuf_tensor("h_rows", [P, D], F32))
            query_block(nc, A, keep, s_all)
            expert_block(nc, A, keep, s_all, S_dram, G_dram)
        value_block(nc, A, keep, S_dram, G_dram, out)


_INS = ["x", "c", "positions", "w_mod", "b_mod", "g_pre_mix", "g_post_mix", "w_in", "conv_w", "b_igate", "b_fgate",
        "mlstm_norm_g", "att_sinks", "w_out", "g_pre_ffn", "g_post_ffn", "peer_wq", "peer_keys1", "peer_keys2",
        "peer_u", "peer_v"]


def kernel(**inputs):
    import numpy as np
    import concourse.bacc as bacc
    from concourse.bass_utils import run_bass_kernel_spmd

    nc = bacc.Bacc("TRN2", target_bir_lowering=False, num_devices=1)
    arrays, A = {}, {}
    for name in _INS:
        a = np.ascontiguousarray(inputs[name])
        arrays[f"in_{name}"] = a
        A[name] = nc.dram_tensor(f"in_{name}", a.shape, mybir.dt.from_np(a.dtype), kind="ExternalInput").ap()
    inv = np.float32(10000.0) ** (-np.arange(0, DH, 2, dtype=np.float32) / np.float32(DH))
    arrays["in_inv_freq"] = inv.astype(np.float32)
    A["inv_freq"] = nc.dram_tensor("in_inv_freq", inv.shape, F32, kind="ExternalInput").ap()
    out = nc.dram_tensor("out_0", (1, T, D), F32, kind="ExternalOutput").ap()
    build(nc, A, out)
    r = run_bass_kernel_spmd(nc, [arrays], core_ids=[0])
    return r.results[0]["out_0"]
```
